# Optimizing a Trainium2 kernel written in Bass

```python
import jax, jax.numpy as jnp
from jax import lax
import numpy as np

D_MODEL = 1024
BATCH = 1
SEQ = 256
DEPTH = 1
DEC_BATCH = 1
DEC_SEQ = 1024
PAST_LEN = 256

GRID_W = 64
N_MOD = 6
RET_HEADS = 8
RET_DK = 64
RET_DV = 64
RET_WIDTH = RET_HEADS * RET_DV
RET_QK_WIDTH = RET_HEADS * RET_DK
RET_CHUNK = 128
RWKV_HEADS = 8
RWKV_HD = 64
RWKV_WIDTH = RWKV_HEADS * RWKV_HD
LORA_W = 64
LORA_A = 64
LORA_G = 128
CONV_W = 3
PEER_HEADS = 8
N_KEYS = 128
N_EXPERTS = N_KEYS * N_KEYS
PEER_DQ = 256
PEER_TOPK = 16
PEER_BLOCK = 128
ROPE_BASE = 10000.0
NORM_EPS = 1e-6
GN_EPS = 64e-5
IN_SIZES = (RET_QK_WIDTH, RET_QK_WIDTH, RET_WIDTH, RET_WIDTH,
            RWKV_WIDTH, RWKV_WIDTH, RWKV_WIDTH, LORA_W, LORA_A, LORA_G,
            D_MODEL, D_MODEL)
IN_COLS = sum(IN_SIZES)
IN_SPLITS = tuple(sum(IN_SIZES[:i + 1]) for i in range(len(IN_SIZES) - 1))

kernel_name = 'hybrid_retention_rwkv7_peer_diffusion_step'

def rms_norm(x, g):
    xf = x.astype(jnp.float32)
    y = xf * lax.rsqrt(jnp.mean(xf * xf, axis=-1, keepdims=True) + NORM_EPS)
    return (y * g.astype(jnp.float32)).astype(x.dtype)

def head_norm(y, w, b):
    H, hd = y.shape[-2:]
    mu = jnp.mean(y, axis=-1, keepdims=True)
    var = jnp.mean(jnp.square(y - mu), axis=-1, keepdims=True)
    return ((y - mu) * lax.rsqrt(var + GN_EPS) * w.astype(jnp.float32).reshape(H, hd)
            + b.astype(jnp.float32).reshape(H, hd))

def rope_1d(x, pos):
    q = x.shape[-1] // 2
    inv = ROPE_BASE ** (-jnp.arange(q, dtype=jnp.float32) / q)
    ang = pos.astype(jnp.float32)[:, None] * inv[None, :]
    cos = jnp.cos(ang)[None, :, None, :]
    sin = jnp.sin(ang)[None, :, None, :]
    x1, x2 = x[..., :q], x[..., q:]
    return jnp.concatenate([x1 * cos - x2 * sin, x1 * sin + x2 * cos], axis=-1)

def rope_2d(x, row, col):
    half = x.shape[-1] // 2
    return jnp.concatenate([rope_1d(x[..., :half], row), rope_1d(x[..., half:], col)], axis=-1)

def retention_scan(q, k, v, log_gamma, r0):
    B, S, H, dk = q.shape
    dv = v.shape[-1]
    n = S // RET_CHUNK
    C = RET_CHUNK
    to_chunks = lambda t: t.reshape(B, n, C, H, t.shape[-1]).transpose(1, 0, 3, 2, 4)
    qc, kc, vc = to_chunks(q), to_chunks(k), to_chunks(v)
    idx = jnp.arange(C, dtype=jnp.float32)
    diff = idx[:, None] - idx[None, :]
    lg = log_gamma[:, None, None]
    decay_in = jnp.where(diff >= 0, jnp.exp(jnp.maximum(diff, 0.0) * lg), 0.0)
    cross_decay = jnp.exp((idx + 1.0)[None, :] * log_gamma[:, None])
    state_decay = jnp.exp((C - 1.0 - idx)[None, :] * log_gamma[:, None])
    chunk_decay = jnp.exp(C * log_gamma)

    def step(R, xs):
        qi, ki, vi = xs
        scores = jnp.einsum('bhid,bhjd->bhij', qi, ki) * decay_in
        o = (jnp.einsum('bhij,bhjv->bhiv', scores, vi)
             + jnp.einsum('bhid,bhdv->bhiv', qi, R) * cross_decay[None, :, :, None])
        R = (R * chunk_decay[None, :, None, None]
             + jnp.einsum('bhjd,bhjv->bhdv', ki * state_decay[None, :, :, None], vi))
        return R, o

    R, o = lax.scan(step, r0, (qc, kc, vc))
    o = o.transpose(1, 0, 3, 2, 4).reshape(B, S, H, dv)
    return o, R

def retention_bidir(q, k, v, log_gamma, s0):
    o_f, r_f = retention_scan(q, k, v, log_gamma[0], s0[:, 0])
    o_b, r_b = retention_scan(jnp.flip(q, 1), jnp.flip(k, 1), jnp.flip(v, 1), log_gamma[1], s0[:, 1])
    return o_f + jnp.flip(o_b, 1), jnp.stack([r_f, r_b], axis=1)

def rwkv7_scan(r, w, k, v, kk, a, s0):
    xs = tuple(jnp.moveaxis(t, 1, 0) for t in (r, w, k, v, kk, a))

    def step(S, xt):
        r_t, w_t, k_t, v_t, kk_t, a_t = xt
        sk = jnp.einsum('bhvk,bhk->bhv', S, kk_t)
        S = (S * w_t[:, :, None, :] - sk[..., None] * (kk_t * a_t)[:, :, None, :]
             + v_t[..., None] * k_t[:, :, None, :])
        y = jnp.einsum('bhvk,bhk->bhv', S, r_t)
        return S, y

    S, y = lax.scan(step, s0, xs)
    return jnp.moveaxis(y, 0, 1), S

def rwkv7_mixer(r, k, v, dw, da, dg, s0, lp):
    f32 = jnp.float32
    B, S, _ = r.shape
    heads = lambda t: t.reshape(B, S, RWKV_HEADS, RWKV_HD)
    r, k, v, dw, da, dg = (t.astype(f32) for t in (r, k, v, dw, da, dg))
    kk = heads(k * lp['rwkv_k_k'].astype(f32))
    kk = kk * lax.rsqrt(jnp.sum(kk * kk, axis=-1, keepdims=True) + 1e-12)
    ys, finals = [], []
    for d in range(2):
        w_log = -jax.nn.softplus(-(lp['rwkv_w0'][d] + jnp.tanh(dw) @ lp['rwkv_w2'][d])) - 0.5
        decay = jnp.exp(-jnp.exp(w_log))
        a = jax.nn.sigmoid(lp['rwkv_a0'][d] + da @ lp['rwkv_a2'][d])
        kd = k * (1.0 + (a - 1.0) * lp['rwkv_k_a'].astype(f32))
        seqs = (heads(r), heads(decay), heads(kd), heads(v), kk, heads(a))
        if d == 1:
            seqs = tuple(jnp.flip(t, 1) for t in seqs)
        y, s_fin = rwkv7_scan(*seqs, s0[:, d].astype(f32))
        if d == 1:
            y = jnp.flip(y, 1)
        ys.append(y)
        finals.append(s_fin)
    y = head_norm(ys[0] + ys[1], lp['rwkv_gn_w'], lp['rwkv_gn_b'])
    bonus = jnp.sum(heads(r) * heads(k) * lp['rwkv_r_k'].astype(f32), axis=-1, keepdims=True)
    y = y + bonus * heads(v)
    g = jax.nn.sigmoid(dg) @ lp['rwkv_g2'].astype(f32)
    return y.reshape(B, S, RWKV_WIDTH) * g, jnp.stack(finals, axis=1)

def centred_dwconv(x, w):
    return lax.conv_general_dilated(x, w[:, None, :].astype(x.dtype), window_strides=(1,),
                                    padding='SAME', dimension_numbers=('NWC', 'WIO', 'NWC'),
                                    feature_group_count=x.shape[-1])

def token_mixer(h, rot, s_ret0, s_rwkv0, lp):
    f32 = jnp.float32
    B, S, _ = h.shape
    parts = jnp.split(h @ lp['w_in'], IN_SPLITS, axis=-1)
    rq, rk, rv, rg, wr, wk, wv, dw, da, dg, gate_a, gate_b = parts
    q = rq.astype(f32).reshape(B, S, RET_HEADS, RET_DK)
    k = rk.astype(f32).reshape(B, S, RET_HEADS, RET_DK)
    v = rv.astype(f32).reshape(B, S, RET_HEADS, RET_DV)
    if rot is not None:
        q = rope_2d(q, rot[0], rot[1])
        k = rope_2d(k, rot[0], rot[1])
    log_gamma = jax.nn.log_sigmoid(lp['ret_decay'].astype(f32))
    o, ret_fin = retention_bidir(q, k * RET_DK ** -0.5, v, log_gamma, s_ret0.astype(f32))
    y_a = head_norm(o, lp['ret_gn_w'], lp['ret_gn_b']).reshape(B, S, RET_WIDTH) * jax.nn.silu(rg.astype(f32))
    rkv = centred_dwconv(jnp.concatenate([wr, wk, wv], axis=-1), lp['rwkv_conv'])
    wr, wk, wv = jnp.split(rkv, 3, axis=-1)
    y_b, rwkv_fin = rwkv7_mixer(wr, wk, wv, dw, da, dg, s_rwkv0, lp)
    br_a = y_a.astype(h.dtype) @ lp['w_br_a']
    br_b = y_b.astype(h.dtype) @ lp['w_br_b']
    merged = jax.nn.sigmoid(gate_a) * br_a + jax.nn.sigmoid(gate_b) * br_b
    return merged @ lp['w_out'], ret_fin, rwkv_fin

def peer_ffn(h, wq, sub_keys, u_tab, v_tab):
    B, S, D = h.shape
    xb = h.reshape((B * S) // PEER_BLOCK, PEER_BLOCK, D)

    def block(xt):
        q = (xt @ wq).reshape(PEER_BLOCK, PEER_HEADS, 2, PEER_DQ // 2)
        s = jnp.einsum('thcd,hckd->thck', q, sub_keys).astype(jnp.float32)
        s1, i1 = lax.top_k(s[:, :, 0], PEER_TOPK)
        s2, i2 = lax.top_k(s[:, :, 1], PEER_TOPK)
        cand = (s1[..., :, None] + s2[..., None, :]).reshape(PEER_BLOCK, PEER_HEADS, PEER_TOPK * PEER_TOPK)
        cidx = (i1[..., :, None] * N_KEYS + i2[..., None, :]).reshape(PEER_BLOCK, PEER_HEADS, PEER_TOPK * PEER_TOPK)
        top, pos = lax.top_k(cand, PEER_TOPK)
        idx = jnp.take_along_axis(cidx, pos, axis=-1)
        gate = jax.nn.softmax(top, axis=-1)
        act = jax.nn.gelu(jnp.einsum('td,thkd->thk', xt, u_tab[idx]).astype(jnp.float32))
        return jnp.einsum('thk,thkd->td', (gate * act).astype(xt.dtype), v_tab[idx])

    return lax.map(block, xb).reshape(B, S, D)

def trunk_layer(x, mod, rot, s_ret0, s_rwkv0, lp):
    sh1, sc1, g1, sh2, sc2, g2 = jnp.split(mod, N_MOD, axis=-1)
    h = rms_norm(x, lp['norm1_g']) * (1.0 + sc1) + sh1
    m, ret_fin, rwkv_fin = token_mixer(h, rot, s_ret0, s_rwkv0, lp)
    x = x + g1 * m
    h = rms_norm(x, lp['norm2_g']) * (1.0 + sc2) + sh2
    x = x + g2 * peer_ffn(h, lp['peer_wq'], lp['peer_keys'], lp['peer_u'], lp['peer_v'])
    return x, ret_fin, rwkv_fin

def setup_inputs(seed: int = 0) -> dict:
    key = jax.random.key(seed)
    ks = jax.random.split(key, 40)
    f32 = jnp.float32

    def nrm(i, shape, scale):
        return scale * jax.random.normal(ks[i], shape, f32)

    base_decay = jnp.log(2.0 ** (5.0 + jnp.arange(RET_HEADS, dtype=f32)) - 1.0)
    conv_base = jnp.array([0.25, 1.0, 0.25], f32)[None, :, None]
    return {
        'x_prompt': nrm(0, (BATCH, SEQ, D_MODEL), 1.0),
        'x_sample': nrm(1, (DEC_BATCH, DEC_SEQ, D_MODEL), 1.0),
        'state_ret': nrm(2, (DEC_BATCH, DEPTH, 2, RET_HEADS, RET_DK, RET_DV), 1.0),
        'state_rwkv': nrm(3, (DEC_BATCH, DEPTH, 2, RWKV_HEADS, RWKV_HD, RWKV_HD), 1.0),
        'c': nrm(4, (DEC_BATCH, D_MODEL), 1.0),
        'c_ctx': nrm(5, (D_MODEL,), 1.0),
        'ada_w': nrm(6, (DEPTH, D_MODEL, N_MOD * D_MODEL), 0.5 * D_MODEL ** -0.5),
        'ada_b': nrm(7, (DEPTH, N_MOD * D_MODEL), 0.02),
        'norm1_g': 1.0 + nrm(8, (DEPTH, D_MODEL), 0.02),
        'w_in': nrm(9, (DEPTH, D_MODEL, IN_COLS), D_MODEL ** -0.5),
        'ret_decay': base_decay[None, None, :] + nrm(10, (DEPTH, 2, RET_HEADS), 0.1),
        'ret_gn_w': 1.0 + nrm(11, (DEPTH, RET_WIDTH), 0.02),
        'ret_gn_b': nrm(12, (DEPTH, RET_WIDTH), 0.02),
        'rwkv_conv': conv_base + nrm(13, (DEPTH, CONV_W, 3 * RWKV_WIDTH), 0.05),
        'rwkv_w0': jax.random.uniform(ks[14], (DEPTH, 2, RWKV_WIDTH), f32, -5.0, 1.0),
        'rwkv_w2': nrm(15, (DEPTH, 2, LORA_W, RWKV_WIDTH), 0.5 * LORA_W ** -0.5),
        'rwkv_a0': nrm(16, (DEPTH, 2, RWKV_WIDTH), 0.5),
        'rwkv_a2': nrm(17, (DEPTH, 2, LORA_A, RWKV_WIDTH), 0.5 * LORA_A ** -0.5),
        'rwkv_g2': nrm(18, (DEPTH, LORA_G, RWKV_WIDTH), LORA_G ** -0.5),
        'rwkv_k_k': 0.85 + nrm(19, (DEPTH, RWKV_WIDTH), 0.05),
        'rwkv_k_a': 1.0 + nrm(20, (DEPTH, RWKV_WIDTH), 0.05),
        'rwkv_r_k': nrm(21, (DEPTH, RWKV_HEADS, RWKV_HD), 0.1),
        'rwkv_gn_w': 1.0 + nrm(22, (DEPTH, RWKV_WIDTH), 0.02),
        'rwkv_gn_b': nrm(23, (DEPTH, RWKV_WIDTH), 0.02),
        'w_br_a': nrm(24, (DEPTH, RET_WIDTH, D_MODEL), RET_WIDTH ** -0.5),
        'w_br_b': nrm(25, (DEPTH, RWKV_WIDTH, D_MODEL), RWKV_WIDTH ** -0.5),
        'w_out': nrm(26, (DEPTH, D_MODEL, D_MODEL), D_MODEL ** -0.5),
        'norm2_g': 1.0 + nrm(27, (DEPTH, D_MODEL), 0.02),
        'peer_wq': nrm(28, (DEPTH, D_MODEL, PEER_HEADS * PEER_DQ), D_MODEL ** -0.5),
        'peer_keys': nrm(29, (DEPTH, PEER_HEADS, 2, N_KEYS, PEER_DQ // 2), (PEER_DQ // 2) ** -0.5),
        'peer_u': nrm(30, (DEPTH, N_EXPERTS, D_MODEL), D_MODEL ** -0.5),
        'peer_v': nrm(31, (DEPTH, N_EXPERTS, D_MODEL), 1.0),
        'final_norm_g': 1.0 + nrm(32, (D_MODEL,), 0.02),
    }

def reference(x_prompt, x_sample, state_ret, state_rwkv, c, c_ctx, ada_w, ada_b, norm1_g, w_in,
              ret_decay, ret_gn_w, ret_gn_b, rwkv_conv, rwkv_w0, rwkv_w2, rwkv_a0, rwkv_a2,
              rwkv_g2, rwkv_k_k, rwkv_k_a, rwkv_r_k, rwkv_gn_w, rwkv_gn_b, w_br_a, w_br_b,
              w_out, norm2_g, peer_wq, peer_keys, peer_u, peer_v, final_norm_g):
    n_lat = x_sample.shape[1]
    rows = n_lat // GRID_W
    grid_row, grid_col = jnp.meshgrid(jnp.arange(rows), jnp.arange(GRID_W), indexing='ij')
    rot = (grid_row.reshape(-1), grid_col.reshape(-1))

    b_ctx = x_prompt.shape[0]
    zero_ret = jnp.zeros((b_ctx, 2, RET_HEADS, RET_DK, RET_DV), jnp.float32)
    zero_rwkv = jnp.zeros((b_ctx, 2, RWKV_HEADS, RWKV_HD, RWKV_HD), jnp.float32)

    xp, xs = x_prompt, x_sample
    new_ret, new_rwkv = [], []
    for l in range(DEPTH):
        lp = {
            'norm1_g': norm1_g[l], 'w_in': w_in[l], 'ret_decay': ret_decay[l],
            'ret_gn_w': ret_gn_w[l], 'ret_gn_b': ret_gn_b[l], 'rwkv_conv': rwkv_conv[l],
            'rwkv_w0': rwkv_w0[l], 'rwkv_w2': rwkv_w2[l], 'rwkv_a0': rwkv_a0[l],
            'rwkv_a2': rwkv_a2[l], 'rwkv_g2': rwkv_g2[l], 'rwkv_k_k': rwkv_k_k[l],
            'rwkv_k_a': rwkv_k_a[l], 'rwkv_r_k': rwkv_r_k[l], 'rwkv_gn_w': rwkv_gn_w[l],
            'rwkv_gn_b': rwkv_gn_b[l], 'w_br_a': w_br_a[l], 'w_br_b': w_br_b[l],
            'w_out': w_out[l], 'norm2_g': norm2_g[l], 'peer_wq': peer_wq[l],
            'peer_keys': peer_keys[l], 'peer_u': peer_u[l], 'peer_v': peer_v[l],
        }
        mod_ctx = (jax.nn.silu(c_ctx) @ ada_w[l] + ada_b[l])[None, None, :]
        mod_lat = (jax.nn.silu(c) @ ada_w[l] + ada_b[l])[:, None, :]
        xp, ret_fin, rwkv_fin = trunk_layer(xp, mod_ctx, None, zero_ret, zero_rwkv, lp)
        new_ret.append(ret_fin.astype(x_prompt.dtype))
        new_rwkv.append(rwkv_fin.astype(x_prompt.dtype))
        xs, _, _ = trunk_layer(xs, mod_lat, rot, state_ret[:, l], state_rwkv[:, l], lp)

    y_prompt = rms_norm(xp, final_norm_g)
    y_sample = rms_norm(xs, final_norm_g)
    new_state_ret = jnp.stack(new_ret, axis=1)
    new_state_rwkv = jnp.stack(new_rwkv, axis=1)
    return (y_prompt, y_sample, new_state_ret, new_state_rwkv)


_drawn_inputs = setup_inputs


def setup_inputs(seed=0):
    import zlib

    import numpy as np

    out = dict(_drawn_inputs(seed))
    spreads = {}
    factors = {'state_rwkv': 6.762,
     'ret_gn_w': 65.114,
     'ret_gn_b': 70.441,
     'rwkv_gn_w': 80.13,
     'rwkv_gn_b': 81.024,
     'final_norm_g': 20.395,
     'norm2_g': 11.62}
    for name, (base, spread) in spreads.items():
        noise = np.random.default_rng([zlib.crc32(name.encode()), seed]).standard_normal(out[name].shape)
        drawn = base * np.exp(spread * noise) if base else spread * noise
        out[name] = __import__('jax').numpy.asarray(drawn.astype(out[name].dtype))
    for name, factor in factors.items():
        out[name] = (out[name] * factor).astype(out[name].dtype)
    return out
```

```python
import math
from contextlib import ExitStack

import numpy as np

import concourse.bass as bass
from concourse import mybir
from concourse.alu_op_type import AluOpType as ALU

ACT = mybir.ActivationFunctionType
AX = mybir.AxisListType
F32 = mybir.dt.float32
U32 = mybir.dt.uint32

P = 128
D = 1024
KD = D // P
T_CTX, T_LAT = 256, 1024
T = T_CTX + T_LAT
NT = T // P
SEGS = [(0, 0, T_CTX), (1, T_CTX, T)]
COLS = [(0, 512), (512, 1024), (1024, T)]
H, HD = 8, 64
PAIRS = H // 2
MODS = 6
A_BLOCKS = 3
B_BLOCKS = 34
RG, WR, WK, WV, DWDA, DG, GA, GB = 0, 4, 8, 12, 16, 17, 18, 26
NORM_EPS, GN_EPS = 1e-6, 64e-5


def linker(eng, sem, again=False):
    count = [0]
    if again:
        eng.sem_clear(sem)

    def link(ins):
        count[0] += 1
        ins.then_inc(sem, 1)
        eng.wait_ge(sem, count[0])

    return link


def hold(eng, passed, *waits):
    for s, v in waits:
        eng.wait_ge(s, v)
    eng.sem_inc(passed, 1)


def count_from_one(nc, *semaphores):
    for s in semaphores:
        for x in s if isinstance(s, list) else [s]:
            nc.gpsimd.sem_inc(x, 1)
    nc.all_engine_barrier()


def opener(nc, ctx):
    taken = []

    def release():
        if taken:
            nc.clear_and_free_semaphores(taken)
            nc.all_engine_barrier()

    ctx.callback(release)

    def sb(name, shape, dt=F32):
        return ctx.enter_context(nc.sbuf_tensor(name, shape, dt))

    def pb(name, shape, dt=F32):
        return ctx.enter_context(nc.psum_tensor(name, shape, dt))

    def sem(name):
        taken.append(nc.alloc_semaphore(name))
        return taken[-1]

    return sb, pb, sem


def modulation(nc, g, d):
    NB = MODS * D // 512
    with ExitStack() as ctx:
        sb, pb, sem = opener(nc, ctx)
        cT = sb("cT", [P, KD, 2])
        sig = sb("mod_sig", [P, KD, 2])
        act_c = sb("act_c", [P, KD, 2])
        adaw = [sb(f"adaw{u}", [P, KD, 512]) for u in range(2)]
        adab = sb("adab", [P, MODS * KD])
        one = sb("one_plus", [P, KD, 2])
        pm = pb("mod_psum", [P, MODS * KD, 2])
        in_c, in_small = sem("m_in_c"), sem("m_in_small")
        in_w = [sem(f"m_in_w{u}") for u in range(2)]
        used_w = [sem(f"m_used_w{u}") for u in range(2)]
        sig_done, c_ready, link_s = sem("m_sig"), sem("m_c"), sem("m_link")
        count_from_one(nc, used_w)
        with nc.Block() as block:

            @block.sync
            def _(sp):
                sp.dma_start(cT[:], d["cT"]).then_inc(in_c, 16)
                with sp.Fori(0, NB // 2) as i:
                    for u in range(2):
                        sp.wait_ge(used_w[u], i + 1)
                        sp.dma_start(adaw[u][:], d["ada_w"][bass.ds(i * 2 + u, 1), :, :, :]
                                     .rearrange("o p k n -> p (o k) n")).then_inc(in_w[u], 16)

            @block.scalar
            def _(act):
                act.dma_start(adab[:], d["ada_b"]).then_inc(in_small, 16)
                act.dma_start(g["n1g"][:], d["norm1_g"]).then_inc(in_small, 16)
                act.dma_start(g["n2g"][:], d["norm2_g"]).then_inc(in_small, 16)
                act.dma_start(g["nfg"][:], d["final_g"]).then_inc(in_small, 16)
                act.wait_ge(in_c, 16)
                nc.scalar.activation(sig[:], cT[:], ACT.Sigmoid).then_inc(sig_done, 1)

            @block.tensor
            def _(pe):
                pe.wait_ge(c_ready, 1)
                with pe.Fori(0, NB // 2) as i:
                    for u in range(2):
                        pe.wait_ge(in_w[u], i * 16 + 16)
                        for c in range(4):
                            for k in range(KD):
                                mm = nc.tensor.matmul(pm[:, bass.ds(i * 8 + u * 4 + c, 1), :],
                                                      adaw[u][:, k, c * P:(c + 1) * P], act_c[:, k, :],
                                                      start=(k == 0), stop=(k == KD - 1))
                        mm.then_inc(used_w[u], 1)

            @block.vector
            def _(dve):
                link = linker(dve, link_s)
                dve.wait_ge(sig_done, 1)
                nc.vector.tensor_tensor(act_c[:], cT[:], sig[:], ALU.mult).then_inc(c_ready, 1)
                for u in range(2):
                    dve.wait_ge(used_w[u], NB // 2 + 1)
                dve.wait_ge(in_small, 64)
                link(nc.vector.tensor_tensor(g["mod"][:], pm[:], adab[:].unsqueeze(2).broadcast_to([P, MODS * KD, 2]),
                                             ALU.add))
                for part, gain, out in ((1, "n1g", "gain1"), (4, "n2g", "gain2")):
                    link(nc.vector.tensor_scalar(one[:], g["mod"][:, part * KD:(part + 1) * KD, :], 1.0, None, ALU.add))
                    link(nc.vector.tensor_tensor(g[out][:], one[:],
                                                 g[gain][:].unsqueeze(2).broadcast_to([P, KD, 2]), ALU.mult))


def rms_norm(nc, g, name, x_dram, out, gain, shift):
    with ExitStack() as ctx:
        sb, pb, sem = opener(nc, ctx)
        xT = sb(name + "_xT", [P, KD, T])
        sq = sb(name + "_sq", [P, 2, T])
        rs = sb(name + "_rs", [P, T])
        ones = sb(name + "_ones", [P, P])
        eps = sb(name + "_eps", [P, 1])
        ps = pb(name + "_ps", [P, 3 * 512])
        in_x, sq_done, sum_done = sem(name + "_in_x"), sem(name + "_sq"), sem(name + "_sum")
        root_done, ones_done, link_s = sem(name + "_root"), sem(name + "_ones"), sem(name + "_link")
        with nc.Block() as block:

            @block.sync
            def _(sp):
                for k in range(KD):
                    sp.dma_start(xT[:, k, :], x_dram[k]).then_inc(in_x, 16)

            @block.scalar
            def _(act):
                act.wait_ge(in_x, 16 * KD)
                for k in range(KD):
                    if k >= 2:
                        act.wait_ge(sum_done, k - 1)
                    nc.scalar.activation(sq[:, k % 2, :], xT[:, k, :], ACT.Square).then_inc(sq_done, 1)
                act.wait_ge(sum_done, KD)
                act.wait_ge(ones_done, 2)
                nc.scalar.activation(rs[:], ps[:, 0:T], ACT.Sqrt, bias=eps[:, 0:1], scale=1.0 / D)\
                    .then_inc(root_done, 1)

            @block.tensor
            def _(pe):
                pe.wait_ge(ones_done, 1)
                for k in range(KD):
                    pe.wait_ge(sq_done, k + 1)
                    for a, b in COLS:
                        mm = nc.tensor.matmul(ps[:, a:b], ones[:], sq[:, k % 2, a:b],
                                              start=(k == 0), stop=(k == KD - 1))
                    mm.then_inc(sum_done, 1)

            @block.vector
            def _(dve):
                link = linker(dve, link_s)
                nc.vector.memset(ones[:], 1.0).then_inc(ones_done, 1)
                nc.vector.memset(eps[:], NORM_EPS).then_inc(ones_done, 1)
                dve.wait_ge(root_done, 1)
                dve.wait_ge(in_x, 16 * KD)
                link(nc.vector.reciprocal(rs[:], rs[:]))
                for k in range(KD):
                    link(nc.vector.tensor_tensor(out[:, k, :], xT[:, k, :], rs[:], ALU.mult))
                    for s, a, b in SEGS:
                        link(nc.vector.tensor_scalar(
                            out[:, k, a:b], out[:, k, a:b], gain[:, k, s:s + 1],
                            None if shift is None else shift[:, k, s:s + 1],
                            ALU.mult, ALU.bypass if shift is None else ALU.add))


def projection(nc, name, hT, weights, blocks, out_dram, pairs_of=2):
    with ExitStack() as ctx:
        sb, pb, sem = opener(nc, ctx)
        w = [sb(f"{name}_w{u}", [P, KD, P]) for u in range(2)]
        o = [sb(f"{name}_o{u}", [P, T]) for u in range(2)]
        ps = [pb(f"{name}_ps{u}", [P, 3 * 512]) for u in range(2)]
        in_w = [sem(f"{name}_in_w{u}") for u in range(2)]
        mm_done = [sem(f"{name}_mm{u}") for u in range(2)]
        copied = [sem(f"{name}_cp{u}") for u in range(2)]
        stored = [sem(f"{name}_st{u}") for u in range(2)]
        n = blocks // 2
        count_from_one(nc, copied, mm_done, stored)
        with nc.Block() as block:

            @block.sync
            def _(sp):
                with sp.Fori(0, n) as i:
                    for u in range(2):
                        sp.wait_ge(mm_done[u], i + 1)
                        sp.dma_start(w[u][:], weights[bass.ds(i * 2 + u, 1), :, :, :]
                                     .rearrange("o p k n -> p (o k) n")).then_inc(in_w[u], 16)

            @block.tensor
            def _(pe):
                with pe.Fori(0, n) as i:
                    for u in range(2):
                        pe.wait_ge(in_w[u], i * 16 + 16)
                        pe.wait_ge(copied[u], i + 1)
                        for a, b in COLS:
                            for k in range(KD):
                                mm = nc.tensor.matmul(ps[u][:, a:b], w[u][:, k, :], hT[:, k, a:b],
                                                      start=(k == 0), stop=(k == KD - 1))
                        mm.then_inc(mm_done[u], 1)

            @block.scalar
            def _(act):
                with act.Fori(0, n) as i:
                    act.wait_ge(mm_done[0], i + 2)
                    act.wait_ge(stored[0], i * 16 + 1)
                    nc.scalar.activation(o[0][:], ps[0][:, 0:T], ACT.Copy).then_inc(copied[0], 1)
                    for u in range(2):
                        act.wait_ge(copied[u], i + 2)
                        act.dma_start(out_dram[bass.ds(i * 2 + u, 1), :, :].rearrange("o p t -> p (o t)"), o[u][:])\
                            .then_inc(stored[u], 16)
                for u in range(2):
                    act.wait_ge(stored[u], n * 16 + 1)

            @block.vector
            def _(dve):
                with dve.Fori(0, n) as i:
                    dve.wait_ge(mm_done[1], i + 2)
                    dve.wait_ge(stored[1], i * 16 + 1)
                    nc.vector.tensor_copy(o[1][:], ps[1][:, 0:T]).then_inc(copied[1], 1)


def qkv_projection(nc, hT, weights, out_dram):
    with ExitStack() as ctx:
        sb, pb, sem = opener(nc, ctx)
        w = [sb(f"qkv_w{u}", [P, KD, 512]) for u in range(2)]
        o = [sb(f"qkv_o{u}", [P, 512]) for u in range(2)]
        ps = [pb(f"qkv_ps{u}", [P, 512]) for u in range(2)]
        in_w = [sem(f"qkv_in_w{a}") for a in range(A_BLOCKS)]
        mm_done, copied = sem("qkv_mm"), sem("qkv_cp")
        stored = [sem(f"qkv_st{u}") for u in range(2)]
        with nc.Block() as block:

            @block.sync
            def _(sp):
                for a in range(A_BLOCKS):
                    if a >= 2:
                        sp.wait_ge(mm_done, NT * (a - 1))
                    sp.dma_start(w[a % 2][:], weights[a]).then_inc(in_w[a], 16)

            @block.gpsimd
            def _(pool):
                for n in range(A_BLOCKS * NT):
                    pool.wait_ge(copied, n + 1)
                    pool.dma_start(out_dram[n % NT, :, n // NT, :], o[n % 2][:]).then_inc(stored[n % 2], 16)
                for u in range(2):
                    pool.wait_ge(stored[u], 16 * A_BLOCKS * NT // 2)

            @block.tensor
            def _(pe):
                for n in range(A_BLOCKS * NT):
                    a, t = n // NT, n % NT
                    if t == 0:
                        pe.wait_ge(in_w[a], 16)
                    if n >= 2:
                        pe.wait_ge(copied, n - 1)
                    for k in range(KD):
                        mm = nc.tensor.matmul(ps[n % 2][:], hT[:, k, t * P:(t + 1) * P], w[a % 2][:, k, :],
                                              start=(k == 0), stop=(k == KD - 1))
                    mm.then_inc(mm_done, 1)

            @block.vector
            def _(dve):
                for n in range(A_BLOCKS * NT):
                    dve.wait_ge(mm_done, n + 1)
                    if n >= 2:
                        dve.wait_ge(stored[n % 2], 16 * (n // 2))
                    nc.vector.tensor_copy(o[n % 2][:], ps[n % 2][:]).then_inc(copied, 1)


def retention(nc, g, d, qkv, oT, state_out):
    C = P
    with ExitStack() as outer:
        sb, pb, sem = opener(nc, outer)
        kv = sb("ret_kv", [P, NT, 2 * PAIRS, HD])
        rin = sb("ret_rin", [P, NT, 2 * PAIRS, HD])
        cst = sb("ret_cst", [P, 6, P])
        col = sb("ret_col", [P, 2])
        lgp, lgr = sb("ret_lgp", [P, 2, PAIRS]), sb("ret_lgr", [P, 2, H])
        qd = sb("ret_qd", [P, 2, PAIRS, P])
        sd = sb("ret_sd", [P, 2, H])
        cd = sb("ret_cd", [P, 2, PAIRS])
        mask = sb("ret_mask", [P, H, P])
        qkT_dram = nc.dram_tensor("ret_qkT", [NT, P, 2 * PAIRS, P], F32).ap()
        n = NT // 2

        with ExitStack() as ctx:
            sb, pb, sem = opener(nc, ctx)
            tmp = sb("ret_tmp", [P, 4, 16])
            mt = sb("ret_mt", [P, 2, P])
            x = [sb(f"ret_x{u}", [P, 3, 512]) for u in range(2)]
            cos = [sb(f"ret_cos{u}", [P, 2, HD]) for u in range(2)]
            sin = [sb(f"ret_sin{u}", [P, 2, HD // 2]) for u in range(2)]
            xc = sb("ret_xc", [P, 2, 512])
            t1, t2 = sb("ret_t1", [P, 2, 256]), sb("ret_t2", [P, 2, 256])
            ks = [sb(f"ret_ks{u}", [P, 2, 512]) for u in range(2)]
            rot = [sb(f"ret_rot{u}", [P, 2, 512]) for u in range(2)]
            qkT = [sb(f"ret_qkTs{u}", [P, 2 * PAIRS, P]) for u in range(2)]
            ident = sb("ret_ident", [P, P])
            ptr = [pb(f"ret_ptr{u}", [P, 2 * PAIRS, P]) for u in range(2)]
            pkv = [pb(f"ret_pkv{u}", [P, 2 * PAIRS, P]) for u in range(2)]
            in_c, abs_s, dec_s, lg_s, tab_s = sem("r_in_c"), sem("r_abs"), sem("r_dec"), sem("r_lg"), sem("r_tab")
            mask_e, mask_u, link_s, link2_s = sem("r_mask_e"), sem("r_mask_u"), sem("r_link"), sem("r_link2")
            in_x = [sem(f"r_in_x{u}") for u in range(2)]
            rot_s = [sem(f"r_rot{u}") for u in range(2)]
            ks_s = [sem(f"r_ks{u}") for u in range(2)]
            mm_s = [sem(f"r_mm{u}") for u in range(2)]
            tcp_s = [sem(f"r_tcp{u}") for u in range(2)]
            kcp_s = [sem(f"r_kcp{u}") for u in range(2)]
            st_s = [sem(f"r_st{u}") for u in range(2)]
            count_from_one(nc, kcp_s, mask_u, mm_s, rot_s, st_s, tcp_s)
            with nc.Block() as block:

                @block.sync
                def _(sp):
                    sp.dma_start(lgp[:], d["decay_part"]).then_inc(in_c, 16)
                    sp.dma_start(lgr[:], d["decay_row"]).then_inc(in_c, 16)
                    sp.dma_start(cst[:], d["c_ret"]).then_inc(in_c, 16)
                    sp.dma_start(col[:], d["c_col"]).then_inc(in_c, 16)
                    sp.dma_start(ident[:], d["c_ident"]).then_inc(in_c, 16)
                    with sp.Fori(0, n) as i:
                        for u in range(2):
                            sp.wait_ge(mm_s[u], i + 1)
                            sp.wait_ge(rot_s[u], i + 1)
                            t = i * 2 + u
                            sp.dma_start(x[u][:], qkv[bass.ds(t, 1), :, :, :].rearrange("o p a n -> p (o a) n"))\
                                .then_inc(in_x[u], 16)
                            sp.dma_start(cos[u][:], d["c_cos"][bass.ds(t, 1), :, :, :]
                                         .rearrange("o p a n -> p (o a) n")).then_inc(in_x[u], 16)
                            sp.dma_start(sin[u][:], d["c_sin"][bass.ds(t, 1), :, :, :]
                                         .rearrange("o p a n -> p (o a) n")).then_inc(in_x[u], 16)

                @block.scalar
                def _(act):
                    link = linker(act, abs_s)
                    act.wait_ge(in_c, 80)
                    link(nc.scalar.activation(tmp[:, 0, 0:8], lgp[:].rearrange("p a b -> p (a b)"), ACT.Abs))
                    link(nc.scalar.activation(tmp[:, 1, :], lgr[:].rearrange("p a b -> p (a b)"), ACT.Abs))
                    link(nc.scalar.activation(tmp[:, 2, 0:8], tmp[:, 0, 0:8], ACT.Exp, scale=-1.0))
                    link(nc.scalar.activation(tmp[:, 3, :], tmp[:, 1, :], ACT.Exp, scale=-1.0))
                    act.wait_ge(dec_s, 2)
                    link(nc.scalar.activation(tmp[:, 2, 0:8], tmp[:, 2, 0:8], ACT.Ln))
                    nc.scalar.activation(tmp[:, 3, :], tmp[:, 3, :], ACT.Ln).then_inc(lg_s, 1)
                    act.wait_ge(dec_s, 4)
                    for r in range(2):
                        for j in range(PAIRS):
                            nc.scalar.activation(qd[:, r, j, :], cst[:, r, :], ACT.Exp, scale=lgp[:, r, j:j + 1])\
                                .then_inc(tab_s, 1)
                        nc.scalar.activation(sd[:, r, :], lgr[:, r, :], ACT.Exp, scale=col[:, r:r + 1])\
                            .then_inc(tab_s, 1)
                    nc.scalar.activation(cd[:], lgp[:], ACT.Exp, scale=float(C)).then_inc(tab_s, 1)
                    for h in range(H):
                        for r in range(2):
                            if h:
                                act.wait_ge(mask_u, h + 1)
                            nc.scalar.activation(mt[:, r, :], cst[:, 2 + r, :], ACT.Exp, scale=lgr[:, r, h:h + 1])\
                                .then_inc(mask_e, 1)
                    with act.Fori(0, n) as i:
                        for u in range(2):
                            act.wait_ge(mm_s[u], i + 2)
                            act.wait_ge(st_s[u], i * 16 + 1)
                            nc.scalar.activation(qkT[u][:], ptr[u][:], ACT.Copy).then_inc(tcp_s[u], 1)
                            act.wait_ge(tcp_s[u], i + 2)
                            act.dma_start(qkT_dram[bass.ds(i * 2 + u, 1), :, :, :]
                                          .rearrange("o p a n -> p (o a) n"), qkT[u][:]).then_inc(st_s[u], 16)
                    for u in range(2):
                        act.wait_ge(st_s[u], 16 * n + 1)

                @block.tensor
                def _(pe):
                    pe.wait_ge(in_c, 80)
                    with pe.Fori(0, n) as i:
                        for u in range(2):
                            pe.wait_ge(rot_s[u], i + 2)
                            pe.wait_ge(tcp_s[u], i + 1)
                            for a in range(2 * PAIRS):
                                nc.tensor.transpose(ptr[u][:, a, :], rot[u][:].rearrange("p a n -> p (a n)")
                                                    [:, a * P:(a + 1) * P], ident[:])
                            pe.wait_ge(ks_s[u], i + 1)
                            pe.wait_ge(kcp_s[u], i + 1)
                            for r in range(2):
                                for j in range(PAIRS):
                                    mm = nc.tensor.matmul(pkv[u][:, r * PAIRS + j, :], ks[u][:, r, j * P:(j + 1) * P],
                                                          x[u][:, 2, j * P:(j + 1) * P], start=True, stop=True)
                            mm.then_inc(mm_s[u], 1)

                @block.vector
                def _(dve):
                    link = linker(dve, link_s)
                    dve.wait_ge(abs_s, 4)
                    nc.vector.tensor_scalar(tmp[:, 2, 0:8], tmp[:, 2, 0:8], 1.0, None, ALU.add).then_inc(dec_s, 1)
                    nc.vector.tensor_scalar(tmp[:, 3, :], tmp[:, 3, :], 1.0, None, ALU.add).then_inc(dec_s, 1)
                    dve.wait_ge(lg_s, 1)
                    dve.wait_ge(abs_s, 5)
                    for lg, q, w in ((lgp, 2, 8), (lgr, 3, 16)):
                        v = lg[:].rearrange("p a b -> p (a b)")
                        nc.vector.scalar_tensor_tensor(v, v, 0.0, tmp[:, q, 0:w], ALU.min, ALU.subtract)\
                            .then_inc(dec_s, 1)
                    for h in range(H):
                        dve.wait_ge(mask_e, 2 * h + 2)
                        link(nc.vector.tensor_tensor(mt[:], mt[:], cst[:, 4:6, :], ALU.mult))
                        nc.vector.tensor_tensor(mask[:, (h % 2) * PAIRS + h // 2, :], mt[:, 0, :], mt[:, 1, :], ALU.add).then_inc(mask_u, 1)
                    dve.wait_ge(tab_s, 11)
                    with dve.Fori(0, n) as i:
                        step = linker(dve, link2_s, again=True)
                        for u in range(2):
                            xq = x[u][:, 0:2, :]
                            dve.wait_ge(in_x[u], i * 48 + 48)
                            step(nc.vector.tensor_tensor(
                                xc[:].rearrange("p a (h c) -> p a h c", h=H), xq.rearrange("p a (h c) -> p a h c", h=H),
                                cos[u][:].unsqueeze(2).broadcast_to([P, 2, H, HD]), ALU.mult))
                            for a in range(2):
                                v = xq[:, a, :].rearrange("p (h s j f) -> p h s j f", h=H, s=2, j=2)
                                sn = sin[u][:, a, :].rearrange("p (s f) -> p s f", s=2).unsqueeze(1)\
                                    .broadcast_to([P, H, 2, 16])
                                for j, t in ((0, t1), (1, t2)):
                                    step(nc.vector.tensor_tensor(
                                        t[:, a, :].rearrange("p (h s f) -> p h s f", h=H, s=2), v[:, :, :, j, :],
                                        sn, ALU.mult))
                            dve.wait_ge(mm_s[u], i + 1)
                            half = lambda w, j: w[:].rearrange("p a (b j f) -> p (a b) j f", j=2, f=16)[:, :, j, :]
                            full = lambda w: w[:].rearrange("p a (b f) -> p (a b) f", f=16)
                            step(nc.vector.tensor_tensor(half(rot[u], 0), half(xc, 0), full(t2), ALU.subtract))
                            nc.vector.tensor_tensor(half(rot[u], 1), half(xc, 1), full(t1), ALU.add)\
                                .then_inc(rot_s[u], 1)
                            dve.wait_ge(rot_s[u], i + 2)
                            step(nc.vector.tensor_tensor(
                                ks[u][:, 0, :].rearrange("p (h c) -> p h c", h=H),
                                rot[u][:, 1, :].rearrange("p (h c) -> p h c", h=H),
                                sd[:, 0, :].unsqueeze(2).broadcast_to([P, H, HD]), ALU.mult))
                            nc.vector.tensor_tensor(
                                ks[u][:, 1, :].rearrange("p (h c) -> p h c", h=H),
                                rot[u][:, 1, :].rearrange("p (h c) -> p h c", h=H),
                                sd[:, 1, :].unsqueeze(2).broadcast_to([P, H, HD]), ALU.mult).then_inc(ks_s[u], 1)
                            dve.wait_ge(mm_s[u], i + 2)
                            for e in range(2):
                                q = slice(e * HD, (e + 1) * HD)
                                cp = nc.vector.tensor_copy(
                                    kv[q, bass.ds(i * 2 + u, 1), :, :].rearrange("p o a c -> p (o a) c"),
                                    pkv[u][q, :, q])
                            cp.then_inc(kcp_s[u], 1)

        with ExitStack() as ctx:
            sb, pb, sem = opener(nc, ctx)
            qk = [sb(f"ret_qk{u}", [P, 2 * PAIRS, P]) for u in range(2)]
            v = [sb(f"ret_v{u}", [P, 512]) for u in range(2)]
            qs = [sb(f"ret_qs{u}", [P, 2, PAIRS, P]) for u in range(2)]
            rs = [sb(f"ret_rs{u}", [P, 2 * PAIRS, HD]) for u in range(2)]
            pm = [sb(f"ret_pm{u}", [P, H, P]) for u in range(2)]
            fin = sb("ret_fin", [P, 2 * PAIRS, HD])
            dead = sb("ret_dead", [P, 2 * PAIRS, HD])
            psc = [pb(f"ret_psc{u}", [P, H, P]) for u in range(2)]
            po = [pb(f"ret_po{u}", [P, PAIRS, P]) for u in range(2)]
            in_s, zero_s, rec_s, fin_s, out_s = sem("r2_in"), sem("r2_zero"), sem("r2_rec"), sem("r2_fin"), sem("r2_out")
            in_q = [sem(f"r2_in_q{u}") for u in range(2)]
            rs_s = [sem(f"r2_rs{u}") for u in range(2)]
            qs_s = [sem(f"r2_qs{u}") for u in range(2)]
            sc_s = [sem(f"r2_sc{u}") for u in range(2)]
            pm_s = [sem(f"r2_pm{u}") for u in range(2)]
            po_s = [sem(f"r2_po{u}") for u in range(2)]
            oc_s = [sem(f"r2_oc{u}") for u in range(2)]
            FW, BW = slice(0, PAIRS), slice(PAIRS, 2 * PAIRS)
            count_from_one(nc, oc_s, pm_s, po_s)
            with nc.Block() as block:

                @block.sync
                def _(sp):
                    sp.dma_start(rin[:, 2, FW, :], d["ret_state"][:, FW, :]).then_inc(in_s, 16)
                    sp.dma_start(rin[:, NT - 1, BW, :], d["ret_state"][:, BW, :]).then_inc(in_s, 16)
                    with sp.Fori(0, n) as i:
                        for u in range(2):
                            sp.wait_ge(po_s[u], i + 1)
                            t = i * 2 + u
                            sp.dma_start(qk[u][:], qkT_dram[bass.ds(t, 1), :, :, :].rearrange("o p a n -> p (o a) n"))\
                                .then_inc(in_q[u], 16)
                            sp.dma_start(v[u][:], qkv[bass.ds(t, 1), :, 2, :].rearrange("o p n -> p (o n)"))\
                                .then_inc(in_q[u], 16)
                    sp.wait_ge(fin_s, 1)
                    sp.dma_start(state_out, fin[:]).then_inc(out_s, 16)
                    sp.wait_ge(out_s, 16)

                @block.scalar
                def _(act):
                    act.wait_ge(fin_s, 1)
                    with act.Fori(0, n) as i:
                        for u in range(2):
                            act.wait_ge(po_s[u], i + 1)
                            nc.scalar.activation(rs[u][:], rin[:, bass.ds(i * 2 + u, 1), :, :]
                                                 .rearrange("p o a c -> p (o a) c"), ACT.Copy).then_inc(rs_s[u], 1)
                            act.wait_ge(po_s[u], i + 2)
                            nc.scalar.activation(oT[:, :, bass.ds((i * 2 + u) * P, P)], po[u][:], ACT.Copy)\
                                .then_inc(oc_s[u], 1)

                @block.tensor
                def _(pe):
                    with pe.Fori(0, n) as i:
                        for u in range(2):
                            pe.wait_ge(in_q[u], i * 32 + 32)
                            pe.wait_ge(pm_s[u], i + 1)
                            for h in range(H):
                                e, j = h % 2, h // 2
                                q = slice(e * HD, (e + 1) * HD)
                                mm = nc.tensor.matmul(psc[u][:, e * PAIRS + j, :], qk[u][q, PAIRS + j, :], qk[u][q, j, :],
                                                      start=True, stop=True)
                            mm.then_inc(sc_s[u], 1)
                            pe.wait_ge(rs_s[u], i + 1)
                            pe.wait_ge(qs_s[u], i + 1)
                            pe.wait_ge(pm_s[u], i + 2)
                            pe.wait_ge(oc_s[u], i + 1)
                            for h in range(H):
                                e, j = h % 2, h // 2
                                q = slice(e * HD, (e + 1) * HD)
                                nc.tensor.matmul(po[u][q, j, :], v[u][:, h * HD:(h + 1) * HD], pm[u][:, e * PAIRS + j, :],
                                                 start=True, stop=False)
                                for r in range(2):
                                    mm = nc.tensor.matmul(po[u][q, j, :], rs[u][q, r * PAIRS + j, :],
                                                          qs[u][q, r, j, :], start=False, stop=(r == 1))
                            mm.then_inc(po_s[u], 1)

                @block.vector
                def _(dve):
                    link = linker(dve, rec_s)
                    link(nc.vector.memset(rin[:, 0, FW, :], 0.0))
                    link(nc.vector.memset(rin[:, 1, BW, :], 0.0))
                    dve.wait_ge(in_s, 32)
                    for lo, hi in ((0, 1), (2, NT - 1)):
                        for s in range(hi - lo + 1):
                            for r, t, to, part in ((0, lo + s, lo + s + 1, FW), (1, hi - s, hi - s - 1, BW)):
                                if lo <= to <= hi:
                                    dst = rin[:, to, part, :]
                                else:
                                    dst = (fin if hi == 1 else dead)[:, part, :]
                                link(nc.vector.tensor_tensor(dst, rin[:, t, part, :],
                                                             cd[:, r, :].unsqueeze(2).broadcast_to([P, PAIRS, HD]),
                                                             ALU.mult))
                                link(nc.vector.tensor_tensor(dst, dst, kv[:, t, part, :], ALU.add))
                    nc.vector.memset(dead[:, 0, 0:1], 0.0).then_inc(fin_s, 1)
                    with dve.Fori(0, n) as i:
                        for u in range(2):
                            dve.wait_ge(in_q[u], i * 32 + 32)
                            dve.wait_ge(po_s[u], i + 1)
                            for r in range(2):
                                op = nc.vector.tensor_tensor(qs[u][:, r, :, :], qk[u][:, 0:PAIRS, :], qd[:, r, :, :],
                                                             ALU.mult)
                            op.then_inc(qs_s[u], 1)
                            dve.wait_ge(sc_s[u], i + 1)
                            nc.vector.tensor_tensor(pm[u][:], psc[u][:], mask[:], ALU.mult).then_inc(pm_s[u], 1)


CH = 64
NCH = T // CH
GRP = 4
NG = NCH // GRP
GT = GRP * CH
CTX_CH = T_CTX // CH
LEVELS = [1, 2, 4, 8, 16, 32]
QA, QR, QB, QK = range(4)
RW_COLS = 16
COL_W0, COL_A0, COL_KK, COL_KA, COL_RK = 9, 11, 13, 14, 15


def rwkv_operands(nc, d, projT, gs, xs, vs, bonus_v):
    with ExitStack() as ctx:
        sb, pb, sem = opener(nc, ctx)
        raw = sb("rw_raw", [P, 3, T])
        rkv = sb("rw_rkv", [P, 3, T])
        cols = sb("rw_cols", [P, RW_COLS])
        omka = sb("rw_omka", [P, 1])
        wa = sb("rw_wa", [P, 2, P])
        lora = sb("rw_lora", [P, T])
        reset = sb("rw_reset", [P, T])
        blk = sb("rw_blk", [P, P])
        eps = sb("rw_eps", [P, 1])
        kk, sq, nrm, rkk, bon = (sb("rw_" + x, [P, T]) for x in ("kk", "sq", "nrm", "rkk", "bon"))
        sw, a, cum, u2, kd = (sb("rw_" + x, [P, T]) for x in ("sw", "a", "cum", "u2", "kd"))
        eR, eA, eN = (sb("rw_" + x, [P, T]) for x in ("eR", "eA", "eN"))
        xo = sb("rw_xo", [P, 4, T])
        psA, psB = pb("rw_psA", [P, 3 * 512]), pb("rw_psB", [P, 3 * 512])
        names = ("in0", "in", "tanh", "kkr", "sqr", "n2", "norm", "rkk", "bonmm", "bonv", "zw", "za", "sw", "a", "lw",
                 "u", "e", "xo", "xst", "vc", "vst", "link", "init")
        (in0_s, in_s, tanh_s, kkr_s, sqr_s, n2_s, norm_s, rkk_s, bonmm_s, bonv_s, zw_s, za_s, sw_s, a_s, lw_s,
         u_s, e_s, xo_s, xst_s, vc_s, vst_s, link_s, init_s) = (sem("e1_" + x) for x in names)
        count_from_one(nc, a_s, sw_s, vst_s, xo_s, xst_s)
        with nc.Block() as block:

            @block.sync
            def _(sp):
                sp.dma_start(lora[:], projT[DWDA]).then_inc(in0_s, 16)
                sp.dma_start(reset[:], d["c_reset"]).then_inc(in0_s, 16)
                sp.dma_start(blk[:], d["c_blk"]).then_inc(in0_s, 16)
                with sp.Fori(0, PAIRS) as i:
                    sp.wait_ge(xo_s, 2 * i + 1)
                    for q, first in enumerate((WR, WK, WV)):
                        sp.dma_start(raw[:, q, :], projT[bass.ds(i + first, 1), :, :].rearrange("o p t -> p (o t)"))\
                            .then_inc(in_s, 16)
                    sp.dma_start(cols[:], d["rw_cols"][bass.ds(i, 1), :, :].rearrange("o p t -> p (o t)"))\
                        .then_inc(in_s, 16)
                    sp.dma_start(wa[:], d["rw_wa"][bass.ds(i, 1), :, :, :].rearrange("o p a t -> p (o a) t"))\
                        .then_inc(in_s, 16)
                    groups = bass.ds(i * NG, NG)
                    sp.wait_ge(vc_s, i + 1)
                    sp.dma_start(vs[groups, :, :].rearrange("g p t -> p g t"),
                                   rkv[:, 2, :].rearrange("p (g t) -> p g t", g=NG)).then_inc(vst_s, 16)
                    sp.wait_ge(bonv_s, i + 1)
                    sp.dma_start(bonus_v[bass.ds(i, 1), :, :].rearrange("o p t -> p (o t)"), bon[:])\
                        .then_inc(vst_s, 16)
                    for r in range(2):
                        sp.wait_ge(xo_s, 2 * i + r + 2)
                        for q in range(4):
                            sp.dma_start(xs[groups, :, r, q, :].rearrange("g p t -> p g t"),
                                           xo[:, q, :].rearrange("p (g t) -> p g t", g=NG)).then_inc(xst_s, 16)
                sp.wait_ge(vst_s, 32 * PAIRS + 1)
                sp.wait_ge(xst_s, 16 * 8 * PAIRS + 1)

            @block.scalar
            def _(act):
                act.wait_ge(in0_s, 48)
                nc.scalar.activation(lora[0:HD, :], lora[0:HD, :], ACT.Tanh).then_inc(tanh_s, 1)
                act.wait_ge(init_s, 1)
                with act.Fori(0, PAIRS) as i:
                    act.wait_ge(kkr_s, i + 1)
                    nc.scalar.activation(sq[:], kk[:], ACT.Square).then_inc(sqr_s, 1)
                    act.wait_ge(n2_s, i + 1)
                    nc.scalar.activation(nrm[:], psA[:, 0:T], ACT.Sqrt, bias=eps[:, 0:1]).then_inc(norm_s, 1)
                    for r in range(2):
                        n = 2 * i + r
                        act.wait_ge(zw_s, n + 1)
                        act.wait_ge(xo_s, n + 1)
                        nc.scalar.activation(sw[:], psA[:, 0:T], ACT.Sigmoid, bias=cols[:, COL_W0 + r:COL_W0 + r + 1])\
                            .then_inc(sw_s, 1)
                        act.wait_ge(za_s, n + 1)
                        nc.scalar.activation(a[:], psB[:, 0:T], ACT.Sigmoid, bias=cols[:, COL_A0 + r:COL_A0 + r + 1])\
                            .then_inc(a_s, 1)
                        act.wait_ge(u_s, n + 1)
                        for out, src, sign in (((eR, cum, 1.0), (eA, u2, 1.0), (eN, cum, -1.0)) if r == 0 else
                                               ((eR, u2, -1.0), (eA, cum, -1.0), (eN, u2, 1.0))):
                            nc.scalar.activation(out[:], src[:], ACT.Exp, scale=sign).then_inc(e_s, 1)
                        nc.scalar.activation(gs[:, bass.ds(i, 1), r, :].rearrange("p o c -> p (o c)"),
                                             cum[:].rearrange("p (c t) -> p c t", t=CH)[:, :, CH - 1], ACT.Exp)\
                            .then_inc(e_s, 1)

            @block.tensor
            def _(pe):
                pe.wait_ge(in0_s, 48)
                pe.wait_ge(tanh_s, 1)
                with pe.Fori(0, PAIRS) as i:
                    pe.wait_ge(sqr_s, i + 1)
                    pe.wait_ge(sw_s, 2 * i + 1)
                    for x, y in COLS:
                        mm = nc.tensor.matmul(psA[:, x:y], blk[:], sq[:, x:y], start=True, stop=True)
                    mm.then_inc(n2_s, 1)
                    pe.wait_ge(rkk_s, i + 1)
                    pe.wait_ge(a_s, 2 * i + 1)
                    for x, y in COLS:
                        mm = nc.tensor.matmul(psB[:, x:y], blk[:], rkk[:, x:y], start=True, stop=True)
                    mm.then_inc(bonmm_s, 1)
                    pe.wait_ge(in_s, 80 * i + 80)
                    for r in range(2):
                        if r == 0:
                            pe.wait_ge(norm_s, i + 1)
                        else:
                            pe.wait_ge(sw_s, 2 * i + 2)
                        for x, y in COLS:
                            mm = nc.tensor.matmul(psA[:, x:y], wa[0:HD, r, :], lora[0:HD, x:y], start=True, stop=True)
                        mm.then_inc(zw_s, 1)
                        if r == 0:
                            pe.wait_ge(bonv_s, i + 1)
                        else:
                            pe.wait_ge(a_s, 2 * i + 2)
                        for x, y in COLS:
                            mm = nc.tensor.matmul(psB[:, x:y], wa[HD:P, r, :], lora[HD:P, x:y], start=True, stop=True)
                        mm.then_inc(za_s, 1)

            @block.vector
            def _(dve):
                V = nc.vector
                V.memset(eps[:], 1e-12).then_inc(init_s, 1)
                dve.wait_ge(in0_s, 48)
                with dve.Fori(0, PAIRS) as i:
                    link = linker(dve, link_s, again=True)
                    dve.wait_ge(in_s, 80 * i + 80)
                    dve.wait_ge(vst_s, 32 * i + 1)
                    for q in range(3):
                        w = lambda j: cols[:, 3 * q + j:3 * q + j + 1]
                        x, y = raw[:, q, :], rkv[:, q, :]
                        link(V.tensor_scalar(y, x, w(1), None, ALU.mult))
                        for _, s, e in SEGS:
                            link(V.scalar_tensor_tensor(y[:, s + 1:e], x[:, s:e - 1], w(0), y[:, s + 1:e],
                                                        ALU.mult, ALU.add))
                            ins = V.scalar_tensor_tensor(y[:, s:e - 1], x[:, s + 1:e], w(2), y[:, s:e - 1],
                                                         ALU.mult, ALU.add)
                            if q == 2 and e == T:
                                ins.then_inc(vc_s, 1)
                            else:
                                link(ins)
                    r_, k_, v_ = (rkv[:, q, :] for q in range(3))
                    V.tensor_scalar(kk[:], k_, cols[:, COL_KK:COL_KK + 1], None, ALU.mult).then_inc(kkr_s, 1)
                    V.scalar_tensor_tensor(rkk[:], r_, cols[:, COL_RK:COL_RK + 1], k_, ALU.mult, ALU.mult)\
                        .then_inc(rkk_s, 1)
                    link(V.tensor_scalar(omka[:], cols[:, COL_KA:COL_KA + 1], -1.0, 1.0, ALU.mult, ALU.add))
                    dve.wait_ge(norm_s, i + 1)
                    dve.wait_ge(kkr_s, i + 1)
                    link(V.reciprocal(nrm[:], nrm[:]))
                    link(V.tensor_tensor(kk[:], kk[:], nrm[:], ALU.mult))
                    dve.wait_ge(bonmm_s, i + 1)
                    dve.wait_ge(vc_s, i + 1)
                    V.tensor_tensor(bon[:], psB[:, 0:T], v_, ALU.mult).then_inc(bonv_s, 1)
                    for r in range(2):
                        n = 2 * i + r
                        dve.wait_ge(sw_s, n + 2)
                        link(V.tensor_scalar(sw[:], sw[:], -math.exp(-0.5), None, ALU.mult))
                        link(V.tensor_tensor_scan(cum[:], reset[:], sw[:], 0.0, ALU.mult, ALU.add))
                        c3 = cum[:].rearrange("p (c t) -> p c t", t=CH)
                        link(V.tensor_scalar(kd[:, 0:NCH], c3[:, :, CH - 1], -0.5, None, ALU.mult))
                        link(V.tensor_tensor(c3, c3, kd[:, 0:NCH].unsqueeze(2).broadcast_to([P, NCH, CH]), ALU.add))
                        V.tensor_tensor(u2[:], cum[:], sw[:], ALU.subtract).then_inc(u_s, 1)
                        dve.wait_ge(a_s, n + 2)
                        link(V.tensor_scalar(kd[:], a[:], cols[:, COL_KA:COL_KA + 1], omka[:, 0:1], ALU.mult, ALU.add))
                        link(V.tensor_tensor(kd[:], kd[:], k_, ALU.mult))
                        link(V.tensor_tensor(a[:], a[:], kk[:], ALU.mult))
                        dve.wait_ge(e_s, 4 * n + 4)
                        dve.wait_ge(xst_s, 64 * n + 1)
                        V.tensor_tensor(xo[:, QA, :], kk[:], eA[:], ALU.mult)
                        V.tensor_tensor(xo[:, QR, :], r_, eR[:], ALU.mult)
                        link(V.tensor_tensor(xo[:, QB, :], a[:], eN[:], ALU.mult))
                        V.tensor_tensor(xo[:, QK, :], kd[:], eN[:], ALU.mult).then_inc(xo_s, 1)


def rwkv_chunks(nc, d, xs, vs, ef, mn):
    U = 2 * GRP
    with ExitStack() as ctx:
        sb, pb, sem = opener(nc, ctx)
        x = [sb(f"ch_x{u}", [P, 2, 4, GT]) for u in range(2)]
        vT = [sb(f"ch_vT{u}", [P, GT]) for u in range(2)]
        ident, idb = sb("ch_ident", [P, P]), sb("ch_idb", [P, HD])
        mar = sb("ch_mar", [P, 2, 2 * CH])
        mba = sb("ch_mba", [P, 2, CH])
        lev = sb("ch_lev", [P, len(LEVELS), 2, CH])
        gb = sb("ch_gb", [P, U, 3, CH])
        gk = sb("ch_gk", [P, U, 2, CH])
        lm = sb("ch_lm", [P, U, CH])
        ct = sb("ch_ct", [P, len(LEVELS) + 1, U, CH])
        ay = sb("ch_ay", [P, U, 2, CH])
        kn, vn = sb("ch_kn", [P, U, CH]), sb("ch_vn", [P, GRP, HD])
        tt, uu, yy = sb("ch_tt", [P, U, CH]), sb("ch_uu", [P, U, CH]), sb("ch_yy", [P, U, CH])
        xx, yn = sb("ch_xx", [P, U, CH]), sb("ch_yn", [P, U, CH])
        oe = sb("ch_oe", [P, U + GRP, CH])
        om = sb("ch_om", [P, U, 2, CH])
        b01, b23 = pb("ch_b01", [P, U, 2, CH]), pb("ch_b23", [P, U, 2, CH])
        b4, b5, b6, b7 = (pb(f"ch_b{n}", [P, U, CH]) for n in (4, 5, 6, 7))
        names = ("in0", "gram", "gbm", "gkm", "lm", "nat", "ncp", "vmm", "vcp", "ct", "t0", "y", "ycp", "tm", "um",
                 "tu", "y0", "y0c", "xy", "xyc", "me", "nf", "ec", "mc", "nc", "est", "mst", "link")
        (in0_s, gram_s, gbm_s, gkm_s, lm_s, nat_s, ncp_s, vmm_s, vcp_s, ct_s, t0_s, y_s, ycp_s, tm_s, um_s,
         tu_s, y0_s, y0c_s, xy_s, xyc_s, me_s, nf_s, ec_s, mc_s, nc_s, est_s, mst_s, link_s) = (
            sem("e2_" + n) for n in names)
        in_s = [sem(f"e2_inx{u}") for u in range(2)]
        fc_s = [sem(f"e2_fc{u}") for u in range(2)]
        passed_s = sem("e2_passed")
        NL = len(LEVELS) - 1
        half = [slice(0, HD), slice(HD, P)]
        units = [(e, r, c) for r in range(2) for c in range(GRP) for e in range(2)]
        count_from_one(nc, ct_s, est_s, fc_s, mc_s, mst_s, nc_s, nf_s, tu_s, um_s, xyc_s)
        with nc.Block() as block:

            @block.sync
            def _(sp):
                for t, s in ((ident, "c_ident"), (idb, "c_idb"), (mar, "c_mar"), (mba, "c_mba"), (lev, "c_lev")):
                    sp.dma_start(t[:], d[s]).then_inc(in0_s, 16)
                with sp.Fori(0, PAIRS * NG // 2) as i:
                    for u in range(2):
                        sp.wait_ge(fc_s[u], i + 1)
                        sp.dma_start(x[u][:], xs[bass.ds(2 * i + u, 1), :, :, :, :].rearrange("o p r q t -> p (o r) q t"))\
                            .then_inc(in_s[u], 16)
                        sp.dma_start(vT[u][:], vs[bass.ds(2 * i + u, 1), :, :].rearrange("o p t -> p (o t)"))\
                            .then_inc(in_s[u], 16)

            def parts(u):
                X = lambda e, r, q, c: x[u][half[e], r, q, c * CH:(c + 1) * CH]
                return X

            @block.tensor
            def _(pe):
                MM = nc.tensor.matmul
                pe.wait_ge(in0_s, 80)
                with pe.Fori(0, PAIRS * NG // 2) as i:
                    for u in range(2):
                        n = 2 * i + u
                        X = parts(u)
                        hold(pe, passed_s, (in_s[u], 32 * i + 32), (xyc_s, 2 * n + 1))
                        for e, r, c in units:
                            MM(b01[half[e], r * GRP + c, :, :], X(e, r, QB, c),
                               x[u][half[e], r, QA:QR + 1, c * CH:(c + 1) * CH], start=True, stop=True)
                        hold(pe, passed_s, (mc_s, n + 1))
                        for e, r, c in units:
                            MM(b23[half[e], r * GRP + c, :, :], X(e, r, QK, c),
                               x[u][half[e], r, QA:QR + 1, c * CH:(c + 1) * CH], start=True, stop=True)
                        for e, r, c in units:
                            mm = MM(b4[half[e], r * GRP + c, :], X(e, r, QA, c), X(e, r, QB, c), start=True, stop=True)
                        mm.then_inc(gram_s, 1)
                        hold(pe, passed_s, (nc_s, n + 1), (fc_s[1 - u], i + u + 1))
                        for q, b in ((QA, b5), (QB, b6), (QK, b7)):
                            for e, r, c in units:
                                mm = MM(b[half[e], r * GRP + c, :], X(e, r, q, c), ident[half[e], half[e]],
                                        start=True, stop=True)
                        mm.then_inc(nat_s, 1)
                        hold(pe, passed_s, (lm_s, n + 1))
                        for c in range(GRP):
                            for e in range(2):
                                mm = MM(b4[half[e], c, :], vT[u][half[e], c * CH:(c + 1) * CH],
                                        ident[half[e], half[e]], start=True, stop=True)
                        mm.then_inc(vmm_s, 1)
                        hold(pe, passed_s, (ncp_s, 3 * n + 3))
                        for l in range(NL):
                            hold(pe, passed_s, (ct_s, n * (NL + 2) + l + 3 + 1),
                                 (t0_s, 2 * n + 2) if l == 0 else (tu_s, n * (2 * NL - 1) + 2 * l + 1))
                            for e, r, c in units:
                                j = r * GRP + c
                                mm = MM(b5[half[e], j, :], ct[half[e], l + 1, j, :], tt[half[e], j, :],
                                        start=True, stop=True)
                            mm.then_inc(y_s, 1)
                            hold(pe, passed_s, (ycp_s, n * NL + l + 1))
                            if l < NL - 1:
                                for e, r, c in units:
                                    j = r * GRP + c
                                    mm = MM(b6[half[e], j, :], uu[half[e], j, :], yy[half[e], j, :],
                                            start=True, stop=True)
                                mm.then_inc(tm_s, 1)
                            for e, r, c in units:
                                j = r * GRP + c
                                mm = MM(b7[half[e], j, :], yy[half[e], j, :], uu[half[e], j, :],
                                        start=True, stop=True)
                            mm.then_inc(um_s, 1)
                        hold(pe, passed_s, (gkm_s, n + 1), (vcp_s, n + 1))
                        for e, r, c in units:
                            j = r * GRP + c
                            mm = MM(b4[half[e], j, :], gk[half[e], j, 0, :], vn[half[e], c, :], start=True, stop=True)
                        mm.then_inc(y0_s, 1)
                        hold(pe, passed_s, (y0c_s, n + 1), (tu_s, (n + 1) * (2 * NL - 1) + 1))
                        for e, r, c in units:
                            j = r * GRP + c
                            mm = MM(b01[half[e], j, :, :], uu[half[e], j, :], ay[half[e], j, :, :],
                                    start=True, stop=True)
                        mm.then_inc(xy_s, 1)
                        hold(pe, passed_s, (xyc_s, 2 * n + 2 + 1))
                        for e, r, c in units:
                            j = r * GRP + c
                            mm = MM(b23[half[e], j, :, :], xx[half[e], j, :], gb[half[e], j, 1:3, :],
                                    start=True, stop=True)
                        mm.then_inc(me_s, 1)
                        for e, r, c in units:
                            j = r * GRP + c
                            MM(b5[half[e], j, :], kn[half[e], j, :], vn[half[e], c, :], start=True, stop=False)
                            MM(b5[half[e], j, :], gb[half[e], j, 2, :], yn[half[e], j, :], start=False, stop=True)
                        for c in range(GRP):
                            for e in range(2):
                                for r in range(2):
                                    j = r * GRP + c
                                    MM(b6[half[e], c, :], vn[half[e], c, :], gk[half[e], j, 1, :],
                                       start=(r == 0), stop=False)
                                    mm = MM(b6[half[e], c, :], yn[half[e], j, :], gb[half[e], j, 1, :],
                                            start=False, stop=(r == 1))
                        mm.then_inc(nf_s, 1)

            @block.scalar
            def _(act):
                A = nc.scalar.activation
                with act.Fori(0, PAIRS * NG // 2) as i:
                    for u in range(2):
                        n = 2 * i + u
                        act.wait_ge(nat_s, n + 1)
                        act.wait_ge(nf_s, n + 1)
                        A(ay[:, :, 0, :], b5[:], ACT.Copy).then_inc(ncp_s, 1)
                        A(gb[:, :, 2, :], b6[:], ACT.Copy).then_inc(ncp_s, 1)
                        A(kn[:], b7[:], ACT.Copy).then_inc(ncp_s, 1)
                        act.wait_ge(vmm_s, n + 1)
                        A(vn[:], b4[:, 0:GRP, :], ACT.Copy).then_inc(vcp_s, 1)
                        for l in range(NL):
                            act.wait_ge(y_s, n * NL + l + 1)
                            if l:
                                act.wait_ge(um_s, n * NL + l + 1)
                            A(yy[:], b5[:], ACT.Copy).then_inc(ycp_s, 1)
                        act.wait_ge(y0_s, n + 1)
                        A(ay[:, :, 1, :], b4[:], ACT.Copy).then_inc(y0c_s, 1)
                        act.wait_ge(xy_s, n + 1)
                        A(xx[:], b01[:, :, 0, :], ACT.Copy).then_inc(xyc_s, 1)
                        A(yn[:], b01[:, :, 1, :], ACT.Copy, scale=-1.0).then_inc(xyc_s, 1)
                        act.wait_ge(nf_s, n + 2)
                        act.wait_ge(mst_s, 32 * n + 1)
                        A(om[:, :, 1, :], b5[:], ACT.Copy).then_inc(nc_s, 1)
                        act.wait_ge(nc_s, n + 2)
                        act.wait_ge(mc_s, n + 2)
                        for r in range(2):
                            act.dma_start(mn[r, bass.ds(n * GRP, GRP), :, :].rearrange("c p k -> p c k"),
                                          om[:, r * GRP:(r + 1) * GRP, :, :].rearrange("p c m k -> p c (m k)"))\
                                .then_inc(mst_s, 16)
                        act.wait_ge(fc_s[u], i + 2)
                        act.dma_start(ef[bass.ds(n, 1), :, :, :].rearrange("o p a t -> p (o a) t"), oe[:])\
                            .then_inc(est_s, 16)
                act.wait_ge(mst_s, 32 * PAIRS * NG + 1)
                act.wait_ge(est_s, 16 * PAIRS * NG + 1)

            @block.gpsimd
            def _(pool):
                with pool.Fori(0, PAIRS * NG // 2) as i:
                    for u in range(2):
                        n = 2 * i + u
                        def bc(k, flip):
                            order = (1, 0) if flip else (0, 1)
                            return [lev[:, k, r, :].unsqueeze(1).broadcast_to([P, GRP, CH]) for r in order]
                        pool.wait_ge(lm_s, n + 1)
                        pool.wait_ge(gbm_s, n + 1)
                        pool.wait_ge(um_s, n * NL + 1)
                        for k, src in [(len(LEVELS), lm)] + [(k, gb) for k in range(len(LEVELS))]:
                            m = bc(0, True) if src is lm else bc(k, False)
                            for r in range(2):
                                j = slice(r * GRP, (r + 1) * GRP)
                                op = nc.gpsimd.tensor_tensor(ct[:, k, j, :], lm[:, j, :] if src is lm else gb[:, j, 0, :],
                                                             m[r], ALU.mult)
                            op.then_inc(ct_s, 1)

            @block.vector
            def _(dve):
                V = nc.vector
                dve.wait_ge(in0_s, 80)
                rc = "p (r c) q t -> p r c (q t)"
                with dve.Fori(0, PAIRS * NG // 2) as i:
                    for u in range(2):
                        n = 2 * i + u
                        dve.wait_ge(gram_s, n + 1)
                        dve.wait_ge(nf_s, n + 1)
                        dve.wait_ge(ct_s, n * (NL + 2) + 1)
                        for r in range(2):
                            j = slice(r * GRP, (r + 1) * GRP)
                            m = mar[:, r, :].unsqueeze(1).broadcast_to([P, GRP, 2 * CH])
                            op = V.tensor_tensor(gb[:, j, 0:2, :].rearrange("p c q t -> p c (q t)"),
                                                 b01[:, j, :, :].rearrange("p c q t -> p c (q t)"), m, ALU.mult)
                        op.then_inc(gbm_s, 1)
                        for r in range(2):
                            j = slice(r * GRP, (r + 1) * GRP)
                            op = V.tensor_tensor(lm[:, j, :], b4[:, j, :],
                                                 mba[:, r, :].unsqueeze(1).broadcast_to([P, GRP, CH]), ALU.mult)
                        op.then_inc(lm_s, 1)
                        for r in range(2):
                            j = slice(r * GRP, (r + 1) * GRP)
                            m = mar[:, r, :].unsqueeze(1).broadcast_to([P, GRP, 2 * CH])
                            op = V.tensor_tensor(gk[:, j, :, :].rearrange("p c q t -> p c (q t)"),
                                                 b23[:, j, :, :].rearrange("p c q t -> p c (q t)"), m, ALU.mult)
                        op.then_inc(gkm_s, 1)
                        eye = idb[:].unsqueeze(1).broadcast_to([P, U, CH])
                        dve.wait_ge(ct_s, n * (NL + 2) + 2 + 1)
                        V.tensor_tensor(tt[:], eye, ct[:, len(LEVELS), :, :], ALU.subtract).then_inc(t0_s, 1)
                        V.tensor_tensor(uu[:], eye, ct[:, 0, :, :], ALU.subtract).then_inc(t0_s, 1)
                        for l in range(NL):
                            if l == 0:
                                dve.wait_ge(t0_s, 2 * n + 2)
                            if l < NL - 1:
                                dve.wait_ge(tm_s, n * (NL - 1) + l + 1)
                                V.tensor_tensor(tt[:], tt[:], b6[:], ALU.subtract).then_inc(tu_s, 1)
                            dve.wait_ge(um_s, n * NL + l + 2)
                            V.tensor_tensor(uu[:], uu[:], b7[:], ALU.subtract).then_inc(tu_s, 1)
                            dve.wait_ge(tu_s, n * (2 * NL - 1) + min(2 * l + 2, 2 * NL - 1) + 1)
                        dve.wait_ge(me_s, n + 1)
                        dve.wait_ge(est_s, 16 * n + 1)
                        dve.wait_ge(mst_s, 32 * n + 1)
                        V.tensor_tensor(oe[:, 0:U, :].rearrange("p (r c) t -> p r c t", r=2),
                                        x[u][:, :, QR, :].rearrange("p r (c t) -> p r c t", c=GRP),
                                        b23[:, :, 0, :].rearrange("p (r c) t -> p r c t", r=2), ALU.subtract)\
                            .then_inc(ec_s, 1)
                        V.tensor_tensor(om[:, :, 0, :], eye, b23[:, :, 1, :], ALU.subtract).then_inc(mc_s, 1)
                        dve.wait_ge(nf_s, n + 2)
                        V.tensor_copy(oe[:, U:U + GRP, :], b6[:, 0:GRP, :]).then_inc(fc_s[u], 1)


def rwkv_scan(nc, d, mn, gs, qs, state_out):
    U = 2 * PAIRS
    LAT = NCH - CTX_CH
    with ExitStack() as ctx:
        sb, pb, sem = opener(nc, ctx)
        mb = [sb(f"sc_mn{u}", [P, U, 2 * CH]) for u in range(2)]
        q = sb("sc_q", [P, U, HD])
        t = sb("sc_t", [P, U, HD])
        fin = sb("sc_fin", [P, U, HD])
        init = sb("sc_init", [P, U, HD])
        g2 = sb("sc_g2", [P, PAIRS, 2, NCH])
        ps = pb("sc_ps", [P, U, HD])
        init_s, mm_s, q_s, cp_s, t_s, fin_s, out_s, link_s, g_s = (
            sem("e3_" + x) for x in ("init", "mm", "q", "cp", "t", "fin", "out", "link", "g"))
        in_s = [sem(f"e3_in{u}") for u in range(2)]
        half = [slice(0, HD), slice(HD, P)]
        FW, BW = slice(0, PAIRS), slice(PAIRS, U)
        passed_s = sem("e3_passed")
        ctx_steps = [(s, CTX_CH - 1 - s) for s in range(CTX_CH)]
        mnv = [mn[r].rearrange("(j c) p k -> p c j k", c=NCH) for r in range(2)]
        count_from_one(nc, in_s, t_s)
        with nc.Block() as block:

            @block.sync
            def _(sp):
                sp.dma_start(init[:], d["rw_state"]).then_inc(init_s, 16)

                def load(u, chunks, k):
                    sp.wait_ge(t_s, k + 1)
                    for r, c in enumerate(chunks):
                        sp.dma_start(mb[u][:, r * PAIRS:(r + 1) * PAIRS, :],
                                     mnv[r][:, bass.ds(c, 1), :, :].rearrange("p o j k -> p (o j) k"))\
                            .then_inc(in_s[u], 16)

                for k, chunks in enumerate(ctx_steps):
                    if k < 2:
                        for r, c in enumerate(chunks):
                            sp.dma_start(mb[k][:, r * PAIRS:(r + 1) * PAIRS, :], mnv[r][:, c, :, :])\
                                .then_inc(in_s[k], 16)
                    else:
                        load(k % 2, chunks, k - 1)
                with sp.Fori(0, LAT // 2) as i:
                    for u in range(2):
                        s = 2 * i + u
                        load(u, (s + CTX_CH, s * -1 + (NCH - 1)), s + CTX_CH - 1)
                sp.wait_ge(fin_s, 1)
                sp.dma_start(state_out, fin[:]).then_inc(out_s, 16)
                sp.wait_ge(out_s, 16)

            @block.tensor
            def _(pe):
                def step(u, arrivals, k):
                    hold(pe, passed_s, (in_s[u], arrivals + 1), (q_s, k + 1))
                    for j in range(U):
                        for e in range(2):
                            mm = nc.tensor.matmul(ps[half[e], j, :], mb[u][half[e], j, 0:CH], q[half[e], j, :],
                                                  start=True, stop=True)
                    mm.then_inc(mm_s, 1)

                for k in range(CTX_CH):
                    step(k % 2, 32 * (k // 2 + 1), k)
                with pe.Fori(0, LAT // 2) as i:
                    for u in range(2):
                        step(u, 32 * i + 32 * (CTX_CH // 2 + 1), 2 * i + (u + CTX_CH))

            @block.scalar
            def _(act):
                def keep(chunks, k):
                    act.wait_ge(q_s, k + 1)
                    for c, w in zip(chunks, (FW, BW)):
                        nc.scalar.activation(qs[:, bass.ds(c, 1), w, :].rearrange("p o j v -> p (o j) v"),
                                             q[:, w, :], ACT.Copy).then_inc(cp_s, 1)

                for k, chunks in enumerate(ctx_steps):
                    keep(chunks, k)
                with act.Fori(0, LAT) as i:
                    keep((i + CTX_CH, i * -1 + (NCH - 1)), i + CTX_CH)

            @block.vector
            def _(dve):
                V = nc.vector
                link = linker(dve, link_s)
                gv = lambda r, c, a=gs: a[:, :, r, bass.ds(c, 1)].broadcast_to([P, PAIRS, HD])
                V.tensor_tensor(g2[:, :, 0, 0:NCH - 1], gs[:, :, 0, 0:NCH - 1], gs[:, :, 0, 1:NCH], ALU.mult)\
                    .then_inc(g_s, 1)
                V.tensor_tensor(g2[:, :, 1, 1:NCH], gs[:, :, 1, 1:NCH], gs[:, :, 1, 0:NCH - 1], ALU.mult)\
                    .then_inc(g_s, 1)
                V.memset(g2[:, :, 0, NCH - 1:NCH], 0.0).then_inc(g_s, 1)
                V.memset(g2[:, :, 1, 0:1], 0.0).then_inc(g_s, 1)
                V.memset(q[:], 0.0).then_inc(q_s, 1)
                dve.wait_ge(g_s, 4)
                dve.wait_ge(init_s, 16)

                def summed(k, u):
                    dve.wait_ge(mm_s, k + 1)
                    V.tensor_tensor(t[:], ps[:], mb[u][:, :, CH:2 * CH], ALU.add).then_inc(t_s, 1)
                    dve.wait_ge(t_s, k + 2)
                    dve.wait_ge(cp_s, 2 * k + 2)

                def hand_over(chunks):
                    V.tensor_tensor(q[:, FW, :], t[:, FW, :], gv(0, chunks[0], g2), ALU.mult)
                    V.tensor_tensor(q[:, BW, :], t[:, BW, :], gv(1, chunks[1], g2), ALU.mult).then_inc(q_s, 1)

                for k, chunks in enumerate(ctx_steps):
                    summed(k, k % 2)
                    if k < CTX_CH - 1:
                        hand_over(chunks)
                link(V.tensor_tensor(fin[:, FW, :], t[:, FW, :], gv(0, CTX_CH - 1), ALU.mult))
                V.tensor_tensor(fin[:, BW, :], t[:, BW, :], gv(1, 0), ALU.mult).then_inc(fin_s, 1)
                V.tensor_tensor(q[:, FW, :], init[:, FW, :], gv(0, CTX_CH), ALU.mult)
                V.tensor_tensor(q[:, BW, :], init[:, BW, :], gv(1, NCH - 1), ALU.mult).then_inc(q_s, 1)
                with dve.Fori(0, LAT // 2) as i:
                    for u in range(2):
                        s = 2 * i + u
                        summed(s + CTX_CH, u)
                        hand_over((s + CTX_CH, s * -1 + (NCH - 1)))


def rwkv_outputs(nc, d, ef, qs, yT):
    U = 2 * GRP
    with ExitStack() as ctx:
        sb, pb, sem = opener(nc, ctx)
        e_ = [sb(f"y_ef{u}", [P, U + GRP, CH]) for u in range(2)]
        qv = [sb(f"y_q{u}", [P, 2, GRP, HD]) for u in range(2)]
        ps = [pb(f"y_ps{u}", [P, GRP, CH]) for u in range(2)]
        in_s, qc_s, mm_s, y_s = ([sem(f"e4_{x}{u}") for u in range(2)] for x in ("in", "qc", "mm", "y"))
        half = [slice(0, HD), slice(HD, P)]
        n2 = PAIRS // 2
        passed_s = sem("e4_passed")
        count_from_one(nc, mm_s, y_s)
        with nc.Block() as block:

            @block.sync
            def _(sp):
                with sp.Fori(0, PAIRS * NG // 2) as i:
                    for u in range(2):
                        sp.wait_ge(y_s[u], i + 1)
                        sp.dma_start(e_[u][:], ef[bass.ds(2 * i + u, 1), :, :, :].rearrange("o p a t -> p (o a) t"))\
                            .then_inc(in_s[u], 16)

            @block.scalar
            def _(act):
                for j in range(PAIRS):
                    for q in range(NG):
                        n = j * NG + q
                        u = n % 2
                        if n >= 2:
                            act.wait_ge(mm_s[u], n // 2 + 1)
                        for r in range(2):
                            op = nc.scalar.activation(qv[u][:, r, :, :], qs[:, q * GRP:(q + 1) * GRP, r * PAIRS + j, :],
                                                      ACT.Copy)
                        op.then_inc(qc_s[u], 1)

            @block.tensor
            def _(pe):
                with pe.Fori(0, PAIRS * NG // 2) as i:
                    for u in range(2):
                        hold(pe, passed_s, (in_s[u], 16 * i + 16), (qc_s[u], i + 1), (y_s[u], i + 1))
                        for c in range(GRP):
                            for e in range(2):
                                for r in range(2):
                                    mm = nc.tensor.matmul(ps[u][half[e], c, :], qv[u][half[e], r, c, :],
                                                          e_[u][half[e], r * GRP + c, :], start=(r == 0), stop=(r == 1))
                        mm.then_inc(mm_s[u], 1)

            @block.vector
            def _(dve):
                yv = yT[:].rearrange("p j (g t) -> p (j g) t", g=NG)
                with dve.Fori(0, PAIRS * NG // 2) as i:
                    for u in range(2):
                        dve.wait_ge(mm_s[u], i + 2)
                        nc.vector.tensor_tensor(yv[:, bass.ds(2 * i + u, 1), :].rearrange("p o t -> p (o t)"),
                                                ps[u][:].rearrange("p c t -> p (c t)"),
                                                e_[u][:, U:U + GRP, :].rearrange("p c t -> p (c t)"), ALU.add)\
                            .then_inc(y_s[u], 1)


def group_norms(nc, d, projT, bonus_v, oT, yT):
    with ExitStack() as ctx:
        sb, pb, sem = opener(nc, ctx)
        blk = sb("gn_blk", [P, P])
        eps = sb("gn_eps", [P, 1])
        wb = sb("gn_wb", [P, 2, 2, PAIRS])
        g2 = [sb(f"gn_g2{u}", [P, P]) for u in range(2)]
        dg = sb("gn_dg", [P, T])
        dev = [sb(f"gn_dev{u}", [P, T]) for u in range(2)]
        sq = [sb(f"gn_sq{u}", [P, T]) for u in range(2)]
        gate, sg, bv = sb("gn_gate", [P, T]), sb("gn_sg", [P, T]), sb("gn_bv", [P, T])
        psA, psB = pb("gn_psA", [P, 3 * 512]), pb("gn_psB", [P, 3 * 512])
        names = ("in0", "eps", "dg", "sum", "dev", "sq", "var", "root", "gmm", "sg", "rg", "out", "link")
        (in0_s, eps_s, dg_s, sum_s, dev_s, sq_s, var_s, root_s, gmm_s, sg_s, rg_s, out_s, link_s) = (
            sem("f1_" + x) for x in names)
        in_s = sem("f1_in")
        z = [oT, yT]
        flat = lambda a: a.rearrange("p o t -> p (o t)")
        count_from_one(nc, out_s, root_s)
        with nc.Block() as block:

            @block.sync
            def _(sp):
                sp.dma_start(blk[:], d["c_blk"]).then_inc(in0_s, 16)
                sp.dma_start(wb[:], d["gn_wb"]).then_inc(in0_s, 16)
                sp.dma_start(dg[:], projT[DG]).then_inc(in0_s, 16)
                with sp.Fori(0, PAIRS) as i:
                    sp.wait_ge(out_s, 2 * i + 1)
                    for dst, src in ((gate, projT), (bv, bonus_v)):
                        sp.dma_start(dst[:], src[bass.ds(i, 1), :, :].rearrange("o p t -> p (o t)"))\
                            .then_inc(in_s, 16)
                    sp.dma_start(g2[0][:], d["rw_g2"][bass.ds(i, 1), :, :].rearrange("o p t -> p (o t)"))\
                        .then_inc(in_s, 16)

            @block.scalar
            def _(act):
                act.wait_ge(in0_s, 48)
                act.wait_ge(eps_s, 1)
                nc.scalar.activation(dg[:], dg[:], ACT.Sigmoid).then_inc(dg_s, 1)
                with act.Fori(0, PAIRS) as i:
                    act.wait_ge(in_s, 48 * i + 48)
                    act.wait_ge(out_s, 2 * i + 1)
                    nc.scalar.activation(sg[:], gate[:], ACT.Sigmoid).then_inc(sg_s, 1)
                    for u in range(2):
                        act.wait_ge(dev_s, 2 * i + u + 1)
                        nc.scalar.activation(sq[u][:], dev[u][:], ACT.Square).then_inc(sq_s, 1)
                        act.wait_ge(var_s, 2 * i + u + 1)
                        nc.scalar.activation(sq[u][:], psA[:, 0:T], ACT.Sqrt, bias=eps[:, 0:1], scale=1.0 / HD)\
                            .then_inc(root_s, 1)

            @block.tensor
            def _(pe):
                pe.wait_ge(in0_s, 48)
                pe.wait_ge(dg_s, 1)
                with pe.Fori(0, PAIRS) as i:
                    for u in range(2):
                        zf = flat(z[u][:, bass.ds(i, 1), :])
                        pe.wait_ge(root_s, 2 * i + u + 1)
                        for x, y in COLS:
                            mm = nc.tensor.matmul(psA[:, x:y], blk[:], z[u][:, bass.ds(i, 1), x:y]
                                                  .rearrange("p o t -> p (o t)"), start=True, stop=True)
                        mm.then_inc(sum_s, 1)
                        pe.wait_ge(sq_s, 2 * i + u + 1)
                        for x, y in COLS:
                            mm = nc.tensor.matmul(psA[:, x:y], blk[:], sq[u][:, x:y], start=True, stop=True)
                        mm.then_inc(var_s, 1)
                    pe.wait_ge(in_s, 48 * i + 48)
                    pe.wait_ge(out_s, 2 * i + 1)
                    for x, y in COLS:
                        mm = nc.tensor.matmul(psB[:, x:y], g2[0][:], dg[:, x:y], start=True, stop=True)
                    mm.then_inc(gmm_s, 1)

            @block.vector
            def _(dve):
                V = nc.vector
                V.memset(eps[:], GN_EPS).then_inc(eps_s, 1)
                dve.wait_ge(in0_s, 48)
                with dve.Fori(0, PAIRS) as i:
                    link = linker(dve, link_s, again=True)
                    for u in range(2):
                        zf = flat(z[u][:, bass.ds(i, 1), :])
                        w, b = (wb[:, q, u, bass.ds(i, 1)] for q in range(2))
                        dve.wait_ge(sum_s, 2 * i + u + 1)
                        V.scalar_tensor_tensor(dev[u][:], psA[:, 0:T], -1.0 / HD, zf, ALU.mult, ALU.add)\
                            .then_inc(dev_s, 1)
                        if u == 0:
                            dve.wait_ge(sg_s, i + 1)
                            link(V.tensor_tensor(gate[:], gate[:], sg[:], ALU.mult))
                        dve.wait_ge(root_s, 2 * i + u + 2)
                        link(V.reciprocal(sq[u][:], sq[u][:]))
                        link(V.tensor_tensor(dev[u][:], dev[u][:], sq[u][:], ALU.mult))
                        link(V.tensor_scalar(dev[u][:], dev[u][:], w, b, ALU.mult, ALU.add))
                        if u == 0:
                            V.tensor_tensor(zf, dev[u][:], gate[:], ALU.mult).then_inc(out_s, 1)
                        else:
                            link(V.tensor_tensor(dev[u][:], dev[u][:], bv[:], ALU.add))
                            dve.wait_ge(gmm_s, i + 1)
                            link(V.tensor_copy(sq[0][:, 0:1], psB[:, 0:1]))
                            V.tensor_tensor(zf, psB[:, 0:T], dev[u][:], ALU.mult).then_inc(out_s, 1)


def branches(nc, d, projT, oT, yT, merged):
    with ExitStack() as ctx:
        sb, pb, sem = opener(nc, ctx)
        w = [sb(f"br_w{u}", [P, 2, PAIRS, P]) for u in range(2)]
        ga = [sb(f"br_ga{u}", [P, 2, T]) for u in range(2)]
        t1 = sb("br_t1", [P, T])
        t2 = sb("br_t2", [P, T])
        ps = [pb(f"br_ps{q}", [P, 3 * 512]) for q in range(2)]
        in_s = [sem(f"f2_in{u}") for u in range(2)]
        ing_s = [sem(f"f2_ing{u}") for u in range(2)]
        mm_s = [sem(f"f2_mm{q}") for q in range(2)]
        sg_s, cp_s, out_s = sem("f2_sg"), sem("f2_cp"), sem("f2_out")
        z = [oT, yT]
        count_from_one(nc, cp_s, out_s)
        with nc.Block() as block:

            @block.sync
            def _(sp):
                with sp.Fori(0, KD // 2) as i:
                    for u in range(2):
                        sp.wait_ge(out_s, 2 * i + 1) if u == 0 else sp.wait_ge(out_s, 2 * i + 1)
                        m = 2 * i + u
                        sp.dma_start(w[u][:], d["w_br"][bass.ds(m, 1), :, :, :, :].rearrange("o p q k n -> p (o q) k n"))\
                            .then_inc(in_s[u], 16)
                        for q, first in enumerate((GA, GB)):
                            sp.dma_start(ga[u][:, q, :], projT[bass.ds(m + first, 1), :, :]
                                         .rearrange("o p t -> p (o t)")).then_inc(ing_s[u], 16)

            @block.scalar
            def _(act):
                with act.Fori(0, KD // 2) as i:
                    for u in range(2):
                        act.wait_ge(ing_s[u], 32 * i + 32)
                        nc.scalar.activation(ga[u][:], ga[u][:], ACT.Sigmoid).then_inc(sg_s, 1)

            @block.tensor
            def _(pe):
                with pe.Fori(0, KD // 2) as i:
                    for u in range(2):
                        m = 2 * i + u
                        pe.wait_ge(in_s[u], 16 * i + 16)
                        for q in range(2):
                            pe.wait_ge(cp_s, 2 * m + q + 1) if q == 0 else pe.wait_ge(cp_s, 2 * m + 1)
                            for x, y in COLS:
                                for k in range(PAIRS):
                                    mm = nc.tensor.matmul(ps[q][:, x:y], w[u][:, q, k, :], z[q][:, k, x:y],
                                                          start=(k == 0), stop=(k == PAIRS - 1))
                            mm.then_inc(mm_s[q], 1)

            @block.vector
            def _(dve):
                V = nc.vector
                with dve.Fori(0, KD // 2) as i:
                    for u in range(2):
                        m = 2 * i + u
                        dve.wait_ge(sg_s, m + 1)
                        for q, t in enumerate((t1, t2)):
                            dve.wait_ge(mm_s[q], m + 1)
                            if q == 0:
                                dve.wait_ge(out_s, m + 1)
                            V.tensor_tensor(t[:], ps[q][:, 0:T], ga[u][:, q, :], ALU.mult).then_inc(cp_s, 1)
                        dve.wait_ge(cp_s, 2 * m + 2 + 1)
                        V.tensor_tensor(merged[:, bass.ds(m, 1), :].rearrange("p o t -> p (o t)"), t1[:], t2[:],
                                        ALU.add).then_inc(out_s, 1)


def out_projection(nc, d, g, merged, x1):
    with ExitStack() as ctx:
        sb, pb, sem = opener(nc, ctx)
        w = [sb(f"op_w{u}", [P, KD, P]) for u in range(2)]
        x = [sb(f"op_x{u}", [P, T]) for u in range(2)]
        ps = [pb(f"op_ps{u}", [P, 3 * 512]) for u in range(2)]
        in_s, mm_s, out_s, st_s = ([sem(f"f3_{n}{u}") for u in range(2)] for n in ("in", "mm", "out", "st"))
        count_from_one(nc, out_s, st_s)
        with nc.Block() as block:

            @block.sync
            def _(sp):
                with sp.Fori(0, KD // 2) as i:
                    for u in range(2):
                        sp.wait_ge(st_s[u], 16 * i + 1)
                        sp.dma_start(w[u][:], d["w_out"][bass.ds(2 * i + u, 1), :, :, :].rearrange("o p k n -> p (o k) n"))\
                            .then_inc(in_s[u], 16)
                        sp.dma_start(x[u][:], d["xT"][bass.ds(2 * i + u, 1), :, :].rearrange("o p t -> p (o t)"))\
                            .then_inc(in_s[u], 16)

            @block.tensor
            def _(pe):
                with pe.Fori(0, KD // 2) as i:
                    for u in range(2):
                        pe.wait_ge(in_s[u], 32 * i + 32)
                        pe.wait_ge(out_s[u], i + 1)
                        for a, b in COLS:
                            for k in range(KD):
                                mm = nc.tensor.matmul(ps[u][:, a:b], w[u][:, k, :], merged[:, k, a:b],
                                                      start=(k == 0), stop=(k == KD - 1))
                        mm.then_inc(mm_s[u], 1)

            @block.vector
            def _(dve):
                g1 = g["mod"][:, 2 * KD:3 * KD, :]
                with dve.Fori(0, KD // 2) as i:
                    for u in range(2):
                        dve.wait_ge(mm_s[u], i + 1)
                        dve.wait_ge(in_s[u], 32 * i + 32)
                        for s, a, b in SEGS:
                            op = nc.vector.scalar_tensor_tensor(
                                x[u][:, a:b], ps[u][:, a:b], g1[:, bass.ds(2 * i + u, 1), s:s + 1]
                                .rearrange("p o s -> p (o s)"), x[u][:, a:b], ALU.mult, ALU.add)
                        op.then_inc(out_s[u], 1)

            @block.scalar
            def _(act):
                with act.Fori(0, KD // 2) as i:
                    for u in range(2):
                        act.wait_ge(out_s[u], i + 2)
                        act.dma_start(x1[bass.ds(2 * i + u, 1), :, :].rearrange("o p t -> p (o t)"), x[u][:])\
                            .then_inc(st_s[u], 16)
                for u in range(2):
                    act.wait_ge(st_s[u], 16 * KD // 2 + 1)


def store_rows(nc, name, pairs):
    with ExitStack() as ctx:
        done = opener(nc, ctx)[2](name)
        block = ctx.enter_context(nc.Block())

        @block.sync
        def _(sp):
            for dst, src in pairs:
                sp.dma_start(dst, src).then_inc(done, 16)
            sp.wait_ge(done, 16 * len(pairs))


N_KEYS = 128
TOPK = 16
SLOTS = H * TOPK
TG = 256
GROUPS = T // TG
TB = T_CTX // TG


def peer_select(nc, d, hT, slots):
    NTC = 2 * NT
    with ExitStack() as ctx:
        sb, pb, sem = opener(nc, ctx)
        w = [sb(f"ps_w{c}", [P, KD, P]) for c in range(2)]
        keys = sb("ps_keys", [P, 2, N_KEYS])
        qT = [sb(f"ps_qT{c}", [P, T]) for c in range(2)]
        sc = sb("ps_sc", [P, NTC, N_KEYS])
        sc2 = sb("ps_sc2", [P, NTC, N_KEYS])
        v = sb("ps_v", [P, NTC, TOPK])
        ix = sb("ps_ix", [P, NTC, TOPK], U32)
        ixf = sb("ps_ixf", [P, NTC, TOPK])
        cand, cand2 = sb("ps_cand", [P, NT, TOPK, TOPK]), sb("ps_cand2", [P, NT, TOPK, TOPK])
        top = sb("ps_top", [P, NT, TOPK])
        pos, pa = sb("ps_pos", [P, NT, TOPK], U32), sb("ps_pa", [P, NT, TOPK], U32)
        paf = sb("ps_paf", [P, NT, TOPK])
        ex, sm = sb("ps_ex", [P, NT, TOPK]), sb("ps_sm", [P, NT])
        iota = sb("ps_iota", [P, TOPK])
        ident = sb("ps_ident", [P, P])
        res = sb("ps_res", [P, 3, NT, SLOTS])
        resT = sb("ps_resT", [P, 3, T])
        psq = pb("ps_psq", [P, 3 * 512])
        pss = pb("ps_pss", [P, NTC, N_KEYS])
        names = ("in0", "qmm", "qcp", "smm", "scp", "used", "sub", "ex", "head", "tr", "tcp", "st", "link")
        (in0_s, qmm_s, qcp_s, smm_s, scp_s, used_s, sub_s, ex_s, head_s, tr_s, tcp_s, st_s, link_s) = (
            sem("g1_" + x) for x in names)
        inw_s = [sem(f"g1_inw{c}") for c in range(2)]
        ink_s = sem("g1_ink")
        passed_s = sem("g1_passed")
        TR = 5
        count_from_one(nc, qcp_s, qmm_s, scp_s, smm_s, tcp_s, used_s)
        with nc.Block() as block:

            @block.sync
            def _(sp):
                sp.dma_start(iota[:], d["c_iota"][:, 0:TOPK]).then_inc(in0_s, 16)
                sp.dma_start(ident[:], d["c_ident"]).then_inc(in0_s, 16)
                with sp.Fori(0, H) as i:
                    for c in range(2):
                        sp.wait_ge(qmm_s, 2 * i + 1)
                        sp.dma_start(w[c][:], d["peer_wq"][bass.ds(2 * i + c, 1), :, :, :]
                                     .rearrange("o p k n -> p (o k) n")).then_inc(inw_s[c], 16)
                    sp.wait_ge(smm_s, i + 1)
                    sp.dma_start(keys[:], d["peer_keys"][bass.ds(i, 1), :, :, :].rearrange("o p c n -> p (o c) n"))\
                        .then_inc(ink_s, 16)
                sp.wait_ge(tcp_s, 3 * NT // TR + 1)
                for q in range(GROUPS):
                    sp.dma_start(slots[q], resT[:, :, q * TG:(q + 1) * TG]).then_inc(st_s, 16)
                sp.wait_ge(st_s, 16 * GROUPS)

            @block.tensor
            def _(pe):
                with pe.Fori(0, H) as i:
                    for c in range(2):
                        pe.wait_ge(inw_s[c], 16 * i + 16)
                        pe.wait_ge(qcp_s, 2 * i + c + 1)
                        for a, b in COLS:
                            for k in range(KD):
                                mm = nc.tensor.matmul(psq[:, a:b], w[c][:, k, :], hT[:, k, a:b],
                                                      start=(k == 0), stop=(k == KD - 1))
                        mm.then_inc(qmm_s, 1)
                    pe.wait_ge(qcp_s, 2 * i + 2 + 1)
                    pe.wait_ge(ink_s, 16 * i + 16)
                    pe.wait_ge(scp_s, i + 1)
                    for t in range(NT):
                        for c in range(2):
                            mm = nc.tensor.matmul(pss[:, 2 * t + c, :], qT[c][:, t * P:(t + 1) * P], keys[:, c, :],
                                                  start=True, stop=True)
                    mm.then_inc(smm_s, 1)
                pe.wait_ge(head_s, H)
                pe.wait_ge(scp_s, H + 1)
                pe.wait_ge(in0_s, 32)
                for n in range(3 * NT // TR):
                    if n >= 2:
                        pe.wait_ge(tcp_s, n)
                    for y in range(TR):
                        q, t = divmod(n * TR + y, NT)
                        mm = nc.tensor.transpose(pss[:, 8 * (n % 2) + y, :], res[:, q, t, :], ident[:])
                    mm.then_inc(tr_s, 1)

            @block.scalar
            def _(act):
                with act.Fori(0, H) as i:
                    for c in range(2):
                        act.wait_ge(qmm_s, 2 * i + c + 2)
                        act.wait_ge(smm_s, i + 1)
                        nc.scalar.activation(qT[c][:], psq[:, 0:T], ACT.Copy).then_inc(qcp_s, 1)
                    act.wait_ge(smm_s, i + 2)
                    act.wait_ge(used_s, i + 1)
                    nc.scalar.activation(sc[:], pss[:], ACT.Copy).then_inc(scp_s, 1)
                    act.wait_ge(sub_s, i + 1)
                    nc.scalar.activation(ex[:], ex[:], ACT.Exp).then_inc(ex_s, 1)
                for n in range(3 * NT // TR):
                    act.wait_ge(tr_s, n + 1)
                    q, t = divmod(n * TR, NT)
                    nc.scalar.activation(resT[:, q, t * P:(t + TR) * P],
                                         pss[:, 8 * (n % 2):8 * (n % 2) + TR, :].rearrange("p a t -> p (a t)"),
                                         ACT.Copy).then_inc(tcp_s, 1)

            @block.vector
            def _(dve):
                V = nc.vector
                LOW = -3.0e38

                def top16(link, values, spare, best, at, done=None):
                    link(V.max(best[:, 0:8], values))
                    link(V.max_index(at[:, 0:8], best[:, 0:8], values))
                    link(V.match_replace(spare, best[:, 0:8], values, LOW))
                    link(V.max(best[:, 8:16], spare))
                    ins = V.max_index(at[:, 8:16], best[:, 8:16], spare)
                    link(ins) if done is None else ins.then_inc(done, 1)

                dve.wait_ge(in0_s, 32)
                with dve.Fori(0, H) as i:
                    link = linker(dve, link_s, again=True)
                    hold(dve, passed_s, (scp_s, i + 2))
                    for n in range(NTC):
                        top16(link, sc[:, n, :], sc2[:, n, :], v[:, n, :], ix[:, n, :],
                              used_s if n == NTC - 1 else None)
                    dve.wait_ge(used_s, i + 2)
                    link(V.tensor_copy(ixf[:], ix[:]))
                    vv = v[:].rearrange("p (t c) k -> p t c k", c=2)
                    link(V.tensor_tensor(cand[:], vv[:, :, 0, :].unsqueeze(3).broadcast_to([P, NT, TOPK, TOPK]),
                                         vv[:, :, 1, :].unsqueeze(2).broadcast_to([P, NT, TOPK, TOPK]), ALU.add))
                    for t in range(NT):
                        top16(link, cand[:, t, :, :].rearrange("p a b -> p (a b)"),
                              cand2[:, t, :, :].rearrange("p a b -> p (a b)"), top[:, t, :], pos[:, t, :])
                    V.tensor_tensor(ex[:], top[:], top[:, :, 0:1].broadcast_to([P, NT, TOPK]), ALU.subtract)\
                        .then_inc(sub_s, 1)
                    ixv = ixf[:].rearrange("p (t c) k -> p t c k", c=2)
                    for c, (op, n) in enumerate(((ALU.logical_shift_right, 4), (ALU.bitwise_and, 15))):
                        link(V.tensor_scalar(pa[:], pos[:], n, None, op))
                        link(V.tensor_copy(paf[:], pa[:]))
                        link(V.tensor_tensor(cand[:].rearrange("p t a b -> p (t a) b"),
                                             paf[:].rearrange("p t k -> p (t k)").unsqueeze(2)
                                             .broadcast_to([P, NT * TOPK, TOPK]),
                                             iota[:].unsqueeze(1).broadcast_to([P, NT * TOPK, TOPK]), ALU.is_equal))
                        link(V.tensor_tensor(cand[:], cand[:], ixv[:, :, c, :].unsqueeze(2)
                                             .broadcast_to([P, NT, TOPK, TOPK]), ALU.mult))
                        link(V.tensor_reduce(res[:, c, :, bass.ds(i * TOPK, TOPK)], cand[:], AX.X, ALU.add))
                    dve.wait_ge(ex_s, i + 1)
                    link(V.tensor_reduce(sm[:], ex[:], AX.X, ALU.add))
                    link(V.reciprocal(sm[:], sm[:]))
                    V.tensor_tensor(res[:, 2, :, bass.ds(i * TOPK, TOPK)], ex[:],
                                    sm[:].unsqueeze(2).broadcast_to([P, NT, TOPK]), ALU.mult).then_inc(head_s, 1)


def peer_experts(nc, g, d, h2, x1, slots, x2):
    with ExitStack() as ctx:
        sb, pb, sem = opener(nc, ctx)
        gd = sb("pe_gd", [P, N_KEYS, TG])
        hg = sb("pe_hg", [P, KD, TG])
        sl = sb("pe_sl", [P, 3, TG])
        xg = sb("pe_xg", [P, KD, TG])
        uu = [sb(f"pe_u{b}", [P, KD, P]) for b in range(2)]
        vv = [sb(f"pe_v{b}", [P, D]) for b in range(2)]
        ge = [sb(f"pe_ge{b}", [P, TG]) for b in range(2)]
        ww = [sb(f"pe_w{b}", [P, TG]) for b in range(2)]
        o1 = [sb(f"pe_o1{b}", [P, 4, P]) for b in range(2)]
        o2 = [sb(f"pe_o2{b}", [P, 4, P]) for b in range(2)]
        iota = sb("pe_iota", [P, P])
        zero = sb("pe_zero", [P, TG])
        g2t = sb("pe_g2t", [P, GROUPS, KD])
        acc = pb("pe_acc", [P, KD, TG])
        psS = [pb(f"pe_s{b}", [P, 512]) for b in range(2)]
        psG = [pb(f"pe_g{b}", [P, 4, P]) for b in range(2)]
        names = ("in0", "ing", "hot", "x", "st", "init", "zero", "fin")
        in0_s, ing_s, hot_s, x_s, st_s, init_s, zero_s, fin_s = (sem("g2_" + x) for x in names)
        oh_s, gm_s, gc_s, uin_s, vin_s, s_s, ge_s, w_s, o_s = (
            [sem(f"g2_{x}{b}") for b in range(2)] for x in ("oh", "gm", "gc", "uin", "vin", "s", "ge", "w", "o"))
        passed_s = sem("g2_passed")
        NJ = N_KEYS // 2
        NQ = TG // 8
        count_from_one(nc, gc_s, ge_s, gm_s, o_s, s_s, st_s, w_s, x_s)
        with nc.Block() as block:

            @block.sync
            def _(sp):
                sp.dma_start(iota[:], d["c_iota"]).then_inc(in0_s, 16)
                with sp.Fori(0, GROUPS) as q:
                    sp.wait_ge(x_s, q + 1)
                    sp.dma_start(sl[:], slots[bass.ds(q, 1), :, :, :].rearrange("o p a t -> p (o a) t"))\
                        .then_inc(ing_s, 16)
                    sp.dma_start(hg[:], h2[:, :, bass.ds(q * TG, TG)].rearrange("k p t -> p k t")).then_inc(ing_s, 16)
                    sp.wait_ge(st_s, 16 * q + 1)
                    sp.dma_start(xg[:], x1[:, :, bass.ds(q * TG, TG)].rearrange("k p t -> p k t")).then_inc(ing_s, 16)
                    with sp.Fori(0, NJ) as i:
                        for b in range(2):
                            n = q * NJ + i
                            j = i * 2 + b
                            sp.wait_ge(s_s[b], n + 1)
                            sp.dma_start(uu[b][:], d["peer_u"][bass.ds(j, 1), :, :, :].rearrange("o p k n -> p (o k) n"))\
                                .then_inc(uin_s[b], 16)
                            sp.wait_ge(o_s[b], n + 1)
                            sp.dma_start(vv[b][:], d["peer_v"][:, bass.ds(j, 1), :].rearrange("p o n -> p (o n)"))\
                                .then_inc(vin_s[b], 16)

            @block.scalar
            def _(act):
                with act.Fori(0, GROUPS) as q:
                    act.wait_ge(x_s, q + 1)
                    with act.Fori(0, NQ) as i:
                        for b in range(2):
                            act.wait_ge(gm_s[b], q * NQ + i + 2)
                            nc.scalar.activation(gd[:, :, bass.ds(i * 8 + b * 4, 4)].rearrange("p k t -> p t k"),
                                                 psG[b][:], ACT.Copy).then_inc(gc_s[b], 1)
                    with act.Fori(0, NJ) as i:
                        for b in range(2):
                            act.wait_ge(s_s[b], q * NJ + i + 2)
                            act.wait_ge(w_s[b], q * NJ + i + 1)
                            nc.scalar.activation(ge[b][:], psS[b][:, 0:TG], ACT.Gelu_apprx_tanh).then_inc(ge_s[b], 1)
                    act.wait_ge(x_s, q + 2)
                    act.dma_start(x2[:, :, bass.ds(q * TG, TG)].rearrange("k p t -> p k t"), xg[:]).then_inc(st_s, 16)
                act.wait_ge(st_s, 16 * GROUPS + 1)

            @block.tensor
            def _(pe):
                MM = nc.tensor.matmul
                pe.wait_ge(zero_s, 1)

                def scores(b, n):
                    pe.wait_ge(uin_s[b], 16 * n + 16)
                    pe.wait_ge(ge_s[b], n + 1)
                    for k in range(KD):
                        mm = MM(psS[b][:, 0:TG], uu[b][:, k, :], hg[:, k, :], start=(k == 0), stop=(k == KD - 1))
                    mm.then_inc(s_s[b], 1)

                def values(b, n):
                    pe.wait_ge(vin_s[b], 16 * n + 16)
                    pe.wait_ge(w_s[b], n + 2)
                    for m in range(KD):
                        mm = MM(acc[:, m, :], vv[b][:, m * P:(m + 1) * P], ww[b][:], start=False, stop=False,
                                skip_group_check=True)
                    mm.then_inc(o_s[b], 1)

                with pe.Fori(0, GROUPS) as q:
                    with pe.Fori(0, NQ) as i:
                        for b in range(2):
                            pe.wait_ge(oh_s[b], q * NQ + i + 1)
                            pe.wait_ge(gc_s[b], q * NQ + i + 1)
                            for t in range(4):
                                mm = MM(psG[b][:, t, :], o1[b][:, t, :], o2[b][:, t, :], start=True, stop=True)
                            mm.then_inc(gm_s[b], 1)
                    pe.wait_ge(x_s, q + 1)
                    for m in range(KD):
                        MM(acc[:, m, :], zero[:, 0:P], zero[:], start=(m % 2 == 0), stop=False, skip_group_check=True)
                    pe.wait_ge(ing_s, 48 * q + 48)
                    scores(0, q * NJ)
                    with pe.Fori(0, NJ - 1) as i:
                        n = q * NJ + i
                        scores(1, n)
                        values(0, n)
                        scores(0, n + 1)
                        values(1, n)
                    n = q * NJ + (NJ - 1)
                    scores(1, n)
                    values(0, n)
                    values(1, n)
                    for m in range(KD):
                        mm = MM(acc[:, m, :], zero[:, 0:P], zero[:], start=False, stop=(m % 2 == 1),
                                skip_group_check=True)
                    mm.then_inc(fin_s, 1)

            @block.vector
            def _(dve):
                V = nc.vector
                V.memset(zero[:], 0.0).then_inc(zero_s, 1)
                g2 = g["mod"][:, 5 * KD:6 * KD, :]
                for q in range(GROUPS):
                    V.tensor_copy(g2t[:, q, :], g2[:, :, 0 if q < TB else 1]).then_inc(init_s, 1)
                dve.wait_ge(in0_s, 16)
                dve.wait_ge(init_s, GROUPS)
                with dve.Fori(0, GROUPS) as q:
                    hold(dve, passed_s, (ing_s, 48 * q + 48))
                    with dve.Fori(0, NQ) as i:
                        for b in range(2):
                            dve.wait_ge(gm_s[b], q * NQ + i + 1)
                            for t in range(4):
                                at = lambda a: sl[:, a, bass.ds(i * 8 + (b * 4 + t), 1)]
                                V.tensor_scalar(o1[b][:, t, :], iota[:], at(0), None, ALU.is_equal)
                                op = V.tensor_scalar(o2[b][:, t, :], iota[:], at(1), at(2), ALU.is_equal, ALU.mult)
                            op.then_inc(oh_s[b], 1)
                    hold(dve, passed_s, *((gc_s[b], q * NQ + NQ + 1) for b in range(2)))
                    with dve.Fori(0, NJ) as i:
                        for b in range(2):
                            n = q * NJ + i
                            dve.wait_ge(ge_s[b], n + 2)
                            dve.wait_ge(o_s[b], n + 1)
                            V.tensor_tensor(ww[b][:], ge[b][:], gd[:, bass.ds(i * 2 + b, 1), :]
                                            .rearrange("p o t -> p (o t)"), ALU.mult).then_inc(w_s[b], 1)
                    dve.wait_ge(fin_s, q + 1)
                    for m in range(KD):
                        op = V.scalar_tensor_tensor(xg[:, m, :], acc[:, m, :], g2t[:, bass.ds(q, 1), m:m + 1]
                                                    .rearrange("p o m -> p (o m)"), xg[:, m, :], ALU.mult, ALU.add)
                    op.then_inc(x_s, 1)


def constants():
    f = np.float32
    i = np.arange(P)
    row, c = np.meshgrid(np.arange(T_LAT // 64), np.arange(64), indexing="ij")
    quarter = HD // 4
    inv = (f(10000.0) ** (-np.arange(quarter, dtype=f) / f(quarter))).astype(f)
    ang = np.stack([row.reshape(-1), c.reshape(-1)], 1).astype(f)[:, :, None] * inv
    ang = np.concatenate([np.zeros((T_CTX, 2, quarter), f), ang])
    scale = np.array([1.0, HD ** -0.5], f)[None, :, None]
    cos = np.repeat(np.cos(ang)[:, :, None, :], 2, axis=2).reshape(T, 1, HD) * scale
    sin = np.sin(ang).reshape(T, 1, HD // 2) * scale
    one = np.ones((P, 1))
    diff = i[None, :] - i[:, None]
    return {
        "c_cos": cos.reshape(NT, P, 2, HD).astype(f), "c_sin": sin.reshape(NT, P, 2, HD // 2).astype(f),
        "c_ret": np.stack([one * (i + 1), one * (P - i), np.maximum(diff, 0), np.maximum(-diff, 0),
                           diff >= 0, diff <= 0], axis=1).astype(f),
        "c_col": np.stack([P - 1 - i, i], axis=1).astype(f),
        "c_iota": np.repeat(np.arange(P, dtype=f)[None], P, axis=0),
        "c_ident": np.eye(P, dtype=f),
        "c_reset": np.repeat((np.arange(T) % CH != 0)[None], P, axis=0).astype(f),
        "c_blk": np.kron(np.eye(2), np.ones((HD, HD))).astype(f),
        "c_idb": np.tile(np.eye(CH), (2, 1)).astype(f),
        **chunk_masks(),
    }


def chunk_masks():
    s, t = np.arange(CH)[:, None], np.arange(CH)[None, :]
    before = [s < t, s > t]
    mar = np.stack([np.concatenate([b, b | (s == t)], axis=1) for b in before], axis=1)
    mba = np.stack([b.T for b in before], axis=1)
    lev = np.stack([np.stack([b & (s // (2 * n) == t // (2 * n)) & (s // n != t // n) for b in before], axis=1)
                    for n in LEVELS], axis=1)
    both = lambda m: np.ascontiguousarray(np.tile(m, (2,) + (1,) * (m.ndim - 1)).astype(np.float32))
    return {"c_mar": both(mar), "c_mba": both(mba), "c_lev": both(lev)}


def pair_rows(s):
    return s.reshape(2, PAIRS, 2, HD, HD).transpose(2, 3, 0, 1, 4).reshape(P, 2 * PAIRS, HD)


def layouts(i):
    a = {k: np.ascontiguousarray(v) for k, v in i.items()}
    rows = lambda w, n: w.reshape(KD, P, n, -1).transpose(2, 1, 0, 3)
    col = lambda v, n: v.reshape(n, P).T
    x = np.concatenate([a["x_prompt"][0], a["x_sample"][0]])
    out = {
        "xT": x.T.reshape(KD, P, T),
        "cT": np.stack([a["c_ctx"], a["c"][0]]).reshape(2, KD, P).transpose(2, 1, 0),
        "ada_w": rows(a["ada_w"][0], MODS * D // 512),
        "ada_b": col(a["ada_b"][0], MODS * KD),
        "norm1_g": col(a["norm1_g"][0], KD), "norm2_g": col(a["norm2_g"][0], KD),
        "final_g": np.repeat(col(a["final_norm_g"], KD)[:, :, None], 2, axis=2),
        "w_br": np.stack([a[n][0].reshape(PAIRS, P, KD, P) for n in ("w_br_a", "w_br_b")]).transpose(3, 2, 0, 1, 4),
        "w_out": rows(a["w_out"][0], KD),
        "rw_g2": a["rwkv_g2"][0].reshape(P, PAIRS, P).transpose(1, 0, 2),
        "gn_wb": np.stack([a[n][0].reshape(PAIRS, P) for n in ("ret_gn_w", "rwkv_gn_w", "ret_gn_b", "rwkv_gn_b")])
                   .reshape(2, 2, PAIRS, P).transpose(3, 0, 1, 2),
        "peer_wq": rows(a["peer_wq"][0], 2 * H),
        "peer_keys": a["peer_keys"][0].transpose(0, 3, 1, 2),
        "peer_u": a["peer_u"][0].reshape(N_KEYS, N_KEYS, KD, P).transpose(1, 3, 2, 0),
        "peer_v": a["peer_v"][0].reshape(N_KEYS, N_KEYS, D),
        "w_qkv": rows(a["w_in"][0][:, :A_BLOCKS * 512], A_BLOCKS),
        "w_rest": rows(a["w_in"][0][:, A_BLOCKS * 512:], B_BLOCKS),
        "ret_state": pair_rows(a["state_ret"][0, 0]),
        "decay_part": np.repeat(a["ret_decay"][0].reshape(2, PAIRS, 2).transpose(2, 0, 1), HD, axis=0),
        "decay_row": np.repeat(a["ret_decay"][0][None], P, axis=0),
    }
    taps = a["rwkv_conv"][0].reshape(3, 3, PAIRS, P).transpose(2, 3, 1, 0).reshape(PAIRS, P, 9)
    ch = lambda v: v.reshape(-1, PAIRS, P).transpose(1, 2, 0)
    out["rw_cols"] = np.concatenate([taps, ch(a["rwkv_w0"][0]), ch(a["rwkv_a0"][0]), ch(a["rwkv_k_k"][0]),
                                     ch(a["rwkv_k_a"][0]), ch(a["rwkv_r_k"][0].reshape(-1))], axis=2)
    out["rw_wa"] = np.concatenate([a["rwkv_w2"][0], a["rwkv_a2"][0]], axis=1).reshape(2, P, PAIRS, P)\
        .transpose(2, 1, 0, 3)
    out["rw_state"] = pair_rows(a["state_rwkv"][0, 0].transpose(0, 1, 3, 2))
    out.update(constants())
    return {k: np.ascontiguousarray(v) for k, v in out.items()}


def rwkv(nc, d, projT, bonus_v, yT, state_out):
    n = PAIRS * NG
    xs = nc.dram_tensor("rw_xs", [n, P, 2, 4, GT], F32).ap()
    vs = nc.dram_tensor("rw_vs", [n, P, GT], F32).ap()
    ef = nc.dram_tensor("rw_ef", [n, P, 3 * GRP, CH], F32).ap()
    mn = nc.dram_tensor("rw_mn", [2, PAIRS * NCH, P, 2 * CH], F32).ap()
    with ExitStack() as ctx:
        gs = ctx.enter_context(nc.sbuf_tensor("rw_gs", [P, PAIRS, 2, NCH], F32))
        rwkv_operands(nc, d, projT, gs, xs, vs, bonus_v)
        rwkv_chunks(nc, d, xs, vs, ef, mn)
        qs = ctx.enter_context(nc.sbuf_tensor("rw_qs", [P, NCH, 2 * PAIRS, HD], F32))
        rwkv_scan(nc, d, mn, gs, qs, state_out)
        rwkv_outputs(nc, d, ef, qs, yT)


def feed_forward(nc, d, g, x1, y):
    slots = nc.dram_tensor("slots", [GROUPS, SLOTS, 3, TG], F32).ap()
    h2 = nc.dram_tensor("h2", [KD, P, T], F32).ap()
    x2 = nc.dram_tensor("x2", [KD, P, T], F32).ap()
    with ExitStack() as ctx:
        hT = ctx.enter_context(nc.sbuf_tensor("h2T", [P, KD, T], F32))
        rms_norm(nc, g, "n2", x1, hT, g["gain2"], g["mod"][:, 3 * KD:4 * KD, :])
        store_rows(nc, "h2_stored", [(h2[k], hT[:, k, :]) for k in range(KD)])
        peer_select(nc, d, hT, slots)
    peer_experts(nc, g, d, h2, x1, slots, x2)
    with ExitStack() as ctx:
        yT = ctx.enter_context(nc.sbuf_tensor("outT", [P, KD, T], F32))
        rms_norm(nc, g, "n3", x2, yT, g["nfg"], None)
        store_rows(nc, "y_stored", [(y[k], yT[:, k, :]) for k in range(KD)])


def program(nc, d, out):
    with ExitStack() as ctx:
        sb, pb, sem = opener(nc, ctx)
        g = {
            "mod": sb("mod", [P, MODS * KD, 2]), "gain1": sb("gain1", [P, KD, 2]), "gain2": sb("gain2", [P, KD, 2]),
            "n1g": sb("n1g", [P, KD]), "n2g": sb("n2g", [P, KD]), "nfg": sb("nfg", [P, KD, 2]),
        }
        projT = nc.dram_tensor("projT", [B_BLOCKS, P, T], F32).ap()
        qkv = nc.dram_tensor("qkv", [NT, P, A_BLOCKS, 512], F32).ap()
        modulation(nc, g, d)
        with ExitStack() as c2:
            hT = c2.enter_context(nc.sbuf_tensor("hT", [P, KD, T], F32))
            rms_norm(nc, g, "n1", d["xT"], hT, g["gain1"], g["mod"][:, 0:KD, :])
            projection(nc, "proj", hT, d["w_rest"], B_BLOCKS, projT)
            qkv_projection(nc, hT, d["w_qkv"], qkv)
        mixers = ExitStack()
        oT = mixers.enter_context(nc.sbuf_tensor("oT", [P, PAIRS, T], F32))
        retention(nc, g, d, qkv, oT, out["ret"])
        bonus_v = nc.dram_tensor("bonus_v", [PAIRS, P, T], F32).ap()
        yT = mixers.enter_context(nc.sbuf_tensor("yT", [P, PAIRS, T], F32))
        rwkv(nc, d, projT, bonus_v, yT, out["rwkv"])
        x1 = nc.dram_tensor("x1", [KD, P, T], F32).ap()
        group_norms(nc, d, projT, bonus_v, oT, yT)
        with ExitStack() as c2:
            merged = c2.enter_context(nc.sbuf_tensor("merged", [P, KD, T], F32))
            branches(nc, d, projT, oT, yT, merged)
            out_projection(nc, d, g, merged, x1)
        mixers.close()
        feed_forward(nc, d, g, x1, out["y"])


def kernel(**inputs):
    import concourse.bacc as bacc
    from concourse.bass_utils import run_bass_kernel_spmd

    laid = layouts({k: np.asarray(v) for k, v in inputs.items()})
    nc = bacc.Bacc("TRN2", target_bir_lowering=False, num_devices=1)
    d = {k: nc.dram_tensor("in_" + k, v.shape, mybir.dt.from_np(v.dtype), kind="ExternalInput").ap()
         for k, v in laid.items()}
    shapes = {"y": [KD, P, T], "ret": [P, 2 * PAIRS, HD], "rwkv": [P, 2 * PAIRS, HD]}
    out = {k: nc.dram_tensor("out_" + k, s, F32, kind="ExternalOutput").ap() for k, s in shapes.items()}
    program(nc, d, out)
    r = run_bass_kernel_spmd(nc, [{"in_" + k: v for k, v in laid.items()}], core_ids=[0]).results[0]
    y = r["out_y"].reshape(D, T).T
    heads = lambda s: s.reshape(2, HD, 2, PAIRS, HD).transpose(2, 3, 0, 1, 4).reshape(2, H, HD, HD)
    ret, rwkv_ = heads(r["out_ret"]), heads(r["out_rwkv"]).transpose(0, 1, 3, 2)
    full = lambda s: np.ascontiguousarray(s)[None, None]
    return (np.ascontiguousarray(y[:T_CTX])[None], np.ascontiguousarray(y[T_CTX:])[None], full(ret), full(rwkv_))
```

```python
import math
from contextlib import ExitStack

import numpy as np

import concourse.bass as bass
from concourse import mybir
from concourse.alu_op_type import AluOpType as ALU

ACT = mybir.ActivationFunctionType
AX = mybir.AxisListType
F32 = mybir.dt.float32
F32R = mybir.dt.float32r
BF16 = mybir.dt.bfloat16
U32 = mybir.dt.uint32

P = 128
D = 1024
KD = D // P
T_CTX, T_LAT = 256, 1024
T = T_CTX + T_LAT
NT = T // P
SEGS = [(0, 0, T_CTX), (1, T_CTX, T)]
COLS = [(0, 512), (512, 1024), (1024, T)]
H, HD = 8, 64
PAIRS = H // 2
MODS = 6
A_BLOCKS = 3
B_BLOCKS = 34
RG, WR, WK, WV, DWDA, DG, GA, GB = 0, 4, 8, 12, 16, 17, 18, 26
NORM_EPS, GN_EPS = 1e-6, 64e-5


def linker(eng, sem, again=False):
    count = [0]
    if again:
        eng.sem_clear(sem)

    def link(ins):
        count[0] += 1
        ins.then_inc(sem, 1)
        eng.wait_ge(sem, count[0])

    return link


def hold(eng, passed, *waits):
    for s, v in waits:
        eng.wait_ge(s, v)
    eng.sem_inc(passed, 1)


def count_from_one(nc, *semaphores):
    for s in semaphores:
        for x in s if isinstance(s, list) else [s]:
            nc.gpsimd.sem_inc(x, 1)
    nc.all_engine_barrier()


def opener(nc, ctx):
    taken = []

    def release():
        if taken:
            nc.clear_and_free_semaphores(taken)
            nc.all_engine_barrier()

    ctx.callback(release)

    def sb(name, shape, dt=F32):
        return ctx.enter_context(nc.sbuf_tensor(name, shape, dt))

    def pb(name, shape, dt=F32):
        return ctx.enter_context(nc.psum_tensor(name, shape, dt))

    def sem(name):
        taken.append(nc.alloc_semaphore(name))
        return taken[-1]

    return sb, pb, sem


def modulation(nc, g, d):
    NB = MODS * D // 512
    with ExitStack() as ctx:
        sb, pb, sem = opener(nc, ctx)
        cT = sb("cT", [P, KD, 2])
        sig = sb("mod_sig", [P, KD, 2])
        act_c = sb("act_c", [P, KD, 2])
        adaw = [sb(f"adaw{u}", [P, KD, 512]) for u in range(2)]
        adab = sb("adab", [P, MODS * KD])
        one = sb("one_plus", [P, KD, 2])
        pm = pb("mod_psum", [P, MODS * KD, 2])
        in_c, in_small = sem("m_in_c"), sem("m_in_small")
        in_w = [sem(f"m_in_w{u}") for u in range(2)]
        used_w = [sem(f"m_used_w{u}") for u in range(2)]
        sig_done, c_ready, link_s = sem("m_sig"), sem("m_c"), sem("m_link")
        count_from_one(nc, used_w)
        with nc.Block() as block:

            @block.sync
            def _(sp):
                sp.dma_start(cT[:], d["cT"]).then_inc(in_c, 16)
                with sp.Fori(0, NB // 2) as i:
                    for u in range(2):
                        sp.wait_ge(used_w[u], i + 1)
                        sp.dma_start(adaw[u][:], d["ada_w"][bass.ds(i * 2 + u, 1), :, :, :]
                                     .rearrange("o p k n -> p (o k) n")).then_inc(in_w[u], 16)

            @block.scalar
            def _(act):
                act.dma_start(adab[:], d["ada_b"]).then_inc(in_small, 16)
                act.dma_start(g["n1g"][:], d["norm1_g"]).then_inc(in_small, 16)
                act.dma_start(g["n2g"][:], d["norm2_g"]).then_inc(in_small, 16)
                act.dma_start(g["nfg"][:], d["final_g"]).then_inc(in_small, 16)
                act.wait_ge(in_c, 16)
                nc.scalar.activation(sig[:], cT[:], ACT.Sigmoid).then_inc(sig_done, 1)

            @block.tensor
            def _(pe):
                pe.wait_ge(c_ready, 1)
                with pe.Fori(0, NB // 2) as i:
                    for u in range(2):
                        pe.wait_ge(in_w[u], i * 16 + 16)
                        for c in range(4):
                            for k in range(KD):
                                mm = nc.tensor.matmul(pm[:, bass.ds(i * 8 + u * 4 + c, 1), :],
                                                      adaw[u][:, k, c * P:(c + 1) * P], act_c[:, k, :],
                                                      start=(k == 0), stop=(k == KD - 1))
                        mm.then_inc(used_w[u], 1)

            @block.vector
            def _(dve):
                link = linker(dve, link_s)
                dve.wait_ge(sig_done, 1)
                nc.vector.tensor_tensor(act_c[:], cT[:], sig[:], ALU.mult).then_inc(c_ready, 1)
                for u in range(2):
                    dve.wait_ge(used_w[u], NB // 2 + 1)
                dve.wait_ge(in_small, 64)
                link(nc.vector.tensor_tensor(g["mod"][:], pm[:], adab[:].unsqueeze(2).broadcast_to([P, MODS * KD, 2]),
                                             ALU.add))
                for part, gain, out in ((1, "n1g", "gain1"), (4, "n2g", "gain2")):
                    link(nc.vector.tensor_scalar(one[:], g["mod"][:, part * KD:(part + 1) * KD, :], 1.0, None, ALU.add))
                    link(nc.vector.tensor_tensor(g[out][:], one[:],
                                                 g[gain][:].unsqueeze(2).broadcast_to([P, KD, 2]), ALU.mult))


def rms_norm(nc, g, name, xT, out, gain, shift, x_dram=None):
    with ExitStack() as ctx:
        sb, pb, sem = opener(nc, ctx)
        sq = sb(name + "_sq", [P, 2, T])
        rs = sb(name + "_rs", [P, T])
        ones = sb(name + "_ones", [P, P])
        eps = sb(name + "_eps", [P, 1])
        ps = pb(name + "_ps", [P, 3 * 512])
        in_x, sq_done, sum_done = sem(name + "_in_x"), sem(name + "_sq"), sem(name + "_sum")
        root_done, ones_done, link_s = sem(name + "_root"), sem(name + "_ones"), sem(name + "_link")
        with nc.Block() as block:

            @block.sync
            def _(sp):
                for k in range(KD if x_dram is not None else 0):
                    sp.dma_start(xT[:, k, :], x_dram[k]).then_inc(in_x, 16)

            @block.scalar
            def _(act):
                for k in range(KD):
                    if x_dram is not None:
                        act.wait_ge(in_x, 16 * KD)
                    if k >= 2:
                        act.wait_ge(sum_done, k - 1)
                    nc.scalar.activation(sq[:, k % 2, :], xT[:, k, :], ACT.Square).then_inc(sq_done, 1)
                act.wait_ge(sum_done, KD)
                act.wait_ge(ones_done, 2)
                nc.scalar.activation(rs[:], ps[:, 0:T], ACT.Sqrt, bias=eps[:, 0:1], scale=1.0 / D)\
                    .then_inc(root_done, 1)

            @block.tensor
            def _(pe):
                pe.wait_ge(ones_done, 1)
                for k in range(KD):
                    pe.wait_ge(sq_done, k + 1)
                    for a, b in COLS:
                        mm = nc.tensor.matmul(ps[:, a:b], ones[:], sq[:, k % 2, a:b],
                                              start=(k == 0), stop=(k == KD - 1))
                    mm.then_inc(sum_done, 1)

            @block.vector
            def _(dve):
                link = linker(dve, link_s)
                nc.vector.memset(ones[:], 1.0).then_inc(ones_done, 1)
                nc.vector.memset(eps[:], NORM_EPS).then_inc(ones_done, 1)
                dve.wait_ge(root_done, 1)
                if x_dram is not None:
                    dve.wait_ge(in_x, 16 * KD)
                link(nc.vector.reciprocal(rs[:], rs[:]))
                for k in range(KD):
                    link(nc.vector.tensor_tensor(out[:, k, :], xT[:, k, :], rs[:], ALU.mult))
                    for s, a, b in SEGS:
                        link(nc.vector.tensor_scalar(
                            out[:, k, a:b], out[:, k, a:b], gain[:, k, s:s + 1],
                            None if shift is None else shift[:, k, s:s + 1],
                            ALU.mult, ALU.bypass if shift is None else ALU.add))


def projection(nc, name, hT, weights, blocks, out_dram, pairs_of=2):
    with ExitStack() as ctx:
        sb, pb, sem = opener(nc, ctx)
        w = [sb(f"{name}_w{u}", [P, KD, P]) for u in range(2)]
        o = [sb(f"{name}_o{u}", [P, T]) for u in range(2)]
        ps = [pb(f"{name}_ps{u}", [P, 3 * 512]) for u in range(2)]
        in_w = [sem(f"{name}_in_w{u}") for u in range(2)]
        mm_done = [sem(f"{name}_mm{u}") for u in range(2)]
        copied = [sem(f"{name}_cp{u}") for u in range(2)]
        stored = [sem(f"{name}_st{u}") for u in range(2)]
        n = blocks // 2
        count_from_one(nc, copied, mm_done, stored)
        with nc.Block() as block:

            @block.sync
            def _(sp):
                with sp.Fori(0, n) as i:
                    for u in range(2):
                        sp.wait_ge(mm_done[u], i + 1)
                        sp.dma_start(w[u][:], weights[bass.ds(i * 2 + u, 1), :, :, :]
                                     .rearrange("o p k n -> p (o k) n")).then_inc(in_w[u], 16)

            @block.tensor
            def _(pe):
                with pe.Fori(0, n) as i:
                    for u in range(2):
                        pe.wait_ge(in_w[u], i * 16 + 16)
                        pe.wait_ge(copied[u], i + 1)
                        for a, b in COLS:
                            for k in range(KD):
                                mm = nc.tensor.matmul(ps[u][:, a:b], w[u][:, k, :], hT[:, k, a:b],
                                                      start=(k == 0), stop=(k == KD - 1))
                        mm.then_inc(mm_done[u], 1)

            @block.scalar
            def _(act):
                with act.Fori(0, n) as i:
                    act.wait_ge(mm_done[0], i + 2)
                    act.wait_ge(stored[0], i * 16 + 1)
                    nc.scalar.activation(o[0][:], ps[0][:, 0:T], ACT.Copy).then_inc(copied[0], 1)
                    for u in range(2):
                        act.wait_ge(copied[u], i + 2)
                        act.dma_start(out_dram[bass.ds(i * 2 + u, 1), :, :].rearrange("o p t -> p (o t)"), o[u][:])\
                            .then_inc(stored[u], 16)
                for u in range(2):
                    act.wait_ge(stored[u], n * 16 + 1)

            @block.vector
            def _(dve):
                with dve.Fori(0, n) as i:
                    dve.wait_ge(mm_done[1], i + 2)
                    dve.wait_ge(stored[1], i * 16 + 1)
                    nc.vector.tensor_copy(o[1][:], ps[1][:, 0:T]).then_inc(copied[1], 1)


def qkv_projection(nc, hT, weights, out_dram):
    with ExitStack() as ctx:
        sb, pb, sem = opener(nc, ctx)
        w = [sb(f"qkv_w{u}", [P, KD, 512]) for u in range(2)]
        o = [sb(f"qkv_o{u}", [P, 512]) for u in range(2)]
        ps = [pb(f"qkv_ps{u}", [P, 512]) for u in range(2)]
        in_w = [sem(f"qkv_in_w{a}") for a in range(A_BLOCKS)]
        mm_done, copied = sem("qkv_mm"), sem("qkv_cp")
        stored = [sem(f"qkv_st{u}") for u in range(2)]
        with nc.Block() as block:

            @block.sync
            def _(sp):
                for a in range(A_BLOCKS):
                    if a >= 2:
                        sp.wait_ge(mm_done, NT * (a - 1))
                    sp.dma_start(w[a % 2][:], weights[a]).then_inc(in_w[a], 16)

            @block.gpsimd
            def _(pool):
                for n in range(A_BLOCKS * NT):
                    pool.wait_ge(copied, n + 1)
                    pool.dma_start(out_dram[n % NT, :, n // NT, :], o[n % 2][:]).then_inc(stored[n % 2], 16)
                for u in range(2):
                    pool.wait_ge(stored[u], 16 * A_BLOCKS * NT // 2)

            @block.tensor
            def _(pe):
                for n in range(A_BLOCKS * NT):
                    a, t = n // NT, n % NT
                    if t == 0:
                        pe.wait_ge(in_w[a], 16)
                    if n >= 2:
                        pe.wait_ge(copied, n - 1)
                    for k in range(KD):
                        mm = nc.tensor.matmul(ps[n % 2][:], hT[:, k, t * P:(t + 1) * P], w[a % 2][:, k, :],
                                              start=(k == 0), stop=(k == KD - 1))
                    mm.then_inc(mm_done, 1)

            @block.vector
            def _(dve):
                for n in range(A_BLOCKS * NT):
                    dve.wait_ge(mm_done, n + 1)
                    if n >= 2:
                        dve.wait_ge(stored[n % 2], 16 * (n // 2))
                    nc.vector.tensor_copy(o[n % 2][:], ps[n % 2][:]).then_inc(copied, 1)


def retention(nc, g, d, qkv, oT, state_out):
    C = P
    with ExitStack() as outer:
        sb, pb, sem = opener(nc, outer)
        kv = sb("ret_kv", [P, NT, 2 * PAIRS, HD])
        rin = sb("ret_rin", [P, NT, 2 * PAIRS, HD])
        cst = sb("ret_cst", [P, 6, P])
        col = sb("ret_col", [P, 2])
        lgp, lgr = sb("ret_lgp", [P, 2, PAIRS]), sb("ret_lgr", [P, 2, H])
        qd = sb("ret_qd", [P, 2, PAIRS, P])
        sd = sb("ret_sd", [P, 2, H])
        cd = sb("ret_cd", [P, 2, PAIRS])
        mask = sb("ret_mask", [P, H, P])
        qkT_dram = nc.dram_tensor("ret_qkT", [NT, P, 2 * PAIRS, P], F32).ap()
        n = NT // 2

        with ExitStack() as ctx:
            sb, pb, sem = opener(nc, ctx)
            tmp = sb("ret_tmp", [P, 4, 16])
            mt = sb("ret_mt", [P, 2, P])
            x = [sb(f"ret_x{u}", [P, 3, 512]) for u in range(2)]
            cos = [sb(f"ret_cos{u}", [P, 2, HD]) for u in range(2)]
            sin = [sb(f"ret_sin{u}", [P, 2, HD // 2]) for u in range(2)]
            xc = sb("ret_xc", [P, 2, 512])
            t1, t2 = sb("ret_t1", [P, 2, 256]), sb("ret_t2", [P, 2, 256])
            ks = [sb(f"ret_ks{u}", [P, 2, 512]) for u in range(2)]
            rot = [sb(f"ret_rot{u}", [P, 2, 512]) for u in range(2)]
            qkT = [sb(f"ret_qkTs{u}", [P, 2 * PAIRS, P]) for u in range(2)]
            ident = sb("ret_ident", [P, P])
            ptr = [pb(f"ret_ptr{u}", [P, 2 * PAIRS, P]) for u in range(2)]
            pkv = [pb(f"ret_pkv{u}", [P, 2 * PAIRS, P]) for u in range(2)]
            in_c, abs_s, dec_s, lg_s, tab_s = sem("r_in_c"), sem("r_abs"), sem("r_dec"), sem("r_lg"), sem("r_tab")
            mask_e, mask_u, link_s, link2_s = sem("r_mask_e"), sem("r_mask_u"), sem("r_link"), sem("r_link2")
            in_x = [sem(f"r_in_x{u}") for u in range(2)]
            rot_s = [sem(f"r_rot{u}") for u in range(2)]
            ks_s = [sem(f"r_ks{u}") for u in range(2)]
            mm_s = [sem(f"r_mm{u}") for u in range(2)]
            tcp_s = [sem(f"r_tcp{u}") for u in range(2)]
            kcp_s = [sem(f"r_kcp{u}") for u in range(2)]
            st_s = [sem(f"r_st{u}") for u in range(2)]
            count_from_one(nc, kcp_s, mask_u, mm_s, rot_s, st_s, tcp_s)
            with nc.Block() as block:

                @block.sync
                def _(sp):
                    sp.dma_start(lgp[:], d["decay_part"]).then_inc(in_c, 16)
                    sp.dma_start(lgr[:], d["decay_row"]).then_inc(in_c, 16)
                    sp.dma_start(cst[:], d["c_ret"]).then_inc(in_c, 16)
                    sp.dma_start(col[:], d["c_col"]).then_inc(in_c, 16)
                    sp.dma_start(ident[:], d["c_ident"]).then_inc(in_c, 16)
                    with sp.Fori(0, n) as i:
                        for u in range(2):
                            sp.wait_ge(mm_s[u], i + 1)
                            sp.wait_ge(rot_s[u], i + 1)
                            t = i * 2 + u
                            sp.dma_start(x[u][:], qkv[bass.ds(t, 1), :, :, :].rearrange("o p a n -> p (o a) n"))\
                                .then_inc(in_x[u], 16)
                            sp.dma_start(cos[u][:], d["c_cos"][bass.ds(t, 1), :, :, :]
                                         .rearrange("o p a n -> p (o a) n")).then_inc(in_x[u], 16)
                            sp.dma_start(sin[u][:], d["c_sin"][bass.ds(t, 1), :, :, :]
                                         .rearrange("o p a n -> p (o a) n")).then_inc(in_x[u], 16)

                @block.scalar
                def _(act):
                    link = linker(act, abs_s)
                    act.wait_ge(in_c, 80)
                    link(nc.scalar.activation(tmp[:, 0, 0:8], lgp[:].rearrange("p a b -> p (a b)"), ACT.Abs))
                    link(nc.scalar.activation(tmp[:, 1, :], lgr[:].rearrange("p a b -> p (a b)"), ACT.Abs))
                    link(nc.scalar.activation(tmp[:, 2, 0:8], tmp[:, 0, 0:8], ACT.Exp, scale=-1.0))
                    link(nc.scalar.activation(tmp[:, 3, :], tmp[:, 1, :], ACT.Exp, scale=-1.0))
                    act.wait_ge(dec_s, 2)
                    link(nc.scalar.activation(tmp[:, 2, 0:8], tmp[:, 2, 0:8], ACT.Ln))
                    nc.scalar.activation(tmp[:, 3, :], tmp[:, 3, :], ACT.Ln).then_inc(lg_s, 1)
                    act.wait_ge(dec_s, 4)
                    for r in range(2):
                        for j in range(PAIRS):
                            nc.scalar.activation(qd[:, r, j, :], cst[:, r, :], ACT.Exp, scale=lgp[:, r, j:j + 1])\
                                .then_inc(tab_s, 1)
                        nc.scalar.activation(sd[:, r, :], lgr[:, r, :], ACT.Exp, scale=col[:, r:r + 1])\
                            .then_inc(tab_s, 1)
                    nc.scalar.activation(cd[:], lgp[:], ACT.Exp, scale=float(C)).then_inc(tab_s, 1)
                    for h in range(H):
                        for r in range(2):
                            if h:
                                act.wait_ge(mask_u, h + 1)
                            nc.scalar.activation(mt[:, r, :], cst[:, 2 + r, :], ACT.Exp, scale=lgr[:, r, h:h + 1])\
                                .then_inc(mask_e, 1)
                    with act.Fori(0, n) as i:
                        for u in range(2):
                            act.wait_ge(mm_s[u], i + 2)
                            act.wait_ge(st_s[u], i * 16 + 1)
                            nc.scalar.activation(qkT[u][:], ptr[u][:], ACT.Copy).then_inc(tcp_s[u], 1)
                            act.wait_ge(tcp_s[u], i + 2)
                            act.dma_start(qkT_dram[bass.ds(i * 2 + u, 1), :, :, :]
                                          .rearrange("o p a n -> p (o a) n"), qkT[u][:]).then_inc(st_s[u], 16)
                    for u in range(2):
                        act.wait_ge(st_s[u], 16 * n + 1)

                @block.tensor
                def _(pe):
                    pe.wait_ge(in_c, 80)
                    with pe.Fori(0, n) as i:
                        for u in range(2):
                            pe.wait_ge(rot_s[u], i + 2)
                            pe.wait_ge(tcp_s[u], i + 1)
                            for a in range(2 * PAIRS):
                                nc.tensor.transpose(ptr[u][:, a, :], rot[u][:].rearrange("p a n -> p (a n)")
                                                    [:, a * P:(a + 1) * P], ident[:])
                            pe.wait_ge(ks_s[u], i + 1)
                            pe.wait_ge(kcp_s[u], i + 1)
                            for r in range(2):
                                for j in range(PAIRS):
                                    mm = nc.tensor.matmul(pkv[u][:, r * PAIRS + j, :], ks[u][:, r, j * P:(j + 1) * P],
                                                          x[u][:, 2, j * P:(j + 1) * P], start=True, stop=True)
                            mm.then_inc(mm_s[u], 1)

                @block.vector
                def _(dve):
                    link = linker(dve, link_s)
                    dve.wait_ge(abs_s, 4)
                    nc.vector.tensor_scalar(tmp[:, 2, 0:8], tmp[:, 2, 0:8], 1.0, None, ALU.add).then_inc(dec_s, 1)
                    nc.vector.tensor_scalar(tmp[:, 3, :], tmp[:, 3, :], 1.0, None, ALU.add).then_inc(dec_s, 1)
                    dve.wait_ge(lg_s, 1)
                    dve.wait_ge(abs_s, 5)
                    for lg, q, w in ((lgp, 2, 8), (lgr, 3, 16)):
                        v = lg[:].rearrange("p a b -> p (a b)")
                        nc.vector.scalar_tensor_tensor(v, v, 0.0, tmp[:, q, 0:w], ALU.min, ALU.subtract)\
                            .then_inc(dec_s, 1)
                    for h in range(H):
                        dve.wait_ge(mask_e, 2 * h + 2)
                        link(nc.vector.tensor_tensor(mt[:], mt[:], cst[:, 4:6, :], ALU.mult))
                        nc.vector.tensor_tensor(mask[:, (h % 2) * PAIRS + h // 2, :], mt[:, 0, :], mt[:, 1, :], ALU.add).then_inc(mask_u, 1)
                    dve.wait_ge(tab_s, 11)
                    with dve.Fori(0, n) as i:
                        step = linker(dve, link2_s, again=True)
                        for u in range(2):
                            xq = x[u][:, 0:2, :]
                            dve.wait_ge(in_x[u], i * 48 + 48)
                            step(nc.vector.tensor_tensor(
                                xc[:].rearrange("p a (h c) -> p a h c", h=H), xq.rearrange("p a (h c) -> p a h c", h=H),
                                cos[u][:].unsqueeze(2).broadcast_to([P, 2, H, HD]), ALU.mult))
                            for a in range(2):
                                v = xq[:, a, :].rearrange("p (h s j f) -> p h s j f", h=H, s=2, j=2)
                                sn = sin[u][:, a, :].rearrange("p (s f) -> p s f", s=2).unsqueeze(1)\
                                    .broadcast_to([P, H, 2, 16])
                                for j, t in ((0, t1), (1, t2)):
                                    step(nc.vector.tensor_tensor(
                                        t[:, a, :].rearrange("p (h s f) -> p h s f", h=H, s=2), v[:, :, :, j, :],
                                        sn, ALU.mult))
                            dve.wait_ge(mm_s[u], i + 1)
                            half = lambda w, j: w[:].rearrange("p a (b j f) -> p (a b) j f", j=2, f=16)[:, :, j, :]
                            full = lambda w: w[:].rearrange("p a (b f) -> p (a b) f", f=16)
                            step(nc.vector.tensor_tensor(half(rot[u], 0), half(xc, 0), full(t2), ALU.subtract))
                            nc.vector.tensor_tensor(half(rot[u], 1), half(xc, 1), full(t1), ALU.add)\
                                .then_inc(rot_s[u], 1)
                            dve.wait_ge(rot_s[u], i + 2)
                            step(nc.vector.tensor_tensor(
                                ks[u][:, 0, :].rearrange("p (h c) -> p h c", h=H),
                                rot[u][:, 1, :].rearrange("p (h c) -> p h c", h=H),
                                sd[:, 0, :].unsqueeze(2).broadcast_to([P, H, HD]), ALU.mult))
                            nc.vector.tensor_tensor(
                                ks[u][:, 1, :].rearrange("p (h c) -> p h c", h=H),
                                rot[u][:, 1, :].rearrange("p (h c) -> p h c", h=H),
                                sd[:, 1, :].unsqueeze(2).broadcast_to([P, H, HD]), ALU.mult).then_inc(ks_s[u], 1)
                            dve.wait_ge(mm_s[u], i + 2)
                            for e in range(2):
                                q = slice(e * HD, (e + 1) * HD)
                                cp = nc.vector.tensor_copy(
                                    kv[q, bass.ds(i * 2 + u, 1), :, :].rearrange("p o a c -> p (o a) c"),
                                    pkv[u][q, :, q])
                            cp.then_inc(kcp_s[u], 1)

        with ExitStack() as ctx:
            sb, pb, sem = opener(nc, ctx)
            qk = [sb(f"ret_qk{u}", [P, 2 * PAIRS, P]) for u in range(2)]
            v = [sb(f"ret_v{u}", [P, 512]) for u in range(2)]
            qs = [sb(f"ret_qs{u}", [P, 2, PAIRS, P]) for u in range(2)]
            rs = [sb(f"ret_rs{u}", [P, 2 * PAIRS, HD]) for u in range(2)]
            pm = [sb(f"ret_pm{u}", [P, H, P]) for u in range(2)]
            fin = sb("ret_fin", [P, 2 * PAIRS, HD])
            dead = sb("ret_dead", [P, 2 * PAIRS, HD])
            psc = [pb(f"ret_psc{u}", [P, H, P]) for u in range(2)]
            po = [pb(f"ret_po{u}", [P, PAIRS, P]) for u in range(2)]
            in_s, zero_s, rec_s, fin_s, out_s = sem("r2_in"), sem("r2_zero"), sem("r2_rec"), sem("r2_fin"), sem("r2_out")
            in_q = [sem(f"r2_in_q{u}") for u in range(2)]
            rs_s = [sem(f"r2_rs{u}") for u in range(2)]
            qs_s = [sem(f"r2_qs{u}") for u in range(2)]
            sc_s = [sem(f"r2_sc{u}") for u in range(2)]
            pm_s = [sem(f"r2_pm{u}") for u in range(2)]
            po_s = [sem(f"r2_po{u}") for u in range(2)]
            oc_s = [sem(f"r2_oc{u}") for u in range(2)]
            FW, BW = slice(0, PAIRS), slice(PAIRS, 2 * PAIRS)
            count_from_one(nc, oc_s, pm_s, po_s)
            with nc.Block() as block:

                @block.sync
                def _(sp):
                    sp.dma_start(rin[:, 2, FW, :], d["ret_state"][:, FW, :]).then_inc(in_s, 16)
                    sp.dma_start(rin[:, NT - 1, BW, :], d["ret_state"][:, BW, :]).then_inc(in_s, 16)
                    with sp.Fori(0, n) as i:
                        for u in range(2):
                            sp.wait_ge(po_s[u], i + 1)
                            t = i * 2 + u
                            sp.dma_start(qk[u][:], qkT_dram[bass.ds(t, 1), :, :, :].rearrange("o p a n -> p (o a) n"))\
                                .then_inc(in_q[u], 16)
                            sp.dma_start(v[u][:], qkv[bass.ds(t, 1), :, 2, :].rearrange("o p n -> p (o n)"))\
                                .then_inc(in_q[u], 16)
                    sp.wait_ge(fin_s, 1)
                    sp.dma_start(state_out, fin[:]).then_inc(out_s, 16)
                    sp.wait_ge(out_s, 16)

                @block.scalar
                def _(act):
                    act.wait_ge(fin_s, 1)
                    with act.Fori(0, n) as i:
                        for u in range(2):
                            act.wait_ge(po_s[u], i + 1)
                            nc.scalar.activation(rs[u][:], rin[:, bass.ds(i * 2 + u, 1), :, :]
                                                 .rearrange("p o a c -> p (o a) c"), ACT.Copy).then_inc(rs_s[u], 1)
                            act.wait_ge(po_s[u], i + 2)
                            nc.scalar.activation(oT[:, :, bass.ds((i * 2 + u) * P, P)], po[u][:], ACT.Copy)\
                                .then_inc(oc_s[u], 1)

                @block.tensor
                def _(pe):
                    with pe.Fori(0, n) as i:
                        for u in range(2):
                            pe.wait_ge(in_q[u], i * 32 + 32)
                            pe.wait_ge(pm_s[u], i + 1)
                            for h in range(H):
                                e, j = h % 2, h // 2
                                q = slice(e * HD, (e + 1) * HD)
                                mm = nc.tensor.matmul(psc[u][:, e * PAIRS + j, :], qk[u][q, PAIRS + j, :], qk[u][q, j, :],
                                                      start=True, stop=True)
                            mm.then_inc(sc_s[u], 1)
                            pe.wait_ge(rs_s[u], i + 1)
                            pe.wait_ge(qs_s[u], i + 1)
                            pe.wait_ge(pm_s[u], i + 2)
                            pe.wait_ge(oc_s[u], i + 1)
                            for h in range(H):
                                e, j = h % 2, h // 2
                                q = slice(e * HD, (e + 1) * HD)
                                nc.tensor.matmul(po[u][q, j, :], v[u][:, h * HD:(h + 1) * HD], pm[u][:, e * PAIRS + j, :],
                                                 start=True, stop=False)
                                for r in range(2):
                                    mm = nc.tensor.matmul(po[u][q, j, :], rs[u][q, r * PAIRS + j, :],
                                                          qs[u][q, r, j, :], start=False, stop=(r == 1))
                            mm.then_inc(po_s[u], 1)

                @block.vector
                def _(dve):
                    link = linker(dve, rec_s)
                    link(nc.vector.memset(rin[:, 0, FW, :], 0.0))
                    link(nc.vector.memset(rin[:, 1, BW, :], 0.0))
                    dve.wait_ge(in_s, 32)
                    for lo, hi in ((0, 1), (2, NT - 1)):
                        for s in range(hi - lo + 1):
                            for r, t, to, part in ((0, lo + s, lo + s + 1, FW), (1, hi - s, hi - s - 1, BW)):
                                if lo <= to <= hi:
                                    dst = rin[:, to, part, :]
                                else:
                                    dst = (fin if hi == 1 else dead)[:, part, :]
                                link(nc.vector.tensor_tensor(dst, rin[:, t, part, :],
                                                             cd[:, r, :].unsqueeze(2).broadcast_to([P, PAIRS, HD]),
                                                             ALU.mult))
                                link(nc.vector.tensor_tensor(dst, dst, kv[:, t, part, :], ALU.add))
                    nc.vector.memset(dead[:, 0, 0:1], 0.0).then_inc(fin_s, 1)
                    with dve.Fori(0, n) as i:
                        for u in range(2):
                            dve.wait_ge(in_q[u], i * 32 + 32)
                            dve.wait_ge(po_s[u], i + 1)
                            for r in range(2):
                                op = nc.vector.tensor_tensor(qs[u][:, r, :, :], qk[u][:, 0:PAIRS, :], qd[:, r, :, :],
                                                             ALU.mult)
                            op.then_inc(qs_s[u], 1)
                            dve.wait_ge(sc_s[u], i + 1)
                            nc.vector.tensor_tensor(pm[u][:], psc[u][:], mask[:], ALU.mult).then_inc(pm_s[u], 1)


CH = 64
NCH = T // CH
GRP = 4
NG = NCH // GRP
GT = GRP * CH
CTX_CH = T_CTX // CH
LEVELS = [1, 2, 4, 8, 16, 32]
QA, QR, QB, QK = range(4)
RW_COLS = 16
COL_W0, COL_A0, COL_KK, COL_KA, COL_RK = 9, 11, 13, 14, 15


def rwkv_operands(nc, d, projT, gs, xs, vs, bonus_v):
    with ExitStack() as ctx:
        sb, pb, sem = opener(nc, ctx)
        raw = sb("rw_raw", [P, 3, T])
        rkv = sb("rw_rkv", [P, 3, T])
        cols = sb("rw_cols", [P, RW_COLS])
        omka = sb("rw_omka", [P, 1])
        wa = sb("rw_wa", [P, 2, P])
        lora = sb("rw_lora", [P, T])
        reset = sb("rw_reset", [P, T])
        blk = sb("rw_blk", [P, P])
        eps = sb("rw_eps", [P, 1])
        kk, sq, nrm, rkk, bon = (sb("rw_" + x, [P, T]) for x in ("kk", "sq", "nrm", "rkk", "bon"))
        sw, a, cum, u2, kd = (sb("rw_" + x, [P, T]) for x in ("sw", "a", "cum", "u2", "kd"))
        eR, eA, eN = (sb("rw_" + x, [P, T]) for x in ("eR", "eA", "eN"))
        xo = sb("rw_xo", [P, 4, T])
        psA, psB = pb("rw_psA", [P, 3 * 512]), pb("rw_psB", [P, 3 * 512])
        names = ("in0", "in", "tanh", "kkr", "sqr", "n2", "norm", "rkk", "bonmm", "bonv", "zw", "za", "sw", "a", "lw",
                 "u", "e", "xo", "xst", "vc", "vst", "link", "init")
        (in0_s, in_s, tanh_s, kkr_s, sqr_s, n2_s, norm_s, rkk_s, bonmm_s, bonv_s, zw_s, za_s, sw_s, a_s, lw_s,
         u_s, e_s, xo_s, xst_s, vc_s, vst_s, link_s, init_s) = (sem("e1_" + x) for x in names)
        count_from_one(nc, a_s, sw_s, vst_s, xo_s, xst_s)
        with nc.Block() as block:

            @block.sync
            def _(sp):
                sp.dma_start(lora[:], projT[DWDA]).then_inc(in0_s, 16)
                sp.dma_start(reset[:], d["c_reset"]).then_inc(in0_s, 16)
                sp.dma_start(blk[:], d["c_blk"]).then_inc(in0_s, 16)
                with sp.Fori(0, PAIRS) as i:
                    sp.wait_ge(xo_s, 2 * i + 1)
                    for q, first in enumerate((WR, WK, WV)):
                        sp.dma_start(raw[:, q, :], projT[bass.ds(i + first, 1), :, :].rearrange("o p t -> p (o t)"))\
                            .then_inc(in_s, 16)
                    sp.dma_start(cols[:], d["rw_cols"][bass.ds(i, 1), :, :].rearrange("o p t -> p (o t)"))\
                        .then_inc(in_s, 16)
                    sp.dma_start(wa[:], d["rw_wa"][bass.ds(i, 1), :, :, :].rearrange("o p a t -> p (o a) t"))\
                        .then_inc(in_s, 16)
                    groups = bass.ds(i * NG, NG)
                    sp.wait_ge(vc_s, i + 1)
                    sp.dma_start(vs[groups, :, :].rearrange("g p t -> p g t"),
                                   rkv[:, 2, :].rearrange("p (g t) -> p g t", g=NG)).then_inc(vst_s, 16)
                    sp.wait_ge(bonv_s, i + 1)
                    sp.dma_start(bonus_v[bass.ds(i, 1), :, :].rearrange("o p t -> p (o t)"), bon[:])\
                        .then_inc(vst_s, 16)
                    for r in range(2):
                        sp.wait_ge(xo_s, 2 * i + r + 2)
                        for q in range(4):
                            sp.dma_start(xs[groups, :, r, q, :].rearrange("g p t -> p g t"),
                                           xo[:, q, :].rearrange("p (g t) -> p g t", g=NG)).then_inc(xst_s, 16)
                sp.wait_ge(vst_s, 32 * PAIRS + 1)
                sp.wait_ge(xst_s, 16 * 8 * PAIRS + 1)

            @block.scalar
            def _(act):
                act.wait_ge(in0_s, 48)
                nc.scalar.activation(lora[0:HD, :], lora[0:HD, :], ACT.Tanh).then_inc(tanh_s, 1)
                act.wait_ge(init_s, 1)
                with act.Fori(0, PAIRS) as i:
                    act.wait_ge(kkr_s, i + 1)
                    nc.scalar.activation(sq[:], kk[:], ACT.Square).then_inc(sqr_s, 1)
                    act.wait_ge(n2_s, i + 1)
                    nc.scalar.activation(nrm[:], psA[:, 0:T], ACT.Sqrt, bias=eps[:, 0:1]).then_inc(norm_s, 1)
                    for r in range(2):
                        n = 2 * i + r
                        act.wait_ge(zw_s, n + 1)
                        act.wait_ge(xo_s, n + 1)
                        nc.scalar.activation(sw[:], psA[:, 0:T], ACT.Sigmoid, bias=cols[:, COL_W0 + r:COL_W0 + r + 1])\
                            .then_inc(sw_s, 1)
                        act.wait_ge(za_s, n + 1)
                        nc.scalar.activation(a[:], psB[:, 0:T], ACT.Sigmoid, bias=cols[:, COL_A0 + r:COL_A0 + r + 1])\
                            .then_inc(a_s, 1)
                        act.wait_ge(u_s, n + 1)
                        for out, src, sign in (((eR, cum, 1.0), (eA, u2, 1.0), (eN, cum, -1.0)) if r == 0 else
                                               ((eR, u2, -1.0), (eA, cum, -1.0), (eN, u2, 1.0))):
                            nc.scalar.activation(out[:], src[:], ACT.Exp, scale=sign).then_inc(e_s, 1)
                        nc.scalar.activation(gs[:, bass.ds(i, 1), r, :].rearrange("p o c -> p (o c)"),
                                             cum[:].rearrange("p (c t) -> p c t", t=CH)[:, :, CH - 1], ACT.Exp)\
                            .then_inc(e_s, 1)

            @block.tensor
            def _(pe):
                pe.wait_ge(in0_s, 48)
                pe.wait_ge(tanh_s, 1)
                with pe.Fori(0, PAIRS) as i:
                    pe.wait_ge(sqr_s, i + 1)
                    pe.wait_ge(sw_s, 2 * i + 1)
                    for x, y in COLS:
                        mm = nc.tensor.matmul(psA[:, x:y], blk[:], sq[:, x:y], start=True, stop=True)
                    mm.then_inc(n2_s, 1)
                    pe.wait_ge(rkk_s, i + 1)
                    pe.wait_ge(a_s, 2 * i + 1)
                    for x, y in COLS:
                        mm = nc.tensor.matmul(psB[:, x:y], blk[:], rkk[:, x:y], start=True, stop=True)
                    mm.then_inc(bonmm_s, 1)
                    pe.wait_ge(in_s, 80 * i + 80)
                    for r in range(2):
                        if r == 0:
                            pe.wait_ge(norm_s, i + 1)
                        else:
                            pe.wait_ge(sw_s, 2 * i + 2)
                        for x, y in COLS:
                            mm = nc.tensor.matmul(psA[:, x:y], wa[0:HD, r, :], lora[0:HD, x:y], start=True, stop=True)
                        mm.then_inc(zw_s, 1)
                        if r == 0:
                            pe.wait_ge(bonv_s, i + 1)
                        else:
                            pe.wait_ge(a_s, 2 * i + 2)
                        for x, y in COLS:
                            mm = nc.tensor.matmul(psB[:, x:y], wa[HD:P, r, :], lora[HD:P, x:y], start=True, stop=True)
                        mm.then_inc(za_s, 1)

            @block.vector
            def _(dve):
                V = nc.vector
                V.memset(eps[:], 1e-12).then_inc(init_s, 1)
                dve.wait_ge(in0_s, 48)
                with dve.Fori(0, PAIRS) as i:
                    link = linker(dve, link_s, again=True)
                    dve.wait_ge(in_s, 80 * i + 80)
                    dve.wait_ge(vst_s, 32 * i + 1)
                    for q in range(3):
                        w = lambda j: cols[:, 3 * q + j:3 * q + j + 1]
                        x, y = raw[:, q, :], rkv[:, q, :]
                        link(V.tensor_scalar(y, x, w(1), None, ALU.mult))
                        for _, s, e in SEGS:
                            link(V.scalar_tensor_tensor(y[:, s + 1:e], x[:, s:e - 1], w(0), y[:, s + 1:e],
                                                        ALU.mult, ALU.add))
                            ins = V.scalar_tensor_tensor(y[:, s:e - 1], x[:, s + 1:e], w(2), y[:, s:e - 1],
                                                         ALU.mult, ALU.add)
                            if q == 2 and e == T:
                                ins.then_inc(vc_s, 1)
                            else:
                                link(ins)
                    r_, k_, v_ = (rkv[:, q, :] for q in range(3))
                    V.tensor_scalar(kk[:], k_, cols[:, COL_KK:COL_KK + 1], None, ALU.mult).then_inc(kkr_s, 1)
                    V.scalar_tensor_tensor(rkk[:], r_, cols[:, COL_RK:COL_RK + 1], k_, ALU.mult, ALU.mult)\
                        .then_inc(rkk_s, 1)
                    link(V.tensor_scalar(omka[:], cols[:, COL_KA:COL_KA + 1], -1.0, 1.0, ALU.mult, ALU.add))
                    dve.wait_ge(norm_s, i + 1)
                    dve.wait_ge(kkr_s, i + 1)
                    link(V.reciprocal(nrm[:], nrm[:]))
                    link(V.tensor_tensor(kk[:], kk[:], nrm[:], ALU.mult))
                    dve.wait_ge(bonmm_s, i + 1)
                    dve.wait_ge(vc_s, i + 1)
                    V.tensor_tensor(bon[:], psB[:, 0:T], v_, ALU.mult).then_inc(bonv_s, 1)
                    for r in range(2):
                        n = 2 * i + r
                        dve.wait_ge(sw_s, n + 2)
                        link(V.tensor_scalar(sw[:], sw[:], -math.exp(-0.5), None, ALU.mult))
                        link(V.tensor_tensor_scan(cum[:], reset[:], sw[:], 0.0, ALU.mult, ALU.add))
                        c3 = cum[:].rearrange("p (c t) -> p c t", t=CH)
                        link(V.tensor_scalar(kd[:, 0:NCH], c3[:, :, CH - 1], -0.5, None, ALU.mult))
                        link(V.tensor_tensor(c3, c3, kd[:, 0:NCH].unsqueeze(2).broadcast_to([P, NCH, CH]), ALU.add))
                        V.tensor_tensor(u2[:], cum[:], sw[:], ALU.subtract).then_inc(u_s, 1)
                        dve.wait_ge(a_s, n + 2)
                        link(V.tensor_scalar(kd[:], a[:], cols[:, COL_KA:COL_KA + 1], omka[:, 0:1], ALU.mult, ALU.add))
                        link(V.tensor_tensor(kd[:], kd[:], k_, ALU.mult))
                        link(V.tensor_tensor(a[:], a[:], kk[:], ALU.mult))
                        dve.wait_ge(e_s, 4 * n + 4)
                        dve.wait_ge(xst_s, 64 * n + 1)
                        V.tensor_tensor(xo[:, QA, :], kk[:], eA[:], ALU.mult)
                        V.tensor_tensor(xo[:, QR, :], r_, eR[:], ALU.mult)
                        link(V.tensor_tensor(xo[:, QB, :], a[:], eN[:], ALU.mult))
                        V.tensor_tensor(xo[:, QK, :], kd[:], eN[:], ALU.mult).then_inc(xo_s, 1)


def rwkv_chunks(nc, d, xs, vs, ef, mn):
    U = 2 * GRP
    with ExitStack() as ctx:
        sb, pb, sem = opener(nc, ctx)
        x = [sb(f"ch_x{u}", [P, 2, 4, GT]) for u in range(2)]
        vT = [sb(f"ch_vT{u}", [P, GT]) for u in range(2)]
        ident, idb = sb("ch_ident", [P, P]), sb("ch_idb", [P, HD])
        mar = sb("ch_mar", [P, 2, 2 * CH])
        mba = sb("ch_mba", [P, 2, CH])
        lev = sb("ch_lev", [P, len(LEVELS), 2, CH])
        gb = sb("ch_gb", [P, U, 3, CH])
        gk = sb("ch_gk", [P, U, 2, CH])
        lm = sb("ch_lm", [P, U, CH])
        ct = sb("ch_ct", [P, len(LEVELS) + 1, U, CH])
        ay = sb("ch_ay", [P, U, 2, CH])
        kn, vn = sb("ch_kn", [P, U, CH]), sb("ch_vn", [P, GRP, HD])
        tt, uu, yy = sb("ch_tt", [P, U, CH]), sb("ch_uu", [P, U, CH]), sb("ch_yy", [P, U, CH])
        xx, yn = sb("ch_xx", [P, U, CH]), sb("ch_yn", [P, U, CH])
        oe = sb("ch_oe", [P, U + GRP, CH])
        om = sb("ch_om", [P, U, 2, CH])
        b01, b23 = pb("ch_b01", [P, U, 2, CH]), pb("ch_b23", [P, U, 2, CH])
        b4, b5, b6, b7 = (pb(f"ch_b{n}", [P, U, CH]) for n in (4, 5, 6, 7))
        names = ("in0", "gram", "gbm", "gkm", "lm", "nat", "ncp", "vmm", "vcp", "ct", "t0", "y", "ycp", "tm", "um",
                 "tu", "y0", "y0c", "xy", "xyc", "me", "nf", "ec", "mc", "nc", "est", "mst", "link")
        (in0_s, gram_s, gbm_s, gkm_s, lm_s, nat_s, ncp_s, vmm_s, vcp_s, ct_s, t0_s, y_s, ycp_s, tm_s, um_s,
         tu_s, y0_s, y0c_s, xy_s, xyc_s, me_s, nf_s, ec_s, mc_s, nc_s, est_s, mst_s, link_s) = (
            sem("e2_" + n) for n in names)
        in_s = [sem(f"e2_inx{u}") for u in range(2)]
        fc_s = [sem(f"e2_fc{u}") for u in range(2)]
        passed_s = sem("e2_passed")
        NL = len(LEVELS) - 1
        half = [slice(0, HD), slice(HD, P)]
        units = [(e, r, c) for r in range(2) for c in range(GRP) for e in range(2)]
        count_from_one(nc, ct_s, est_s, fc_s, mc_s, mst_s, nc_s, nf_s, tu_s, um_s, xyc_s)
        with nc.Block() as block:

            @block.sync
            def _(sp):
                for t, s in ((ident, "c_ident"), (idb, "c_idb"), (mar, "c_mar"), (mba, "c_mba"), (lev, "c_lev")):
                    sp.dma_start(t[:], d[s]).then_inc(in0_s, 16)
                with sp.Fori(0, PAIRS * NG // 2) as i:
                    for u in range(2):
                        sp.wait_ge(fc_s[u], i + 1)
                        sp.dma_start(x[u][:], xs[bass.ds(2 * i + u, 1), :, :, :, :].rearrange("o p r q t -> p (o r) q t"))\
                            .then_inc(in_s[u], 16)
                        sp.dma_start(vT[u][:], vs[bass.ds(2 * i + u, 1), :, :].rearrange("o p t -> p (o t)"))\
                            .then_inc(in_s[u], 16)

            def parts(u):
                X = lambda e, r, q, c: x[u][half[e], r, q, c * CH:(c + 1) * CH]
                return X

            @block.tensor
            def _(pe):
                MM = nc.tensor.matmul
                pe.wait_ge(in0_s, 80)
                with pe.Fori(0, PAIRS * NG // 2) as i:
                    for u in range(2):
                        n = 2 * i + u
                        X = parts(u)
                        hold(pe, passed_s, (in_s[u], 32 * i + 32), (xyc_s, 2 * n + 1))
                        for e, r, c in units:
                            MM(b01[half[e], r * GRP + c, :, :], X(e, r, QB, c),
                               x[u][half[e], r, QA:QR + 1, c * CH:(c + 1) * CH], start=True, stop=True)
                        hold(pe, passed_s, (mc_s, n + 1))
                        for e, r, c in units:
                            MM(b23[half[e], r * GRP + c, :, :], X(e, r, QK, c),
                               x[u][half[e], r, QA:QR + 1, c * CH:(c + 1) * CH], start=True, stop=True)
                        for e, r, c in units:
                            mm = MM(b4[half[e], r * GRP + c, :], X(e, r, QA, c), X(e, r, QB, c), start=True, stop=True)
                        mm.then_inc(gram_s, 1)
                        hold(pe, passed_s, (nc_s, n + 1), (fc_s[1 - u], i + u + 1))
                        for q, b in ((QA, b5), (QB, b6), (QK, b7)):
                            for e, r, c in units:
                                mm = MM(b[half[e], r * GRP + c, :], X(e, r, q, c), ident[half[e], half[e]],
                                        start=True, stop=True)
                        mm.then_inc(nat_s, 1)
                        hold(pe, passed_s, (lm_s, n + 1))
                        for c in range(GRP):
                            for e in range(2):
                                mm = MM(b4[half[e], c, :], vT[u][half[e], c * CH:(c + 1) * CH],
                                        ident[half[e], half[e]], start=True, stop=True)
                        mm.then_inc(vmm_s, 1)
                        hold(pe, passed_s, (ncp_s, 3 * n + 3))
                        for l in range(NL):
                            hold(pe, passed_s, (ct_s, n * (NL + 2) + l + 3 + 1),
                                 (t0_s, 2 * n + 2) if l == 0 else (tu_s, n * (2 * NL - 1) + 2 * l + 1))
                            for e, r, c in units:
                                j = r * GRP + c
                                mm = MM(b5[half[e], j, :], ct[half[e], l + 1, j, :], tt[half[e], j, :],
                                        start=True, stop=True)
                            mm.then_inc(y_s, 1)
                            hold(pe, passed_s, (ycp_s, n * NL + l + 1))
                            if l < NL - 1:
                                for e, r, c in units:
                                    j = r * GRP + c
                                    mm = MM(b6[half[e], j, :], uu[half[e], j, :], yy[half[e], j, :],
                                            start=True, stop=True)
                                mm.then_inc(tm_s, 1)
                            for e, r, c in units:
                                j = r * GRP + c
                                mm = MM(b7[half[e], j, :], yy[half[e], j, :], uu[half[e], j, :],
                                        start=True, stop=True)
                            mm.then_inc(um_s, 1)
                        hold(pe, passed_s, (gkm_s, n + 1), (vcp_s, n + 1))
                        for e, r, c in units:
                            j = r * GRP + c
                            mm = MM(b4[half[e], j, :], gk[half[e], j, 0, :], vn[half[e], c, :], start=True, stop=True)
                        mm.then_inc(y0_s, 1)
                        hold(pe, passed_s, (y0c_s, n + 1), (tu_s, (n + 1) * (2 * NL - 1) + 1))
                        for e, r, c in units:
                            j = r * GRP + c
                            mm = MM(b01[half[e], j, :, :], uu[half[e], j, :], ay[half[e], j, :, :],
                                    start=True, stop=True)
                        mm.then_inc(xy_s, 1)
                        hold(pe, passed_s, (xyc_s, 2 * n + 2 + 1))
                        for e, r, c in units:
                            j = r * GRP + c
                            mm = MM(b23[half[e], j, :, :], xx[half[e], j, :], gb[half[e], j, 1:3, :],
                                    start=True, stop=True)
                        mm.then_inc(me_s, 1)
                        for e, r, c in units:
                            j = r * GRP + c
                            MM(b5[half[e], j, :], kn[half[e], j, :], vn[half[e], c, :], start=True, stop=False)
                            MM(b5[half[e], j, :], gb[half[e], j, 2, :], yn[half[e], j, :], start=False, stop=True)
                        for c in range(GRP):
                            for e in range(2):
                                for r in range(2):
                                    j = r * GRP + c
                                    MM(b6[half[e], c, :], vn[half[e], c, :], gk[half[e], j, 1, :],
                                       start=(r == 0), stop=False)
                                    mm = MM(b6[half[e], c, :], yn[half[e], j, :], gb[half[e], j, 1, :],
                                            start=False, stop=(r == 1))
                        mm.then_inc(nf_s, 1)

            @block.scalar
            def _(act):
                A = nc.scalar.activation
                with act.Fori(0, PAIRS * NG // 2) as i:
                    for u in range(2):
                        n = 2 * i + u
                        act.wait_ge(nat_s, n + 1)
                        act.wait_ge(nf_s, n + 1)
                        A(ay[:, :, 0, :], b5[:], ACT.Copy).then_inc(ncp_s, 1)
                        A(gb[:, :, 2, :], b6[:], ACT.Copy).then_inc(ncp_s, 1)
                        A(kn[:], b7[:], ACT.Copy).then_inc(ncp_s, 1)
                        act.wait_ge(vmm_s, n + 1)
                        A(vn[:], b4[:, 0:GRP, :], ACT.Copy).then_inc(vcp_s, 1)
                        for l in range(NL):
                            act.wait_ge(y_s, n * NL + l + 1)
                            if l:
                                act.wait_ge(um_s, n * NL + l + 1)
                            A(yy[:], b5[:], ACT.Copy).then_inc(ycp_s, 1)
                        act.wait_ge(y0_s, n + 1)
                        A(ay[:, :, 1, :], b4[:], ACT.Copy).then_inc(y0c_s, 1)
                        act.wait_ge(xy_s, n + 1)
                        A(xx[:], b01[:, :, 0, :], ACT.Copy).then_inc(xyc_s, 1)
                        A(yn[:], b01[:, :, 1, :], ACT.Copy, scale=-1.0).then_inc(xyc_s, 1)
                        act.wait_ge(nf_s, n + 2)
                        act.wait_ge(mst_s, 32 * n + 1)
                        A(om[:, :, 1, :], b5[:], ACT.Copy).then_inc(nc_s, 1)
                        act.wait_ge(nc_s, n + 2)
                        act.wait_ge(mc_s, n + 2)
                        for r in range(2):
                            act.dma_start(mn[r, bass.ds(n * GRP, GRP), :, :].rearrange("c p k -> p c k"),
                                          om[:, r * GRP:(r + 1) * GRP, :, :].rearrange("p c m k -> p c (m k)"))\
                                .then_inc(mst_s, 16)
                        act.wait_ge(fc_s[u], i + 2)
                        act.dma_start(ef[bass.ds(n, 1), :, :, :].rearrange("o p a t -> p (o a) t"), oe[:])\
                            .then_inc(est_s, 16)
                act.wait_ge(mst_s, 32 * PAIRS * NG + 1)
                act.wait_ge(est_s, 16 * PAIRS * NG + 1)

            @block.gpsimd
            def _(pool):
                with pool.Fori(0, PAIRS * NG // 2) as i:
                    for u in range(2):
                        n = 2 * i + u
                        def bc(k, flip):
                            order = (1, 0) if flip else (0, 1)
                            return [lev[:, k, r, :].unsqueeze(1).broadcast_to([P, GRP, CH]) for r in order]
                        pool.wait_ge(lm_s, n + 1)
                        pool.wait_ge(gbm_s, n + 1)
                        pool.wait_ge(um_s, n * NL + 1)
                        for k, src in [(len(LEVELS), lm)] + [(k, gb) for k in range(len(LEVELS))]:
                            m = bc(0, True) if src is lm else bc(k, False)
                            for r in range(2):
                                j = slice(r * GRP, (r + 1) * GRP)
                                op = nc.gpsimd.tensor_tensor(ct[:, k, j, :], lm[:, j, :] if src is lm else gb[:, j, 0, :],
                                                             m[r], ALU.mult)
                            op.then_inc(ct_s, 1)

            @block.vector
            def _(dve):
                V = nc.vector
                dve.wait_ge(in0_s, 80)
                rc = "p (r c) q t -> p r c (q t)"
                with dve.Fori(0, PAIRS * NG // 2) as i:
                    for u in range(2):
                        n = 2 * i + u
                        dve.wait_ge(gram_s, n + 1)
                        dve.wait_ge(nf_s, n + 1)
                        dve.wait_ge(ct_s, n * (NL + 2) + 1)
                        for r in range(2):
                            j = slice(r * GRP, (r + 1) * GRP)
                            m = mar[:, r, :].unsqueeze(1).broadcast_to([P, GRP, 2 * CH])
                            op = V.tensor_tensor(gb[:, j, 0:2, :].rearrange("p c q t -> p c (q t)"),
                                                 b01[:, j, :, :].rearrange("p c q t -> p c (q t)"), m, ALU.mult)
                        op.then_inc(gbm_s, 1)
                        for r in range(2):
                            j = slice(r * GRP, (r + 1) * GRP)
                            op = V.tensor_tensor(lm[:, j, :], b4[:, j, :],
                                                 mba[:, r, :].unsqueeze(1).broadcast_to([P, GRP, CH]), ALU.mult)
                        op.then_inc(lm_s, 1)
                        for r in range(2):
                            j = slice(r * GRP, (r + 1) * GRP)
                            m = mar[:, r, :].unsqueeze(1).broadcast_to([P, GRP, 2 * CH])
                            op = V.tensor_tensor(gk[:, j, :, :].rearrange("p c q t -> p c (q t)"),
                                                 b23[:, j, :, :].rearrange("p c q t -> p c (q t)"), m, ALU.mult)
                        op.then_inc(gkm_s, 1)
                        eye = idb[:].unsqueeze(1).broadcast_to([P, U, CH])
                        dve.wait_ge(ct_s, n * (NL + 2) + 2 + 1)
                        V.tensor_tensor(tt[:], eye, ct[:, len(LEVELS), :, :], ALU.subtract).then_inc(t0_s, 1)
                        V.tensor_tensor(uu[:], eye, ct[:, 0, :, :], ALU.subtract).then_inc(t0_s, 1)
                        for l in range(NL):
                            if l == 0:
                                dve.wait_ge(t0_s, 2 * n + 2)
                            if l < NL - 1:
                                dve.wait_ge(tm_s, n * (NL - 1) + l + 1)
                                V.tensor_tensor(tt[:], tt[:], b6[:], ALU.subtract).then_inc(tu_s, 1)
                            dve.wait_ge(um_s, n * NL + l + 2)
                            V.tensor_tensor(uu[:], uu[:], b7[:], ALU.subtract).then_inc(tu_s, 1)
                            dve.wait_ge(tu_s, n * (2 * NL - 1) + min(2 * l + 2, 2 * NL - 1) + 1)
                        dve.wait_ge(me_s, n + 1)
                        dve.wait_ge(est_s, 16 * n + 1)
                        dve.wait_ge(mst_s, 32 * n + 1)
                        V.tensor_tensor(oe[:, 0:U, :].rearrange("p (r c) t -> p r c t", r=2),
                                        x[u][:, :, QR, :].rearrange("p r (c t) -> p r c t", c=GRP),
                                        b23[:, :, 0, :].rearrange("p (r c) t -> p r c t", r=2), ALU.subtract)\
                            .then_inc(ec_s, 1)
                        V.tensor_tensor(om[:, :, 0, :], eye, b23[:, :, 1, :], ALU.subtract).then_inc(mc_s, 1)
                        dve.wait_ge(nf_s, n + 2)
                        V.tensor_copy(oe[:, U:U + GRP, :], b6[:, 0:GRP, :]).then_inc(fc_s[u], 1)


def rwkv_scan(nc, d, mn, gs, qs, state_out):
    U = 2 * PAIRS
    LAT = NCH - CTX_CH
    with ExitStack() as ctx:
        sb, pb, sem = opener(nc, ctx)
        mb = [sb(f"sc_mn{u}", [P, U, 2 * CH]) for u in range(2)]
        q = sb("sc_q", [P, U, HD])
        t = sb("sc_t", [P, U, HD])
        fin = sb("sc_fin", [P, U, HD])
        init = sb("sc_init", [P, U, HD])
        g2 = sb("sc_g2", [P, PAIRS, 2, NCH])
        ps = pb("sc_ps", [P, U, HD])
        init_s, mm_s, q_s, cp_s, t_s, fin_s, out_s, link_s, g_s = (
            sem("e3_" + x) for x in ("init", "mm", "q", "cp", "t", "fin", "out", "link", "g"))
        in_s = [sem(f"e3_in{u}") for u in range(2)]
        half = [slice(0, HD), slice(HD, P)]
        FW, BW = slice(0, PAIRS), slice(PAIRS, U)
        passed_s = sem("e3_passed")
        ctx_steps = [(s, CTX_CH - 1 - s) for s in range(CTX_CH)]
        mnv = [mn[r].rearrange("(j c) p k -> p c j k", c=NCH) for r in range(2)]
        count_from_one(nc, in_s, t_s)
        with nc.Block() as block:

            @block.sync
            def _(sp):
                sp.dma_start(init[:], d["rw_state"]).then_inc(init_s, 16)

                def load(u, chunks, k):
                    sp.wait_ge(t_s, k + 1)
                    for r, c in enumerate(chunks):
                        sp.dma_start(mb[u][:, r * PAIRS:(r + 1) * PAIRS, :],
                                     mnv[r][:, bass.ds(c, 1), :, :].rearrange("p o j k -> p (o j) k"))\
                            .then_inc(in_s[u], 16)

                for k, chunks in enumerate(ctx_steps):
                    if k < 2:
                        for r, c in enumerate(chunks):
                            sp.dma_start(mb[k][:, r * PAIRS:(r + 1) * PAIRS, :], mnv[r][:, c, :, :])\
                                .then_inc(in_s[k], 16)
                    else:
                        load(k % 2, chunks, k - 1)
                with sp.Fori(0, LAT // 2) as i:
                    for u in range(2):
                        s = 2 * i + u
                        load(u, (s + CTX_CH, s * -1 + (NCH - 1)), s + CTX_CH - 1)
                sp.wait_ge(fin_s, 1)
                sp.dma_start(state_out, fin[:]).then_inc(out_s, 16)
                sp.wait_ge(out_s, 16)

            @block.tensor
            def _(pe):
                def step(u, arrivals, k):
                    hold(pe, passed_s, (in_s[u], arrivals + 1), (q_s, k + 1))
                    for j in range(U):
                        for e in range(2):
                            mm = nc.tensor.matmul(ps[half[e], j, :], mb[u][half[e], j, 0:CH], q[half[e], j, :],
                                                  start=True, stop=True)
                    mm.then_inc(mm_s, 1)

                for k in range(CTX_CH):
                    step(k % 2, 32 * (k // 2 + 1), k)
                with pe.Fori(0, LAT // 2) as i:
                    for u in range(2):
                        step(u, 32 * i + 32 * (CTX_CH // 2 + 1), 2 * i + (u + CTX_CH))

            @block.scalar
            def _(act):
                def keep(chunks, k):
                    act.wait_ge(q_s, k + 1)
                    for c, w in zip(chunks, (FW, BW)):
                        nc.scalar.activation(qs[:, bass.ds(c, 1), w, :].rearrange("p o j v -> p (o j) v"),
                                             q[:, w, :], ACT.Copy).then_inc(cp_s, 1)

                for k, chunks in enumerate(ctx_steps):
                    keep(chunks, k)
                with act.Fori(0, LAT) as i:
                    keep((i + CTX_CH, i * -1 + (NCH - 1)), i + CTX_CH)

            @block.vector
            def _(dve):
                V = nc.vector
                link = linker(dve, link_s)
                gv = lambda r, c, a=gs: a[:, :, r, bass.ds(c, 1)].broadcast_to([P, PAIRS, HD])
                V.tensor_tensor(g2[:, :, 0, 0:NCH - 1], gs[:, :, 0, 0:NCH - 1], gs[:, :, 0, 1:NCH], ALU.mult)\
                    .then_inc(g_s, 1)
                V.tensor_tensor(g2[:, :, 1, 1:NCH], gs[:, :, 1, 1:NCH], gs[:, :, 1, 0:NCH - 1], ALU.mult)\
                    .then_inc(g_s, 1)
                V.memset(g2[:, :, 0, NCH - 1:NCH], 0.0).then_inc(g_s, 1)
                V.memset(g2[:, :, 1, 0:1], 0.0).then_inc(g_s, 1)
                V.memset(q[:], 0.0).then_inc(q_s, 1)
                dve.wait_ge(g_s, 4)
                dve.wait_ge(init_s, 16)

                def summed(k, u):
                    dve.wait_ge(mm_s, k + 1)
                    V.tensor_tensor(t[:], ps[:], mb[u][:, :, CH:2 * CH], ALU.add).then_inc(t_s, 1)
                    dve.wait_ge(t_s, k + 2)
                    dve.wait_ge(cp_s, 2 * k + 2)

                def hand_over(chunks):
                    V.tensor_tensor(q[:, FW, :], t[:, FW, :], gv(0, chunks[0], g2), ALU.mult)
                    V.tensor_tensor(q[:, BW, :], t[:, BW, :], gv(1, chunks[1], g2), ALU.mult).then_inc(q_s, 1)

                for k, chunks in enumerate(ctx_steps):
                    summed(k, k % 2)
                    if k < CTX_CH - 1:
                        hand_over(chunks)
                link(V.tensor_tensor(fin[:, FW, :], t[:, FW, :], gv(0, CTX_CH - 1), ALU.mult))
                V.tensor_tensor(fin[:, BW, :], t[:, BW, :], gv(1, 0), ALU.mult).then_inc(fin_s, 1)
                V.tensor_tensor(q[:, FW, :], init[:, FW, :], gv(0, CTX_CH), ALU.mult)
                V.tensor_tensor(q[:, BW, :], init[:, BW, :], gv(1, NCH - 1), ALU.mult).then_inc(q_s, 1)
                with dve.Fori(0, LAT // 2) as i:
                    for u in range(2):
                        s = 2 * i + u
                        summed(s + CTX_CH, u)
                        hand_over((s + CTX_CH, s * -1 + (NCH - 1)))


def rwkv_outputs(nc, d, ef, qs, yT):
    U = 2 * GRP
    with ExitStack() as ctx:
        sb, pb, sem = opener(nc, ctx)
        e_ = [sb(f"y_ef{u}", [P, U + GRP, CH]) for u in range(2)]
        qv = [sb(f"y_q{u}", [P, 2, GRP, HD]) for u in range(2)]
        ps = [pb(f"y_ps{u}", [P, GRP, CH]) for u in range(2)]
        in_s, qc_s, mm_s, y_s = ([sem(f"e4_{x}{u}") for u in range(2)] for x in ("in", "qc", "mm", "y"))
        half = [slice(0, HD), slice(HD, P)]
        n2 = PAIRS // 2
        passed_s = sem("e4_passed")
        count_from_one(nc, mm_s, y_s)
        with nc.Block() as block:

            @block.sync
            def _(sp):
                with sp.Fori(0, PAIRS * NG // 2) as i:
                    for u in range(2):
                        sp.wait_ge(y_s[u], i + 1)
                        sp.dma_start(e_[u][:], ef[bass.ds(2 * i + u, 1), :, :, :].rearrange("o p a t -> p (o a) t"))\
                            .then_inc(in_s[u], 16)

            @block.scalar
            def _(act):
                for j in range(PAIRS):
                    for q in range(NG):
                        n = j * NG + q
                        u = n % 2
                        if n >= 2:
                            act.wait_ge(mm_s[u], n // 2 + 1)
                        for r in range(2):
                            op = nc.scalar.activation(qv[u][:, r, :, :], qs[:, q * GRP:(q + 1) * GRP, r * PAIRS + j, :],
                                                      ACT.Copy)
                        op.then_inc(qc_s[u], 1)

            @block.tensor
            def _(pe):
                with pe.Fori(0, PAIRS * NG // 2) as i:
                    for u in range(2):
                        hold(pe, passed_s, (in_s[u], 16 * i + 16), (qc_s[u], i + 1), (y_s[u], i + 1))
                        for c in range(GRP):
                            for e in range(2):
                                for r in range(2):
                                    mm = nc.tensor.matmul(ps[u][half[e], c, :], qv[u][half[e], r, c, :],
                                                          e_[u][half[e], r * GRP + c, :], start=(r == 0), stop=(r == 1))
                        mm.then_inc(mm_s[u], 1)

            @block.vector
            def _(dve):
                yv = yT[:].rearrange("p j (g t) -> p (j g) t", g=NG)
                with dve.Fori(0, PAIRS * NG // 2) as i:
                    for u in range(2):
                        dve.wait_ge(mm_s[u], i + 2)
                        nc.vector.tensor_tensor(yv[:, bass.ds(2 * i + u, 1), :].rearrange("p o t -> p (o t)"),
                                                ps[u][:].rearrange("p c t -> p (c t)"),
                                                e_[u][:, U:U + GRP, :].rearrange("p c t -> p (c t)"), ALU.add)\
                            .then_inc(y_s[u], 1)


def group_norms(nc, d, projT, bonus_v, oT, yT):
    with ExitStack() as ctx:
        sb, pb, sem = opener(nc, ctx)
        blk = sb("gn_blk", [P, P])
        eps = sb("gn_eps", [P, 1])
        wb = sb("gn_wb", [P, 2, 2, PAIRS])
        g2 = [sb(f"gn_g2{u}", [P, P]) for u in range(2)]
        dg = sb("gn_dg", [P, T])
        dev = [sb(f"gn_dev{u}", [P, T]) for u in range(2)]
        sq = [sb(f"gn_sq{u}", [P, T]) for u in range(2)]
        gate, sg, bv = sb("gn_gate", [P, T]), sb("gn_sg", [P, T]), sb("gn_bv", [P, T])
        psA, psB = pb("gn_psA", [P, 3 * 512]), pb("gn_psB", [P, 3 * 512])
        names = ("in0", "eps", "dg", "sum", "dev", "sq", "var", "root", "gmm", "sg", "rg", "out", "link")
        (in0_s, eps_s, dg_s, sum_s, dev_s, sq_s, var_s, root_s, gmm_s, sg_s, rg_s, out_s, link_s) = (
            sem("f1_" + x) for x in names)
        in_s = sem("f1_in")
        z = [oT, yT]
        flat = lambda a: a.rearrange("p o t -> p (o t)")
        count_from_one(nc, out_s, root_s)
        with nc.Block() as block:

            @block.sync
            def _(sp):
                sp.dma_start(blk[:], d["c_blk"]).then_inc(in0_s, 16)
                sp.dma_start(wb[:], d["gn_wb"]).then_inc(in0_s, 16)
                sp.dma_start(dg[:], projT[DG]).then_inc(in0_s, 16)
                with sp.Fori(0, PAIRS) as i:
                    sp.wait_ge(out_s, 2 * i + 1)
                    for dst, src in ((gate, projT), (bv, bonus_v)):
                        sp.dma_start(dst[:], src[bass.ds(i, 1), :, :].rearrange("o p t -> p (o t)"))\
                            .then_inc(in_s, 16)
                    sp.dma_start(g2[0][:], d["rw_g2"][bass.ds(i, 1), :, :].rearrange("o p t -> p (o t)"))\
                        .then_inc(in_s, 16)

            @block.scalar
            def _(act):
                act.wait_ge(in0_s, 48)
                act.wait_ge(eps_s, 1)
                nc.scalar.activation(dg[:], dg[:], ACT.Sigmoid).then_inc(dg_s, 1)
                with act.Fori(0, PAIRS) as i:
                    act.wait_ge(in_s, 48 * i + 48)
                    act.wait_ge(out_s, 2 * i + 1)
                    nc.scalar.activation(sg[:], gate[:], ACT.Sigmoid).then_inc(sg_s, 1)
                    for u in range(2):
                        act.wait_ge(dev_s, 2 * i + u + 1)
                        nc.scalar.activation(sq[u][:], dev[u][:], ACT.Square).then_inc(sq_s, 1)
                        act.wait_ge(var_s, 2 * i + u + 1)
                        nc.scalar.activation(sq[u][:], psA[:, 0:T], ACT.Sqrt, bias=eps[:, 0:1], scale=1.0 / HD)\
                            .then_inc(root_s, 1)

            @block.tensor
            def _(pe):
                pe.wait_ge(in0_s, 48)
                pe.wait_ge(dg_s, 1)
                with pe.Fori(0, PAIRS) as i:
                    for u in range(2):
                        zf = flat(z[u][:, bass.ds(i, 1), :])
                        pe.wait_ge(root_s, 2 * i + u + 1)
                        for x, y in COLS:
                            mm = nc.tensor.matmul(psA[:, x:y], blk[:], z[u][:, bass.ds(i, 1), x:y]
                                                  .rearrange("p o t -> p (o t)"), start=True, stop=True)
                        mm.then_inc(sum_s, 1)
                        pe.wait_ge(sq_s, 2 * i + u + 1)
                        for x, y in COLS:
                            mm = nc.tensor.matmul(psA[:, x:y], blk[:], sq[u][:, x:y], start=True, stop=True)
                        mm.then_inc(var_s, 1)
                    pe.wait_ge(in_s, 48 * i + 48)
                    pe.wait_ge(out_s, 2 * i + 1)
                    for x, y in COLS:
                        mm = nc.tensor.matmul(psB[:, x:y], g2[0][:], dg[:, x:y], start=True, stop=True)
                    mm.then_inc(gmm_s, 1)

            @block.vector
            def _(dve):
                V = nc.vector
                V.memset(eps[:], GN_EPS).then_inc(eps_s, 1)
                dve.wait_ge(in0_s, 48)
                with dve.Fori(0, PAIRS) as i:
                    link = linker(dve, link_s, again=True)
                    for u in range(2):
                        zf = flat(z[u][:, bass.ds(i, 1), :])
                        w, b = (wb[:, q, u, bass.ds(i, 1)] for q in range(2))
                        dve.wait_ge(sum_s, 2 * i + u + 1)
                        V.scalar_tensor_tensor(dev[u][:], psA[:, 0:T], -1.0 / HD, zf, ALU.mult, ALU.add)\
                            .then_inc(dev_s, 1)
                        if u == 0:
                            dve.wait_ge(sg_s, i + 1)
                            link(V.tensor_tensor(gate[:], gate[:], sg[:], ALU.mult))
                        dve.wait_ge(root_s, 2 * i + u + 2)
                        link(V.reciprocal(sq[u][:], sq[u][:]))
                        link(V.tensor_tensor(dev[u][:], dev[u][:], sq[u][:], ALU.mult))
                        link(V.tensor_scalar(dev[u][:], dev[u][:], w, b, ALU.mult, ALU.add))
                        if u == 0:
                            V.tensor_tensor(zf, dev[u][:], gate[:], ALU.mult).then_inc(out_s, 1)
                        else:
                            link(V.tensor_tensor(dev[u][:], dev[u][:], bv[:], ALU.add))
                            dve.wait_ge(gmm_s, i + 1)
                            link(V.tensor_copy(sq[0][:, 0:1], psB[:, 0:1]))
                            V.tensor_tensor(zf, psB[:, 0:T], dev[u][:], ALU.mult).then_inc(out_s, 1)


def branches(nc, d, projT, oT, yT, merged):
    with ExitStack() as ctx:
        sb, pb, sem = opener(nc, ctx)
        w = [sb(f"br_w{u}", [P, 2, PAIRS, P]) for u in range(2)]
        ga = [sb(f"br_ga{u}", [P, 2, T]) for u in range(2)]
        t1 = sb("br_t1", [P, T])
        t2 = sb("br_t2", [P, T])
        ps = [pb(f"br_ps{q}", [P, 3 * 512]) for q in range(2)]
        in_s = [sem(f"f2_in{u}") for u in range(2)]
        ing_s = [sem(f"f2_ing{u}") for u in range(2)]
        mm_s = [sem(f"f2_mm{q}") for q in range(2)]
        sg_s, cp_s, out_s = sem("f2_sg"), sem("f2_cp"), sem("f2_out")
        z = [oT, yT]
        count_from_one(nc, cp_s, out_s)
        with nc.Block() as block:

            @block.sync
            def _(sp):
                with sp.Fori(0, KD // 2) as i:
                    for u in range(2):
                        sp.wait_ge(out_s, 2 * i + 1) if u == 0 else sp.wait_ge(out_s, 2 * i + 1)
                        m = 2 * i + u
                        sp.dma_start(w[u][:], d["w_br"][bass.ds(m, 1), :, :, :, :].rearrange("o p q k n -> p (o q) k n"))\
                            .then_inc(in_s[u], 16)
                        for q, first in enumerate((GA, GB)):
                            sp.dma_start(ga[u][:, q, :], projT[bass.ds(m + first, 1), :, :]
                                         .rearrange("o p t -> p (o t)")).then_inc(ing_s[u], 16)

            @block.scalar
            def _(act):
                with act.Fori(0, KD // 2) as i:
                    for u in range(2):
                        act.wait_ge(ing_s[u], 32 * i + 32)
                        nc.scalar.activation(ga[u][:], ga[u][:], ACT.Sigmoid).then_inc(sg_s, 1)

            @block.tensor
            def _(pe):
                with pe.Fori(0, KD // 2) as i:
                    for u in range(2):
                        m = 2 * i + u
                        pe.wait_ge(in_s[u], 16 * i + 16)
                        for q in range(2):
                            pe.wait_ge(cp_s, 2 * m + q + 1) if q == 0 else pe.wait_ge(cp_s, 2 * m + 1)
                            for x, y in COLS:
                                for k in range(PAIRS):
                                    mm = nc.tensor.matmul(ps[q][:, x:y], w[u][:, q, k, :], z[q][:, k, x:y],
                                                          start=(k == 0), stop=(k == PAIRS - 1))
                            mm.then_inc(mm_s[q], 1)

            @block.vector
            def _(dve):
                V = nc.vector
                with dve.Fori(0, KD // 2) as i:
                    for u in range(2):
                        m = 2 * i + u
                        dve.wait_ge(sg_s, m + 1)
                        for q, t in enumerate((t1, t2)):
                            dve.wait_ge(mm_s[q], m + 1)
                            if q == 0:
                                dve.wait_ge(out_s, m + 1)
                            V.tensor_tensor(t[:], ps[q][:, 0:T], ga[u][:, q, :], ALU.mult).then_inc(cp_s, 1)
                        dve.wait_ge(cp_s, 2 * m + 2 + 1)
                        V.tensor_tensor(merged[:, bass.ds(m, 1), :].rearrange("p o t -> p (o t)"), t1[:], t2[:],
                                        ALU.add).then_inc(out_s, 1)


def out_projection(nc, d, g, merged, x1):
    with ExitStack() as ctx:
        sb, pb, sem = opener(nc, ctx)
        w = [sb(f"op_w{u}", [P, KD, P]) for u in range(2)]
        x = [sb(f"op_x{u}", [P, T]) for u in range(2)]
        ps = [pb(f"op_ps{u}", [P, 3 * 512]) for u in range(2)]
        in_s, mm_s, out_s, st_s = ([sem(f"f3_{n}{u}") for u in range(2)] for n in ("in", "mm", "out", "st"))
        count_from_one(nc, out_s, st_s)
        with nc.Block() as block:

            @block.sync
            def _(sp):
                with sp.Fori(0, KD // 2) as i:
                    for u in range(2):
                        sp.wait_ge(st_s[u], 16 * i + 1)
                        sp.dma_start(w[u][:], d["w_out"][bass.ds(2 * i + u, 1), :, :, :].rearrange("o p k n -> p (o k) n"))\
                            .then_inc(in_s[u], 16)
                        sp.dma_start(x[u][:], d["xT"][bass.ds(2 * i + u, 1), :, :].rearrange("o p t -> p (o t)"))\
                            .then_inc(in_s[u], 16)

            @block.tensor
            def _(pe):
                with pe.Fori(0, KD // 2) as i:
                    for u in range(2):
                        pe.wait_ge(in_s[u], 32 * i + 32)
                        pe.wait_ge(out_s[u], i + 1)
                        for a, b in COLS:
                            for k in range(KD):
                                mm = nc.tensor.matmul(ps[u][:, a:b], w[u][:, k, :], merged[:, k, a:b],
                                                      start=(k == 0), stop=(k == KD - 1))
                        mm.then_inc(mm_s[u], 1)

            @block.vector
            def _(dve):
                g1 = g["mod"][:, 2 * KD:3 * KD, :]
                with dve.Fori(0, KD // 2) as i:
                    for u in range(2):
                        dve.wait_ge(mm_s[u], i + 1)
                        dve.wait_ge(in_s[u], 32 * i + 32)
                        for s, a, b in SEGS:
                            op = nc.vector.scalar_tensor_tensor(
                                x[u][:, a:b], ps[u][:, a:b], g1[:, bass.ds(2 * i + u, 1), s:s + 1]
                                .rearrange("p o s -> p (o s)"), x[u][:, a:b], ALU.mult, ALU.add)
                        op.then_inc(out_s[u], 1)

            @block.scalar
            def _(act):
                with act.Fori(0, KD // 2) as i:
                    for u in range(2):
                        act.wait_ge(out_s[u], i + 2)
                        act.dma_start(x1[bass.ds(2 * i + u, 1), :, :].rearrange("o p t -> p (o t)"), x[u][:])\
                            .then_inc(st_s[u], 16)
                for u in range(2):
                    act.wait_ge(st_s[u], 16 * KD // 2 + 1)


def store_rows(nc, name, pairs):
    with ExitStack() as ctx:
        done = opener(nc, ctx)[2](name)
        block = ctx.enter_context(nc.Block())

        @block.sync
        def _(sp):
            for dst, src in pairs:
                sp.dma_start(dst, src).then_inc(done, 16)
            sp.wait_ge(done, 16 * len(pairs))


N_KEYS = 128
TOPK = 16
SLOTS = H * TOPK
TG = 256
GROUPS = T // TG
TW = 64
TR8 = 8


def peer_select(nc, d, hh, hl, slots):
    NTC = 2 * NT
    with ExitStack() as ctx:
        sb, pb, sem = opener(nc, ctx)
        w = [sb(f"ps_w{c}", [P, KD, P]) for c in range(2)]
        wh, wl = ([sb(f"ps_w{x}{c}", [P, KD, P], F32R) for c in range(2)] for x in "hl")
        keys = sb("ps_keys", [P, 2, N_KEYS])
        qT = [sb(f"ps_qT{c}", [P, T]) for c in range(2)]
        sc = [sb(f"ps_sc{b}", [P, NTC, N_KEYS]) for b in range(2)]
        sc2 = sb("ps_sc2", [P, 2, N_KEYS])
        v = sb("ps_v", [P, NTC, TOPK])
        ix = sb("ps_ix", [P, NTC, TOPK], U32)
        ixf = sb("ps_ixf", [P, NTC, TOPK])
        cand, cand2 = sb("ps_cand", [P, NT, TOPK, TOPK]), sb("ps_cand2", [P, 2, TOPK, TOPK])
        top = sb("ps_top", [P, NT, TOPK])
        pos, pa = sb("ps_pos", [P, NT, TOPK], U32), sb("ps_pa", [P, NT, TOPK], U32)
        paf = sb("ps_paf", [P, NT, TOPK])
        ex, sm = sb("ps_ex", [P, NT, TOPK]), sb("ps_sm", [P, NT])
        iota = sb("ps_iota", [P, TOPK])
        ident = sb("ps_ident", [P, P])
        res = sb("ps_res", [P, 3, NT, SLOTS])
        psq = pb("ps_psq", [P, 3 * 512])
        pss = pb("ps_pss", [P, NTC, N_KEYS])
        names = ("in0", "ink", "qmm", "qcp", "smm", "scp", "used", "sub", "ex", "head", "tr", "tcp", "link", "passed")
        (in0_s, ink_s, qmm_s, qcp_s, smm_s, scp_s, used_s, sub_s, ex_s, head_s, tr_s, tcp_s, link_s, passed_s) = (
            sem("g1_" + x) for x in names)
        inw_s, w_hi, w_lo = ([sem(f"g1_{x}{c}") for c in range(2)] for x in ("inw", "whi", "wlo"))
        TR = 5
        count_from_one(nc, qcp_s, scp_s, smm_s, used_s, w_lo)
        with nc.Block() as block:

            @block.sync
            def _(sp):
                sp.dma_start(iota[:], d["c_iota"][:, 0:TOPK]).then_inc(in0_s, 16)
                sp.dma_start(ident[:], d["c_ident"]).then_inc(in0_s, 16)
                with sp.Fori(0, H) as i:
                    for c in range(2):
                        sp.wait_ge(w_lo[c], i + 1)
                        sp.dma_start(w[c][:], d["peer_wq"][bass.ds(2 * i + c, 1), :, :, :]
                                     .rearrange("o p k n -> p (o k) n")).then_inc(inw_s[c], 16)
                    sp.wait_ge(smm_s, i + 1)
                    sp.dma_start(keys[:], d["peer_keys"][bass.ds(i, 1), :, :, :].rearrange("o p c n -> p (o c) n"))\
                        .then_inc(ink_s, 16)

            @block.gpsimd
            def _(gp):
                with gp.Fori(0, H) as i:
                    for c in range(2):
                        gp.wait_ge(w_hi[c], i + 1)
                        nc.gpsimd.tensor_tensor(wl[c][:], w[c][:], wh[c][:], ALU.subtract).then_inc(w_lo[c], 1)

            @block.tensor
            def _(pe):
                with pe.Fori(0, H) as i:
                    for c in range(2):
                        pe.wait_ge(w_lo[c], i + 2)
                        pe.wait_ge(qcp_s, 2 * i + c + 1)
                        for a, b in COLS:
                            for k in range(KD):
                                for n, (s, m) in enumerate(((wh, hh), (wh, hl), (wl, hh))):
                                    mm = nc.tensor.matmul(psq[:, a:b], s[c][:, k, :], m[:, k, a:b],
                                                          start=(k == 0 and n == 0), stop=(k == KD - 1 and n == 2))
                        mm.then_inc(qmm_s, 1)
                    pe.wait_ge(qcp_s, 2 * i + 2 + 1)
                    pe.wait_ge(ink_s, 16 * i + 16)
                    pe.wait_ge(scp_s, i + 1)
                    for t in range(NT):
                        for c in range(2):
                            mm = nc.tensor.matmul(pss[:, 2 * t + c, :], qT[c][:, t * P:(t + 1) * P], keys[:, c, :],
                                                  start=True, stop=True)
                    mm.then_inc(smm_s, 1)
                pe.wait_ge(head_s, H)
                pe.wait_ge(scp_s, H + 1)
                pe.wait_ge(in0_s, 32)
                for n in range(3 * NT // TR):
                    if n >= 2:
                        pe.wait_ge(tcp_s, n - 1)
                    for y in range(TR):
                        q, t = divmod(n * TR + y, NT)
                        mm = nc.tensor.transpose(pss[:, 8 * (n % 2) + y, :], res[:, q, t, :], ident[:])
                    mm.then_inc(tr_s, 1)

            @block.scalar
            def _(act):
                Copy = lambda out, x: nc.scalar.activation(out, x, ACT.Copy)

                def split(i, c):
                    act.wait_ge(inw_s[c], 16 * i + 16)
                    Copy(wh[c][:], w[c][:]).then_inc(w_hi[c], 1)

                def scores(i, b, last):
                    h = 2 * i + b
                    for c in range(2):
                        act.wait_ge(qmm_s, 2 * h + c + 1)
                        act.wait_ge(smm_s, h + 1)
                        Copy(qT[c][:], psq[:, 0:T]).then_inc(qcp_s, 1)
                        if not last:
                            split(h + 1, c)
                    act.wait_ge(smm_s, h + 2)
                    act.wait_ge(used_s, h + 1)
                    Copy(sc[b % 2][:], pss[:]).then_inc(scp_s, 1)

                def step(i, b, last=False):
                    if not (last and b == 1):
                        scores(i, b + 1, last)
                    act.wait_ge(sub_s, 2 * i + b + 1)
                    nc.scalar.activation(ex[:], ex[:], ACT.Exp).then_inc(ex_s, 1)

                for c in range(2):
                    split(0, c)
                scores(0, 0, False)
                with act.Fori(0, H // 2 - 1) as i:
                    for b in range(2):
                        step(i, b)
                for b in range(2):
                    step(H // 2 - 1, b, True)
                for n in range(3 * NT // TR):
                    act.wait_ge(tr_s, n + 1)
                    q, t = divmod(n * TR, NT)
                    nc.scalar.activation(slots[:, q, t * P:(t + TR) * P],
                                         pss[:, 8 * (n % 2):8 * (n % 2) + TR, :].rearrange("p a t -> p (a t)"),
                                         ACT.Copy).then_inc(tcp_s, 1)

            @block.vector
            def _(dve):
                V = nc.vector
                LOW = -3.0e38

                def top16(link, rows, done=None):
                    ops = (lambda x, s, t, at: V.max(t[:, 0:8], x),
                           lambda x, s, t, at: V.max_index(at[:, 0:8], t[:, 0:8], x),
                           lambda x, s, t, at: V.match_replace(s, t[:, 0:8], x, LOW),
                           lambda x, s, t, at: V.max(t[:, 8:16], s),
                           lambda x, s, t, at: V.max_index(at[:, 8:16], t[:, 8:16], s))
                    for op in ops:
                        for r in rows[:-1]:
                            op(*r)
                        ins = op(*rows[-1])
                        if op is ops[-1] and done is not None:
                            ins.then_inc(done, 1)
                        else:
                            link(ins)

                def rank(i, b):
                    h = 2 * i + b
                    link = linker(dve, link_s, again=True)
                    hold(dve, passed_s, (scp_s, h + 2))
                    for n in range(0, NTC, 2):
                        top16(link, [(sc[b][:, n + y, :], sc2[:, y, :], v[:, n + y, :], ix[:, n + y, :])
                                     for y in range(2)], used_s if n == NTC - 2 else None)
                    dve.wait_ge(used_s, h + 2)
                    link(V.tensor_copy(ixf[:], ix[:]))
                    vv = v[:].rearrange("p (t c) k -> p t c k", c=2)
                    link(V.tensor_tensor(cand[:], vv[:, :, 0, :].unsqueeze(3).broadcast_to([P, NT, TOPK, TOPK]),
                                         vv[:, :, 1, :].unsqueeze(2).broadcast_to([P, NT, TOPK, TOPK]), ALU.add))
                    for t in range(0, NT, 2):
                        top16(link, [(cand[:, t + y, :, :].rearrange("p a b -> p (a b)"),
                                      cand2[:, y, :, :].rearrange("p a b -> p (a b)"), top[:, t + y, :],
                                      pos[:, t + y, :]) for y in range(2)])
                    V.tensor_tensor(ex[:], top[:], top[:, :, 0:1].broadcast_to([P, NT, TOPK]), ALU.subtract)\
                        .then_inc(sub_s, 1)
                    ixv = ixf[:].rearrange("p (t c) k -> p t c k", c=2)
                    for c, (op, n) in enumerate(((ALU.logical_shift_right, 4), (ALU.bitwise_and, 15))):
                        link(V.tensor_scalar(pa[:], pos[:], n, None, op))
                        link(V.tensor_copy(paf[:], pa[:]))
                        link(V.tensor_tensor(cand[:].rearrange("p t a b -> p (t a) b"),
                                             paf[:].rearrange("p t k -> p (t k)").unsqueeze(2)
                                             .broadcast_to([P, NT * TOPK, TOPK]),
                                             iota[:].unsqueeze(1).broadcast_to([P, NT * TOPK, TOPK]), ALU.is_equal))
                        link(V.tensor_tensor(cand[:], cand[:], ixv[:, :, c, :].unsqueeze(2)
                                             .broadcast_to([P, NT, TOPK, TOPK]), ALU.mult))
                        link(V.tensor_reduce(res[:, c, :, bass.ds(h * TOPK, TOPK)], cand[:], AX.X, ALU.add))
                    dve.wait_ge(ex_s, h + 1)
                    link(V.tensor_reduce(sm[:], ex[:], AX.X, ALU.add))
                    link(V.reciprocal(sm[:], sm[:]))
                    V.tensor_tensor(res[:, 2, :, bass.ds(h * TOPK, TOPK)], ex[:],
                                    sm[:].unsqueeze(2).broadcast_to([P, NT, TOPK]), ALU.mult).then_inc(head_s, 1)

                dve.wait_ge(in0_s, 32)
                with dve.Fori(0, H // 2) as i:
                    for b in range(2):
                        rank(i, b)


def peer_gates(nc, d, slots, gates):
    with ExitStack() as ctx:
        sb, pb, sem = opener(nc, ctx)
        slab = [sb(f"pg_slab{p}", [P, N_KEYS, TW]) for p in range(2)]
        row = sb("pg_row", [P, P])
        iota = sb("pg_iota", [P, P, TR8], BF16)
        part = sb("pg_part", [P, 5, T], BF16)
        rest = sb("pg_rest", [P, T])
        o1 = [sb(f"pg_o1{b}", [P, P, TR8], BF16) for b in range(2)]
        hot = [sb(f"pg_hot{b}", [P, P, TR8], BF16) for b in range(2)]
        o2 = [sb(f"pg_o2{b}", [P, 3, P, TR8], BF16) for b in range(2)]
        ps = [pb(f"pg_ps{b}", [P, TR8, P]) for b in range(2)]
        in_s, link_s = sem("gg_in"), sem("gg_link")
        hot_s, mm_s, copied_s = ([sem(f"gg_{x}{b}") for b in range(2)] for x in ("hot", "mm", "copied"))
        st_s = [sem(f"gg_st{p}") for p in range(2)]
        ROUNDS = TW // TR8
        count_from_one(nc, mm_s, copied_s, st_s)
        with nc.Block() as block:

            @block.sync
            def _(sp):
                sp.dma_start(row[:], d["c_iota"]).then_inc(in_s, 16)
                with sp.Fori(0, T // TW // 2) as s:
                    for p in range(2):
                        for b in range(2):
                            sp.wait_ge(copied_s[b], (2 * s + (p + 1)) * (ROUNDS // 2) + 1)
                        sp.dma_start(gates[:, :, bass.ds(2 * s + p, 1), :, :].rearrange("n p o b t -> p n (o b t)"),
                                     slab[p][:].rearrange("p (n b) t -> p n (b t)", b=2)).then_inc(st_s[p], 16)
                for p in range(2):
                    sp.wait_ge(st_s[p], 16 * (T // TW // 2) + 1)

            @block.vector
            def _(dve):
                V = nc.vector
                link = linker(dve, link_s)
                dve.wait_ge(in_s, 16)
                link(V.tensor_copy(iota[:], row[:].unsqueeze(2).broadcast_to([P, P, TR8])))
                link(V.tensor_copy(part[:, 0:3, :], slots[:]))
                link(V.tensor_tensor(rest[:], slots[:, 2, :], part[:, 2, :], ALU.subtract))
                link(V.tensor_copy(part[:, 3, :], rest[:]))
                link(V.tensor_tensor(rest[:], rest[:], part[:, 3, :], ALU.subtract))
                link(V.tensor_copy(part[:, 4, :], rest[:]))
                with dve.Fori(0, T // TR8 // 2) as i:
                    again = linker(dve, link_s, again=True)
                    for b in range(2):
                        at = lambda a: part[:, a, bass.ds(i * (2 * TR8) + b * TR8, TR8)].unsqueeze(1)\
                            .broadcast_to([P, P, TR8])
                        dve.wait_ge(mm_s[b], i + 1)
                        again(V.tensor_tensor(hot[b][:], iota[:], at(1), ALU.is_equal))
                        V.tensor_tensor(o1[b][:], iota[:], at(0), ALU.is_equal)
                        for a in range(3):
                            op = V.tensor_tensor(o2[b][:, a], hot[b][:], at(2 + a), ALU.mult)
                        op.then_inc(hot_s[b], 1)

            @block.tensor
            def _(pe):
                with pe.Fori(0, T // TR8 // 2) as i:
                    for b in range(2):
                        pe.wait_ge(hot_s[b], i + 1)
                        pe.wait_ge(copied_s[b], i + 1)
                        for t in range(TR8):
                            for a in range(3):
                                mm = nc.tensor.matmul(ps[b][:, t, :], o1[b][:, :, t], o2[b][:, a, :, t],
                                                      start=(a == 0), stop=(a == 2))
                        mm.then_inc(mm_s[b], 1)

            @block.scalar
            def _(act):
                with act.Fori(0, T // TW // 2) as s:
                    for p in range(2):
                        act.wait_ge(st_s[p], 16 * s + 1)
                        with act.Fori(0, ROUNDS // 2) as i:
                            for b in range(2):
                                act.wait_ge(mm_s[b], (2 * s + p) * (ROUNDS // 2) + i + 2)
                                nc.scalar.activation(slab[p][:, :, bass.ds(i * (2 * TR8) + b * TR8, TR8)]
                                                     .rearrange("p k t -> p t k"),
                                                     ps[b][:], ACT.Copy).then_inc(copied_s[b], 1)


def split_rows(nc, x, hi, lo):
    with ExitStack() as ctx:
        sb, pb, sem = opener(nc, ctx)
        hi_s = sem("sr_hi")
        with nc.Block() as block:

            @block.scalar
            def _(act):
                for k in range(KD):
                    nc.scalar.activation(hi[:, k, :], x[:, k, :], ACT.Copy).then_inc(hi_s, 1)

            @block.vector
            def _(dve):
                for k in range(KD):
                    dve.wait_ge(hi_s, k + 1)
                    nc.vector.tensor_tensor(lo[:, k, :], x[:, k, :], hi[:, k, :], ALU.subtract)


def peer_experts(nc, d, hh, hl, gates, acc):
    with ExitStack() as ctx:
        sb, pb, sem = opener(nc, ctx)
        ur, vr = sb("pe_ur", [P, KD, P]), sb("pe_vr", [P, D])
        uh, ul = ([[sb(f"pe_u{x}{b}{y}", [P, KD, P], F32R) for y in range(2)] for b in range(2)] for x in "hl")
        vh, vl = ([[sb(f"pe_v{x}{b}{y}", [P, D], F32R) for y in range(2)] for b in range(2)] for x in "hl")
        gt = [sb(f"pe_gt{b}", [P, TG // TW, 2, TW]) for b in range(2)]
        w = sb("pe_w", [P, 2, TG])
        wh, wl = ([sb(f"pe_w{x}{b}", [P, 2, TG], F32R) for b in range(2)] for x in "hl")
        sums = pb("pe_sums", [P, KD, TG])
        scores = [pb(f"pe_s{b}", [P, 2, TG]) for b in range(2)]
        names = ("u_in", "v_in", "u_hi", "u_lo", "v_hi", "v_lo", "scored", "gelu", "w_hi", "w_lo", "zeroed")
        (u_in, v_in, u_hi, u_lo, v_hi, v_lo, scored, gelu, w_hi, w_lo, zeroed) = (
            sem("g2_" + x) for x in names)
        g_in, gated, summed, added = ([sem(f"g2_{x}{b}") for b in range(2)] for x in ("g_in", "gated", "summed", "added"))
        PAIRED = N_KEYS // 2
        U = 2 * GROUPS
        ROUNDS = PAIRED // 2
        HALF = KD // 2
        count_from_one(nc, u_lo, v_lo, gelu, gated, w_lo, added)

        def split_of(x):
            b, q = divmod(x, GROUPS)
            return None if q == GROUPS - 1 else (q % 2, b + 1, q // 2)

        with nc.Block() as block:

            @block.sync
            def _(sp):
                def weights(i, which, pair, y):
                    m = 4 * i + 2 * pair + y
                    if which == 0:
                        sp.wait_ge(u_lo, m + 1)
                        sp.dma_start(ur[:], d["peer_u"][bass.ds(m, 1), :, :, :].rearrange("o p k n -> p (o k) n"))\
                            .then_inc(u_in, 16)
                    else:
                        sp.wait_ge(v_lo, m + 1)
                        sp.dma_start(vr[:], d["peer_v"][:, bass.ds(m, 1), :].rearrange("p o n -> p (o n)"))\
                            .then_inc(v_in, 16)

                def unit(i, x, last):
                    b, q = divmod(x, GROUPS)
                    sp.wait_ge(gated[x % 2], i * GROUPS + x // 2 + 1)
                    sp.dma_start(gt[x % 2][:], gates[bass.ds(2 * i + b, 1), :, 4 * q:4 * q + 4, :, :]
                                 .rearrange("o p x b t -> p (o x) b t")).then_inc(g_in[x % 2], 16)
                    if split_of(x) and not (last and b == 1):
                        weights(i, *split_of(x))

                for y in range(2):
                    for which in range(2):
                        weights(0, which, 0, y)
                with sp.Fori(0, ROUNDS - 1) as i:
                    for x in range(U):
                        unit(i, x, False)
                for x in range(U):
                    unit(ROUNDS - 1, x, True)

            @block.scalar
            def _(act):
                def split(m, which, pair, y):
                    raw, hi, came, done = ((ur, uh, u_in, u_hi), (vr, vh, v_in, v_hi))[which]
                    act.wait_ge(came, 16 * m + 16)
                    nc.scalar.activation(hi[pair % 2][y][:], raw[:], ACT.Copy).then_inc(done, 1)

                def unit(i, x, last):
                    u = i * U + x
                    act.wait_ge(scored, u + 1)
                    act.wait_ge(w_lo, u + 1)
                    nc.scalar.activation(w[:], scores[x % 2][:], ACT.Gelu_apprx_tanh).then_inc(gelu, 1)
                    act.wait_ge(gated[x % 2], i * GROUPS + x // 2 + 2)
                    nc.scalar.activation(wh[x % 2][:], w[:], ACT.Copy).then_inc(w_hi, 1)
                    if split_of(x) and not (last and x >= GROUPS):
                        which, pair, y = split_of(x)
                        split(4 * i + 2 * pair + y, which, pair, y)

                for y in range(2):
                    for which in range(2):
                        split(y, which, 0, y)
                with act.Fori(0, ROUNDS - 1) as i:
                    for x in range(U):
                        unit(i, x, False)
                for x in range(U):
                    unit(ROUNDS - 1, x, True)

            @block.vector
            def _(dve):
                V = nc.vector

                def split(m, which, pair, y):
                    raw, hi, lo, had, done = ((ur, uh, ul, u_hi, u_lo), (vr, vh, vl, v_hi, v_lo))[which]
                    dve.wait_ge(had, m + 1)
                    V.tensor_tensor(lo[pair % 2][y][:], raw[:], hi[pair % 2][y][:], ALU.subtract).then_inc(done, 1)

                def weigh(i, x):
                    u, b = i * U + x, x % 2
                    dve.wait_ge(gelu, u + 2)
                    dve.wait_ge(g_in[b], (i * GROUPS + x // 2) * 16 + 16)
                    V.tensor_tensor(w[:].rearrange("p b (x t) -> p x b t", t=TW),
                                    w[:].rearrange("p b (x t) -> p x b t", t=TW), gt[b][:], ALU.mult)\
                        .then_inc(gated[b], 1)
                    dve.wait_ge(w_hi, u + 1)
                    V.tensor_tensor(wl[b][:], w[:], wh[b][:], ALU.subtract).then_inc(w_lo, 1)

                def unit(i, x, last):
                    if not (last and x == U - 1):
                        weigh(i, x + 1)
                    if split_of(x) and not (last and x >= GROUPS):
                        which, pair, y = split_of(x)
                        split(4 * i + 2 * pair + y, which, pair, y)
                    q = x % GROUPS
                    for a in range(2):
                        dve.wait_ge(summed[a], i * U + x + 1)
                        part = acc[:, a * HALF:(a + 1) * HALF, q * TG:(q + 1) * TG]
                        V.tensor_tensor(part, part, sums[:, a * HALF:(a + 1) * HALF, :], ALU.add).then_inc(added[a], 1)

                V.memset(acc[:], 0.0).then_inc(zeroed, 1)
                for y in range(2):
                    for which in range(2):
                        split(y, which, 0, y)
                weigh(0, 0)
                dve.wait_ge(zeroed, 1)
                with dve.Fori(0, ROUNDS - 1) as i:
                    for x in range(U):
                        unit(i, x, False)
                for x in range(U):
                    unit(ROUNDS - 1, x, True)

            @block.tensor
            def _(pe):
                MM = nc.tensor.matmul

                def score(i, x):
                    u, (b, q) = i * U + x, divmod(x, GROUPS)
                    if q == 0:
                        pe.wait_ge(u_lo, 4 * i + 2 * b + 3)
                    if x > 0:
                        pe.wait_ge(gelu, u)
                    for y in range(2):
                        for k in range(KD):
                            at = slice(q * TG, (q + 1) * TG)
                            for n, (s, m) in enumerate(((uh, hh), (uh, hl), (ul, hh))):
                                mm = MM(scores[x % 2][:, y, :], s[b % 2][y][:, k, :], m[:, k, at],
                                        start=(k == 0 and n == 0), stop=(k == KD - 1 and n == 2))
                    mm.then_inc(scored, 1)

                def unit(i, x, last):
                    u, (b, q) = i * U + x, divmod(x, GROUPS)
                    if not (last and x == U - 1):
                        score(i, x + 1)
                    if q == 0:
                        pe.wait_ge(v_lo, 4 * i + 2 * b + 3)
                    pe.wait_ge(w_lo, u + 2)
                    for a in range(2):
                        pe.wait_ge(added[a], u + 1)
                        for k in range(a * HALF, (a + 1) * HALF):
                            for y in range(2):
                                for n, (s, m) in enumerate(((vh, wh), (vh, wl), (vl, wh))):
                                    mm = MM(sums[:, k, :], s[b][y][:, k * P:(k + 1) * P], m[x % 2][:, y, :],
                                            start=(y == 0 and n == 0), stop=(y == 1 and n == 2))
                        mm.then_inc(summed[a], 1)

                score(0, 0)
                with pe.Fori(0, ROUNDS - 1) as i:
                    for x in range(U):
                        unit(i, x, False)
                for x in range(U):
                    unit(ROUNDS - 1, x, True)


def add_experts(nc, g, x1, acc):
    with ExitStack() as ctx:
        sb, pb, sem = opener(nc, ctx)
        x = sb("ae_x", [P, KD, T])
        in_s = sem("ae_in")
        g2 = g["mod"][:, 5 * KD:6 * KD, :]
        with nc.Block() as block:

            @block.sync
            def _(sp):
                for k in range(KD):
                    sp.dma_start(x[:, k, :], x1[k]).then_inc(in_s, 16)

            @block.vector
            def _(dve):
                dve.wait_ge(in_s, 16 * KD)
                for k in range(KD):
                    for c, a, b in SEGS:
                        nc.vector.scalar_tensor_tensor(acc[:, k, a:b], acc[:, k, a:b], g2[:, k, c:c + 1],
                                                       x[:, k, a:b], ALU.mult, ALU.add)


def constants():
    f = np.float32
    i = np.arange(P)
    row, c = np.meshgrid(np.arange(T_LAT // 64), np.arange(64), indexing="ij")
    quarter = HD // 4
    inv = (f(10000.0) ** (-np.arange(quarter, dtype=f) / f(quarter))).astype(f)
    ang = np.stack([row.reshape(-1), c.reshape(-1)], 1).astype(f)[:, :, None] * inv
    ang = np.concatenate([np.zeros((T_CTX, 2, quarter), f), ang])
    scale = np.array([1.0, HD ** -0.5], f)[None, :, None]
    cos = np.repeat(np.cos(ang)[:, :, None, :], 2, axis=2).reshape(T, 1, HD) * scale
    sin = np.sin(ang).reshape(T, 1, HD // 2) * scale
    one = np.ones((P, 1))
    diff = i[None, :] - i[:, None]
    return {
        "c_cos": cos.reshape(NT, P, 2, HD).astype(f), "c_sin": sin.reshape(NT, P, 2, HD // 2).astype(f),
        "c_ret": np.stack([one * (i + 1), one * (P - i), np.maximum(diff, 0), np.maximum(-diff, 0),
                           diff >= 0, diff <= 0], axis=1).astype(f),
        "c_col": np.stack([P - 1 - i, i], axis=1).astype(f),
        "c_iota": np.repeat(np.arange(P, dtype=f)[None], P, axis=0),
        "c_ident": np.eye(P, dtype=f),
        "c_reset": np.repeat((np.arange(T) % CH != 0)[None], P, axis=0).astype(f),
        "c_blk": np.kron(np.eye(2), np.ones((HD, HD))).astype(f),
        "c_idb": np.tile(np.eye(CH), (2, 1)).astype(f),
        **chunk_masks(),
    }


def chunk_masks():
    s, t = np.arange(CH)[:, None], np.arange(CH)[None, :]
    before = [s < t, s > t]
    mar = np.stack([np.concatenate([b, b | (s == t)], axis=1) for b in before], axis=1)
    mba = np.stack([b.T for b in before], axis=1)
    lev = np.stack([np.stack([b & (s // (2 * n) == t // (2 * n)) & (s // n != t // n) for b in before], axis=1)
                    for n in LEVELS], axis=1)
    both = lambda m: np.ascontiguousarray(np.tile(m, (2,) + (1,) * (m.ndim - 1)).astype(np.float32))
    return {"c_mar": both(mar), "c_mba": both(mba), "c_lev": both(lev)}


def pair_rows(s):
    return s.reshape(2, PAIRS, 2, HD, HD).transpose(2, 3, 0, 1, 4).reshape(P, 2 * PAIRS, HD)


def layouts(i):
    a = {k: np.ascontiguousarray(v) for k, v in i.items()}
    rows = lambda w, n: w.reshape(KD, P, n, -1).transpose(2, 1, 0, 3)
    col = lambda v, n: v.reshape(n, P).T
    x = np.concatenate([a["x_prompt"][0], a["x_sample"][0]])
    out = {
        "xT": x.T.reshape(KD, P, T),
        "cT": np.stack([a["c_ctx"], a["c"][0]]).reshape(2, KD, P).transpose(2, 1, 0),
        "ada_w": rows(a["ada_w"][0], MODS * D // 512),
        "ada_b": col(a["ada_b"][0], MODS * KD),
        "norm1_g": col(a["norm1_g"][0], KD), "norm2_g": col(a["norm2_g"][0], KD),
        "final_g": np.repeat(col(a["final_norm_g"], KD)[:, :, None], 2, axis=2),
        "w_br": np.stack([a[n][0].reshape(PAIRS, P, KD, P) for n in ("w_br_a", "w_br_b")]).transpose(3, 2, 0, 1, 4),
        "w_out": rows(a["w_out"][0], KD),
        "rw_g2": a["rwkv_g2"][0].reshape(P, PAIRS, P).transpose(1, 0, 2),
        "gn_wb": np.stack([a[n][0].reshape(PAIRS, P) for n in ("ret_gn_w", "rwkv_gn_w", "ret_gn_b", "rwkv_gn_b")])
                   .reshape(2, 2, PAIRS, P).transpose(3, 0, 1, 2),
        "peer_wq": rows(a["peer_wq"][0], 2 * H),
        "peer_keys": a["peer_keys"][0].transpose(0, 3, 1, 2),
        "peer_u": a["peer_u"][0].reshape(N_KEYS, N_KEYS, KD, P).transpose(1, 3, 2, 0),
        "peer_v": a["peer_v"][0].reshape(N_KEYS, N_KEYS, D),
        "w_qkv": rows(a["w_in"][0][:, :A_BLOCKS * 512], A_BLOCKS),
        "w_rest": rows(a["w_in"][0][:, A_BLOCKS * 512:], B_BLOCKS),
        "ret_state": pair_rows(a["state_ret"][0, 0]),
        "decay_part": np.repeat(a["ret_decay"][0].reshape(2, PAIRS, 2).transpose(2, 0, 1), HD, axis=0),
        "decay_row": np.repeat(a["ret_decay"][0][None], P, axis=0),
    }
    taps = a["rwkv_conv"][0].reshape(3, 3, PAIRS, P).transpose(2, 3, 1, 0).reshape(PAIRS, P, 9)
    ch = lambda v: v.reshape(-1, PAIRS, P).transpose(1, 2, 0)
    out["rw_cols"] = np.concatenate([taps, ch(a["rwkv_w0"][0]), ch(a["rwkv_a0"][0]), ch(a["rwkv_k_k"][0]),
                                     ch(a["rwkv_k_a"][0]), ch(a["rwkv_r_k"][0].reshape(-1))], axis=2)
    out["rw_wa"] = np.concatenate([a["rwkv_w2"][0], a["rwkv_a2"][0]], axis=1).reshape(2, P, PAIRS, P)\
        .transpose(2, 1, 0, 3)
    out["rw_state"] = pair_rows(a["state_rwkv"][0, 0].transpose(0, 1, 3, 2))
    out.update(constants())
    return {k: np.ascontiguousarray(v) for k, v in out.items()}


def rwkv(nc, d, projT, bonus_v, yT, state_out):
    n = PAIRS * NG
    xs = nc.dram_tensor("rw_xs", [n, P, 2, 4, GT], F32).ap()
    vs = nc.dram_tensor("rw_vs", [n, P, GT], F32).ap()
    ef = nc.dram_tensor("rw_ef", [n, P, 3 * GRP, CH], F32).ap()
    mn = nc.dram_tensor("rw_mn", [2, PAIRS * NCH, P, 2 * CH], F32).ap()
    with ExitStack() as ctx:
        gs = ctx.enter_context(nc.sbuf_tensor("rw_gs", [P, PAIRS, 2, NCH], F32))
        rwkv_operands(nc, d, projT, gs, xs, vs, bonus_v)
        rwkv_chunks(nc, d, xs, vs, ef, mn)
        qs = ctx.enter_context(nc.sbuf_tensor("rw_qs", [P, NCH, 2 * PAIRS, HD], F32))
        rwkv_scan(nc, d, mn, gs, qs, state_out)
        rwkv_outputs(nc, d, ef, qs, yT)


def feed_forward(nc, d, g, x1, y):
    gates = nc.dram_tensor("gates", [N_KEYS // 2, P, T // TW, 2, TW], F32).ap()
    with ExitStack() as ctx:
        rows = lambda c, name, dt=F32: c.enter_context(nc.sbuf_tensor(name, [P, KD, T], dt))
        hh, hl = rows(ctx, "h2_hi", F32R), rows(ctx, "h2_lo", F32R)
        with ExitStack() as c2:
            x, hT = rows(c2, "n2_x"), rows(c2, "h2T")
            rms_norm(nc, g, "n2", x, hT, g["gain2"], g["mod"][:, 3 * KD:4 * KD, :], x1)
            split_rows(nc, hT, hh, hl)
        with ExitStack() as c2:
            slots = c2.enter_context(nc.sbuf_tensor("slots", [P, 3, T], F32))
            peer_select(nc, d, hh, hl, slots)
            peer_gates(nc, d, slots, gates)
        acc = rows(ctx, "expert_sums")
        peer_experts(nc, d, hh, hl, gates, acc)
        add_experts(nc, g, x1, acc)
        yT = rows(ctx, "outT")
        rms_norm(nc, g, "n3", acc, yT, g["nfg"], None)
        store_rows(nc, "y_stored", [(y[k], yT[:, k, :]) for k in range(KD)])


def program(nc, d, out):
    with ExitStack() as ctx:
        sb, pb, sem = opener(nc, ctx)
        g = {
            "mod": sb("mod", [P, MODS * KD, 2]), "gain1": sb("gain1", [P, KD, 2]), "gain2": sb("gain2", [P, KD, 2]),
            "n1g": sb("n1g", [P, KD]), "n2g": sb("n2g", [P, KD]), "nfg": sb("nfg", [P, KD, 2]),
        }
        projT = nc.dram_tensor("projT", [B_BLOCKS, P, T], F32).ap()
        qkv = nc.dram_tensor("qkv", [NT, P, A_BLOCKS, 512], F32).ap()
        modulation(nc, g, d)
        with ExitStack() as c2:
            hT = c2.enter_context(nc.sbuf_tensor("hT", [P, KD, T], F32))
            with ExitStack() as c3:
                x = c3.enter_context(nc.sbuf_tensor("n1_x", [P, KD, T], F32))
                rms_norm(nc, g, "n1", x, hT, g["gain1"], g["mod"][:, 0:KD, :], d["xT"])
            projection(nc, "proj", hT, d["w_rest"], B_BLOCKS, projT)
            qkv_projection(nc, hT, d["w_qkv"], qkv)
        mixers = ExitStack()
        oT = mixers.enter_context(nc.sbuf_tensor("oT", [P, PAIRS, T], F32))
        retention(nc, g, d, qkv, oT, out["ret"])
        bonus_v = nc.dram_tensor("bonus_v", [PAIRS, P, T], F32).ap()
        yT = mixers.enter_context(nc.sbuf_tensor("yT", [P, PAIRS, T], F32))
        rwkv(nc, d, projT, bonus_v, yT, out["rwkv"])
        x1 = nc.dram_tensor("x1", [KD, P, T], F32).ap()
        group_norms(nc, d, projT, bonus_v, oT, yT)
        with ExitStack() as c2:
            merged = c2.enter_context(nc.sbuf_tensor("merged", [P, KD, T], F32))
            branches(nc, d, projT, oT, yT, merged)
            out_projection(nc, d, g, merged, x1)
        mixers.close()
        feed_forward(nc, d, g, x1, out["y"])


def kernel(**inputs):
    import concourse.bacc as bacc
    from concourse.bass_utils import run_bass_kernel_spmd

    laid = layouts({k: np.asarray(v) for k, v in inputs.items()})
    nc = bacc.Bacc("TRN2", target_bir_lowering=False, num_devices=1)
    d = {k: nc.dram_tensor("in_" + k, v.shape, mybir.dt.from_np(v.dtype), kind="ExternalInput").ap()
         for k, v in laid.items()}
    shapes = {"y": [KD, P, T], "ret": [P, 2 * PAIRS, HD], "rwkv": [P, 2 * PAIRS, HD]}
    out = {k: nc.dram_tensor("out_" + k, s, F32, kind="ExternalOutput").ap() for k, s in shapes.items()}
    program(nc, d, out)
    r = run_bass_kernel_spmd(nc, [{"in_" + k: v for k, v in laid.items()}], core_ids=[0]).results[0]
    y = r["out_y"].reshape(D, T).T
    heads = lambda s: s.reshape(2, HD, 2, PAIRS, HD).transpose(2, 3, 0, 1, 4).reshape(2, H, HD, HD)
    ret, rwkv_ = heads(r["out_ret"]), heads(r["out_rwkv"]).transpose(0, 1, 3, 2)
    full = lambda s: np.ascontiguousarray(s)[None, None]
    return (np.ascontiguousarray(y[:T_CTX])[None], np.ascontiguousarray(y[T_CTX:])[None], full(ret), full(rwkv_))
```

```python
import math
from contextlib import ExitStack

import numpy as np

import concourse.bass as bass
from concourse import mybir
from concourse.alu_op_type import AluOpType as ALU

ACT = mybir.ActivationFunctionType
AX = mybir.AxisListType
F32 = mybir.dt.float32
F32R = mybir.dt.float32r
BF16 = mybir.dt.bfloat16
U32 = mybir.dt.uint32

P = 128
D = 1024
KD = D // P
T_CTX, T_LAT = 256, 1024
T = T_CTX + T_LAT
NT = T // P
SEGS = [(0, 0, T_CTX), (1, T_CTX, T)]
COLS = [(0, 512), (512, 1024), (1024, T)]
H, HD = 8, 64
PAIRS = H // 2
MODS = 6
A_BLOCKS = 3
B_BLOCKS = 34
RG, WR, WK, WV, DWDA, DG, GA, GB = 0, 4, 8, 12, 16, 17, 18, 26
NORM_EPS, GN_EPS = 1e-6, 64e-5


def linker(eng, sem, again=False):
    count = [0]
    if again:
        eng.sem_clear(sem)

    def link(ins):
        count[0] += 1
        ins.then_inc(sem, 1)
        eng.wait_ge(sem, count[0])

    return link


def hold(eng, passed, *waits):
    for s, v in waits:
        eng.wait_ge(s, v)
    eng.sem_inc(passed, 1)


def count_from_one(nc, *semaphores):
    for s in semaphores:
        for x in s if isinstance(s, list) else [s]:
            nc.gpsimd.sem_inc(x, 1)
    nc.all_engine_barrier()


def opener(nc, ctx):
    taken = []

    def release():
        if taken:
            nc.clear_and_free_semaphores(taken)
            nc.all_engine_barrier()

    ctx.callback(release)

    def sb(name, shape, dt=F32):
        return ctx.enter_context(nc.sbuf_tensor(name, shape, dt))

    def pb(name, shape, dt=F32):
        return ctx.enter_context(nc.psum_tensor(name, shape, dt))

    def sem(name):
        taken.append(nc.alloc_semaphore(name))
        return taken[-1]

    return sb, pb, sem


def modulation(nc, g, d):
    NB = MODS * D // 512
    with ExitStack() as ctx:
        sb, pb, sem = opener(nc, ctx)
        cT = sb("cT", [P, KD, 2])
        sig = sb("mod_sig", [P, KD, 2])
        act_c = sb("act_c", [P, KD, 2])
        adaw = [sb(f"adaw{u}", [P, KD, 512]) for u in range(2)]
        adab = sb("adab", [P, MODS * KD])
        one = sb("one_plus", [P, KD, 2])
        row = sb("mod_row", [2, MODS * D])
        one_zero = sb("mod_ident", [2, P])
        pr = [pb(f"mod_row_ps{u}", [2, 512]) for u in range(2)]
        pm = pb("mod_psum", [P, MODS * KD, 2])
        in_c, in_small = sem("m_in_c"), sem("m_in_small")
        in_w = [sem(f"m_in_w{u}") for u in range(2)]
        used_w = [sem(f"m_used_w{u}") for u in range(2)]
        copied = [sem(f"m_copied{u}") for u in range(2)]
        sig_done, c_ready, turned, link_s = sem("m_sig"), sem("m_c"), sem("m_turned"), sem("m_link")
        count_from_one(nc, used_w, copied)
        with nc.Block() as block:

            @block.sync
            def _(sp):
                sp.dma_start(cT[:], d["cT"]).then_inc(in_c, 16)
                with sp.Fori(0, NB // 2) as i:
                    for u in range(2):
                        sp.wait_ge(used_w[u], i + 1)
                        sp.dma_start(adaw[u][:], d["ada_w"][bass.ds(i * 2 + u, 1), :, :, :]
                                     .rearrange("o p k n -> p (o k) n")).then_inc(in_w[u], 16)

            @block.scalar
            def _(act):
                act.dma_start(adab[:], d["ada_b"]).then_inc(in_small, 16)
                act.dma_start(one_zero[:], d["c_ident"][0:2, :]).then_inc(in_small, 16)
                act.dma_start(g["n1g"][:], d["norm1_g"]).then_inc(in_small, 16)
                act.dma_start(g["n2g"][:], d["norm2_g"]).then_inc(in_small, 16)
                act.dma_start(g["nfg"][:], d["final_g"]).then_inc(in_small, 16)
                act.wait_ge(in_c, 16)
                nc.scalar.activation(sig[:], cT[:], ACT.Sigmoid).then_inc(sig_done, 1)

            @block.tensor
            def _(pe):
                pe.wait_ge(c_ready, 1)
                with pe.Fori(0, NB // 2) as i:
                    for u in range(2):
                        pe.wait_ge(in_w[u], i * 16 + 16)
                        pe.wait_ge(copied[u], i + 1)
                        for k in range(KD):
                            mm = nc.tensor.matmul(pr[u][:], act_c[:, k, :], adaw[u][:, k, :],
                                                  start=(k == 0), stop=(k == KD - 1))
                        mm.then_inc(used_w[u], 1)
                pe.wait_ge(in_small, 80)
                for u in range(2):
                    pe.wait_ge(copied[u], NB // 2 + 1)
                for c in range(MODS * KD):
                    mm = nc.tensor.matmul(pm[:, c, :], row[:, c * P:(c + 1) * P], one_zero[:, 0:2],
                                          start=True, stop=True)
                mm.then_inc(turned, 1)

            @block.vector
            def _(dve):
                link = linker(dve, link_s)
                dve.wait_ge(sig_done, 1)
                nc.vector.tensor_tensor(act_c[:], cT[:], sig[:], ALU.mult).then_inc(c_ready, 1)
                with dve.Fori(0, NB // 2) as i:
                    for u in range(2):
                        dve.wait_ge(used_w[u], i + 2)
                        nc.vector.tensor_copy(row[:, bass.ds(i * 1024 + u * 512, 512)], pr[u][:]).then_inc(copied[u], 1)
                dve.wait_ge(turned, 1)
                dve.wait_ge(in_small, 80)
                link(nc.vector.tensor_tensor(g["mod"][:], pm[:], adab[:].unsqueeze(2).broadcast_to([P, MODS * KD, 2]),
                                             ALU.add))
                for part, gain, out in ((1, "n1g", "gain1"), (4, "n2g", "gain2")):
                    link(nc.vector.tensor_scalar(one[:], g["mod"][:, part * KD:(part + 1) * KD, :], 1.0, None, ALU.add))
                    link(nc.vector.tensor_tensor(g[out][:], one[:],
                                                 g[gain][:].unsqueeze(2).broadcast_to([P, KD, 2]), ALU.mult))


def rms_norm(nc, name, x, x_dram, gain, shift, split=None, store=None, residual=None):
    with ExitStack() as ctx:
        sb, pb, sem = opener(nc, ctx)
        sq = sb(name + "_sq", [P, 2, T])
        rs = sb(name + "_rs", [P, T])
        ones = sb(name + "_ones", [P, P])
        eps = sb(name + "_eps", [P, 1])
        ps = pb(name + "_ps", [P, 3 * 512])
        in_x = [sem(f"{name}_in_x{k}") for k in range(KD)]
        names = ("added", "sq", "sum", "root", "ones", "link", "scaled", "hi", "stored")
        added, sq_done, sum_done, root_done, ones_done, link_s, scaled, hi_done, stored = (
            sem(f"{name}_{n}") for n in names)
        with nc.Block() as block:

            @block.sync
            def _(sp):
                for k in range(KD):
                    sp.dma_start(x[:, k, :], x_dram[k]).then_inc(in_x[k], 16)
                if store is not None:
                    for k in range(KD):
                        sp.wait_ge(scaled, k + 1)
                        sp.dma_start(store[k], x[:, k, :]).then_inc(stored, 16)
                    sp.wait_ge(stored, 16 * KD)

            @block.scalar
            def _(act):
                for k in range(KD):
                    if residual is None:
                        act.wait_ge(in_x[k], 16)
                    else:
                        act.wait_ge(added, k + 1)
                    if k >= 2:
                        act.wait_ge(sum_done, k - 1)
                    nc.scalar.activation(sq[:, k % 2, :], x[:, k, :], ACT.Square).then_inc(sq_done, 1)
                act.wait_ge(sum_done, KD)
                act.wait_ge(ones_done, 2)
                nc.scalar.activation(rs[:], ps[:, 0:T], ACT.Sqrt, bias=eps[:, 0:1], scale=1.0 / D)\
                    .then_inc(root_done, 1)
                if split is not None:
                    for k in range(KD):
                        act.wait_ge(scaled, k + 1)
                        for s, a, b in SEGS:
                            ins = nc.scalar.activation(split[0][:, k, a:b], x[:, k, a:b], ACT.Identity,
                                                       bias=shift[:, k, s:s + 1])
                        ins.then_inc(hi_done, 1)

            @block.tensor
            def _(pe):
                pe.wait_ge(ones_done, 1)
                for k in range(KD):
                    pe.wait_ge(sq_done, k + 1)
                    for a, b in COLS:
                        mm = nc.tensor.matmul(ps[:, a:b], ones[:], sq[:, k % 2, a:b],
                                              start=(k == 0), stop=(k == KD - 1))
                    mm.then_inc(sum_done, 1)

            @block.vector
            def _(dve):
                STT = nc.vector.scalar_tensor_tensor
                link = linker(dve, link_s)
                nc.vector.memset(ones[:], 1.0).then_inc(ones_done, 1)
                nc.vector.memset(eps[:], NORM_EPS).then_inc(ones_done, 1)
                if residual is not None:
                    sums, factor = residual
                    for k in range(KD):
                        dve.wait_ge(in_x[k], 16)
                        for s, a, b in SEGS:
                            ins = STT(x[:, k, a:b], sums[:, k, a:b], factor[:, k, s:s + 1], x[:, k, a:b],
                                      ALU.mult, ALU.add)
                        ins.then_inc(added, 1)
                dve.wait_ge(root_done, 1)
                link(nc.vector.reciprocal(rs[:], rs[:]))

                def low(k):
                    dve.wait_ge(hi_done, k + 1)
                    for s, a, b in SEGS:
                        STT(split[1][:, k, a:b], x[:, k, a:b], shift[:, k, s:s + 1], split[0][:, k, a:b],
                            ALU.add, ALU.subtract)

                for k in range(KD):
                    dve.wait_ge(in_x[k], 16)
                    if residual is not None:
                        dve.wait_ge(added, k + 1)
                    for s, a, b in SEGS:
                        ins = STT(x[:, k, a:b], x[:, k, a:b], gain[:, k, s:s + 1], rs[:, a:b], ALU.mult, ALU.mult)
                    ins.then_inc(scaled, 1)
                    if split is not None and k >= 1:
                        low(k - 1)
                if split is not None:
                    low(KD - 1)


def split_matmul(nc, out, s, m, start, stop):
    passes = ((s[0], m[0]), (s[0], m[1]), (s[1], m[0]))
    for n, (a, b) in enumerate(passes):
        mm = nc.tensor.matmul(out, a, b, start=start and n == 0, stop=stop and n == len(passes) - 1)
    return mm


def projection(nc, name, hh, hl, weights, blocks, out_dram):
    with ExitStack() as ctx:
        sb, pb, sem = opener(nc, ctx)
        w = [sb(f"{name}_w{u}", [P, KD, P]) for u in range(2)]
        wh, wl = ([sb(f"{name}_w{x}{u}", [P, KD, P], F32R) for u in range(2)] for x in "hl")
        o = [sb(f"{name}_o{u}", [P, T]) for u in range(2)]
        ps = [pb(f"{name}_ps{u}", [P, 3 * 512]) for u in range(2)]
        in_w, w_hi, w_lo, mm_done, copied, stored = (
            [sem(f"{name}_{x}{u}") for u in range(2)] for x in ("in_w", "whi", "wlo", "mm", "cp", "st"))
        n = blocks // 2
        count_from_one(nc, copied, w_lo, stored)
        with nc.Block() as block:

            @block.gpsimd
            def _(pool):
                with pool.Fori(0, n) as i:
                    for u in range(2):
                        pool.wait_ge(w_lo[u], i + 1)
                        pool.dma_start(w[u][:], weights[bass.ds(i * 2 + u, 1), :, :, :]
                                       .rearrange("o p k n -> p (o k) n")).then_inc(in_w[u], 16)

            @block.sync
            def _(sp):
                with sp.Fori(0, n) as i:
                    for u in range(2):
                        sp.wait_ge(copied[u], i + 2)
                        sp.dma_start(out_dram[bass.ds(i * 2 + u, 1), :, :].rearrange("o p t -> p (o t)"), o[u][:])\
                            .then_inc(stored[u], 16)
                for u in range(2):
                    sp.wait_ge(stored[u], n * 16 + 1)

            @block.tensor
            def _(pe):
                with pe.Fori(0, n) as i:
                    for u in range(2):
                        pe.wait_ge(w_lo[u], i + 2)
                        pe.wait_ge(copied[u], i + 1)
                        for a, b in COLS:
                            for k in range(KD):
                                mm = split_matmul(nc, ps[u][:, a:b], (wh[u][:, k, :], wl[u][:, k, :]),
                                                  (hh[:, k, a:b], hl[:, k, a:b]), k == 0, k == KD - 1)
                        mm.then_inc(mm_done[u], 1)

            @block.scalar
            def _(act):
                def split(i, u):
                    act.wait_ge(in_w[u], i * 16 + 16)
                    nc.scalar.activation(wh[u][:], w[u][:], ACT.Copy).then_inc(w_hi[u], 1)

                def copy_out(i, u):
                    act.wait_ge(stored[u], i * 16 + 1)
                    nc.scalar.activation(o[u][:], ps[u][:, 0:T], ACT.Copy).then_inc(copied[u], 1)

                for u in range(2):
                    split(0, u)
                with act.Fori(0, n - 1) as i:
                    for u in range(2):
                        act.wait_ge(mm_done[u], i + 1)
                        split(i + 1, u)
                        copy_out(i, u)
                for u in range(2):
                    act.wait_ge(mm_done[u], n)
                    copy_out(n - 1, u)

            @block.vector
            def _(dve):
                with dve.Fori(0, n) as i:
                    for u in range(2):
                        dve.wait_ge(w_hi[u], i + 1)
                        nc.vector.tensor_tensor(wl[u][:], w[u][:], wh[u][:], ALU.subtract).then_inc(w_lo[u], 1)


def qkv_projection(nc, hh, hl, weights, out_dram):
    with ExitStack() as ctx:
        sb, pb, sem = opener(nc, ctx)
        w = [sb(f"qkv_w{u}", [P, KD, 512]) for u in range(2)]
        wh, wl = ([sb(f"qkv_w{x}{u}", [P, KD, 512], F32R) for u in range(2)] for x in "hl")
        o = [sb(f"qkv_o{u}", [P, 512]) for u in range(2)]
        ps = [pb(f"qkv_ps{u}", [P, 512]) for u in range(2)]
        in_w = [sem(f"qkv_in_w{a}") for a in range(A_BLOCKS)]
        w_hi, w_lo, mm_done, copied = sem("qkv_whi"), sem("qkv_wlo"), sem("qkv_mm"), sem("qkv_cp")
        stored = [sem(f"qkv_st{u}") for u in range(2)]
        with nc.Block() as block:

            @block.sync
            def _(sp):
                for a in range(A_BLOCKS):
                    if a >= 2:
                        sp.wait_ge(w_lo, KD * (a - 1))
                    sp.dma_start(w[a % 2][:], weights[a]).then_inc(in_w[a], 16)

            @block.gpsimd
            def _(pool):
                for n in range(A_BLOCKS * NT):
                    pool.wait_ge(copied, n + 1)
                    pool.dma_start(out_dram[n % NT, :, n // NT, :], o[n % 2][:]).then_inc(stored[n % 2], 16)
                for u in range(2):
                    pool.wait_ge(stored[u], 16 * A_BLOCKS * NT // 2)

            @block.tensor
            def _(pe):
                for n in range(A_BLOCKS * NT):
                    (a, t), b = divmod(n, NT), n // NT % 2
                    if n >= 2:
                        pe.wait_ge(copied, n - 1)
                    for k in range(KD):
                        if t == 0:
                            pe.wait_ge(w_lo, KD * a + k + 1)
                        mm = split_matmul(nc, ps[n % 2][:], (hh[:, k, t * P:(t + 1) * P], hl[:, k, t * P:(t + 1) * P]),
                                          (wh[b][:, k, :], wl[b][:, k, :]), k == 0, k == KD - 1)
                    mm.then_inc(mm_done, 1)

            @block.scalar
            def _(act):
                for a in range(A_BLOCKS):
                    act.wait_ge(in_w[a], 16)
                    if a >= 2:
                        act.wait_ge(mm_done, NT * (a - 1))
                    for k in range(KD):
                        nc.scalar.activation(wh[a % 2][:, k, :], w[a % 2][:, k, :], ACT.Copy).then_inc(w_hi, 1)

            @block.vector
            def _(dve):
                def split(a, k):
                    dve.wait_ge(w_hi, KD * a + k + 1)
                    nc.vector.tensor_tensor(wl[a % 2][:, k, :], w[a % 2][:, k, :], wh[a % 2][:, k, :], ALU.subtract)\
                        .then_inc(w_lo, 1)

                for a in range(2):
                    for k in range(KD):
                        split(a, k)
                for n in range(A_BLOCKS * NT):
                    dve.wait_ge(mm_done, n + 1)
                    if n >= 2:
                        dve.wait_ge(stored[n % 2], 16 * (n // 2))
                    nc.vector.tensor_copy(o[n % 2][:], ps[n % 2][:]).then_inc(copied, 1)
                    if 0 <= n - NT < KD:
                        split(2, n - NT)


def retention(nc, d, qkv, oT, state_out):
    C = P
    with ExitStack() as outer:
        sb, pb, sem = opener(nc, outer)
        kv = sb("ret_kv", [P, NT, 2 * PAIRS, HD])
        rin = sb("ret_rin", [P, NT, 2 * PAIRS, HD])
        cst = sb("ret_cst", [P, 6, P])
        col = sb("ret_col", [P, 2])
        lgp, lgr = sb("ret_lgp", [P, 2, PAIRS]), sb("ret_lgr", [P, 2, H])
        qd = sb("ret_qd", [P, 2, PAIRS, P])
        sd = sb("ret_sd", [P, 2, H])
        cd = sb("ret_cd", [P, 2, PAIRS])
        mask = sb("ret_mask", [P, H, P])
        qkT_dram = nc.dram_tensor("ret_qkT", [NT, P, 2 * PAIRS, P], F32).ap()
        n = NT // 2

        with ExitStack() as ctx:
            sb, pb, sem = opener(nc, ctx)
            tmp = sb("ret_tmp", [P, 4, 16])
            mt = sb("ret_mt", [P, 2, P])
            x = [sb(f"ret_x{u}", [P, 3, 512]) for u in range(2)]
            cos = [sb(f"ret_cos{u}", [P, 2, HD]) for u in range(2)]
            sin = [sb(f"ret_sin{u}", [P, 2, HD // 2]) for u in range(2)]
            xc = sb("ret_xc", [P, 2, 512])
            t1, t2 = sb("ret_t1", [P, 2, 256]), sb("ret_t2", [P, 2, 256])
            ks = [sb(f"ret_ks{u}", [P, 2, 512]) for u in range(2)]
            rot = [sb(f"ret_rot{u}", [P, 2, 512]) for u in range(2)]
            qkT = [sb(f"ret_qkTs{u}", [P, 2 * PAIRS, P]) for u in range(2)]
            ident = sb("ret_ident", [P, P])
            ptr = [pb(f"ret_ptr{u}", [P, 2 * PAIRS, P]) for u in range(2)]
            pkv = [pb(f"ret_pkv{u}", [P, 2 * PAIRS, P]) for u in range(2)]
            in_c, abs_s, dec_s, lg_s, tab_s = sem("r_in_c"), sem("r_abs"), sem("r_dec"), sem("r_lg"), sem("r_tab")
            mask_e, mask_u, link_s, link2_s = sem("r_mask_e"), sem("r_mask_u"), sem("r_link"), sem("r_link2")
            in_x = [sem(f"r_in_x{u}") for u in range(2)]
            rot_s = [sem(f"r_rot{u}") for u in range(2)]
            ks_s = [sem(f"r_ks{u}") for u in range(2)]
            mm_s = [sem(f"r_mm{u}") for u in range(2)]
            tcp_s = [sem(f"r_tcp{u}") for u in range(2)]
            kcp_s = [sem(f"r_kcp{u}") for u in range(2)]
            st_s = [sem(f"r_st{u}") for u in range(2)]
            count_from_one(nc, kcp_s, mask_u, mm_s, rot_s, st_s, tcp_s)
            with nc.Block() as block:

                @block.sync
                def _(sp):
                    sp.dma_start(lgp[:], d["decay_part"]).then_inc(in_c, 16)
                    sp.dma_start(lgr[:], d["decay_row"]).then_inc(in_c, 16)
                    sp.dma_start(cst[:], d["c_ret"]).then_inc(in_c, 16)
                    sp.dma_start(col[:], d["c_col"]).then_inc(in_c, 16)
                    sp.dma_start(ident[:], d["c_ident"]).then_inc(in_c, 16)
                    with sp.Fori(0, n) as i:
                        for u in range(2):
                            sp.wait_ge(mm_s[u], i + 1)
                            sp.wait_ge(rot_s[u], i + 1)
                            t = i * 2 + u
                            sp.dma_start(x[u][:], qkv[bass.ds(t, 1), :, :, :].rearrange("o p a n -> p (o a) n"))\
                                .then_inc(in_x[u], 16)
                            sp.dma_start(cos[u][:], d["c_cos"][bass.ds(t, 1), :, :, :]
                                         .rearrange("o p a n -> p (o a) n")).then_inc(in_x[u], 16)
                            sp.dma_start(sin[u][:], d["c_sin"][bass.ds(t, 1), :, :, :]
                                         .rearrange("o p a n -> p (o a) n")).then_inc(in_x[u], 16)

                @block.scalar
                def _(act):
                    link = linker(act, abs_s)
                    act.wait_ge(in_c, 80)
                    link(nc.scalar.activation(tmp[:, 0, 0:8], lgp[:].rearrange("p a b -> p (a b)"), ACT.Abs))
                    link(nc.scalar.activation(tmp[:, 1, :], lgr[:].rearrange("p a b -> p (a b)"), ACT.Abs))
                    link(nc.scalar.activation(tmp[:, 2, 0:8], tmp[:, 0, 0:8], ACT.Exp, scale=-1.0))
                    link(nc.scalar.activation(tmp[:, 3, :], tmp[:, 1, :], ACT.Exp, scale=-1.0))
                    act.wait_ge(dec_s, 2)
                    link(nc.scalar.activation(tmp[:, 2, 0:8], tmp[:, 2, 0:8], ACT.Ln))
                    nc.scalar.activation(tmp[:, 3, :], tmp[:, 3, :], ACT.Ln).then_inc(lg_s, 1)
                    act.wait_ge(dec_s, 4)
                    for r in range(2):
                        for j in range(PAIRS):
                            nc.scalar.activation(qd[:, r, j, :], cst[:, r, :], ACT.Exp, scale=lgp[:, r, j:j + 1])\
                                .then_inc(tab_s, 1)
                        nc.scalar.activation(sd[:, r, :], lgr[:, r, :], ACT.Exp, scale=col[:, r:r + 1])\
                            .then_inc(tab_s, 1)
                    nc.scalar.activation(cd[:], lgp[:], ACT.Exp, scale=float(C)).then_inc(tab_s, 1)
                    for h in range(H):
                        for r in range(2):
                            if h:
                                act.wait_ge(mask_u, h + 1)
                            nc.scalar.activation(mt[:, r, :], cst[:, 2 + r, :], ACT.Exp, scale=lgr[:, r, h:h + 1])\
                                .then_inc(mask_e, 1)
                    with act.Fori(0, n) as i:
                        for u in range(2):
                            act.wait_ge(mm_s[u], i + 2)
                            act.wait_ge(st_s[u], i * 16 + 1)
                            nc.scalar.activation(qkT[u][:], ptr[u][:], ACT.Copy).then_inc(tcp_s[u], 1)
                            act.wait_ge(tcp_s[u], i + 2)
                            act.dma_start(qkT_dram[bass.ds(i * 2 + u, 1), :, :, :]
                                          .rearrange("o p a n -> p (o a) n"), qkT[u][:]).then_inc(st_s[u], 16)
                    for u in range(2):
                        act.wait_ge(st_s[u], 16 * n + 1)

                @block.tensor
                def _(pe):
                    pe.wait_ge(in_c, 80)
                    with pe.Fori(0, n) as i:
                        for u in range(2):
                            pe.wait_ge(rot_s[u], i + 2)
                            pe.wait_ge(tcp_s[u], i + 1)
                            for a in range(2 * PAIRS):
                                nc.tensor.transpose(ptr[u][:, a, :], rot[u][:].rearrange("p a n -> p (a n)")
                                                    [:, a * P:(a + 1) * P], ident[:])
                            pe.wait_ge(ks_s[u], i + 1)
                            pe.wait_ge(kcp_s[u], i + 1)
                            for r in range(2):
                                for j in range(PAIRS):
                                    mm = nc.tensor.matmul(pkv[u][:, r * PAIRS + j, :], ks[u][:, r, j * P:(j + 1) * P],
                                                          x[u][:, 2, j * P:(j + 1) * P], start=True, stop=True)
                            mm.then_inc(mm_s[u], 1)

                @block.vector
                def _(dve):
                    link = linker(dve, link_s)
                    dve.wait_ge(abs_s, 4)
                    nc.vector.tensor_scalar(tmp[:, 2, 0:8], tmp[:, 2, 0:8], 1.0, None, ALU.add).then_inc(dec_s, 1)
                    nc.vector.tensor_scalar(tmp[:, 3, :], tmp[:, 3, :], 1.0, None, ALU.add).then_inc(dec_s, 1)
                    dve.wait_ge(lg_s, 1)
                    dve.wait_ge(abs_s, 5)
                    for lg, q, w in ((lgp, 2, 8), (lgr, 3, 16)):
                        v = lg[:].rearrange("p a b -> p (a b)")
                        nc.vector.scalar_tensor_tensor(v, v, 0.0, tmp[:, q, 0:w], ALU.min, ALU.subtract)\
                            .then_inc(dec_s, 1)
                    for h in range(H):
                        dve.wait_ge(mask_e, 2 * h + 2)
                        link(nc.vector.tensor_tensor(mt[:], mt[:], cst[:, 4:6, :], ALU.mult))
                        nc.vector.tensor_tensor(mask[:, (h % 2) * PAIRS + h // 2, :], mt[:, 0, :], mt[:, 1, :],
                                                ALU.add).then_inc(mask_u, 1)
                    dve.wait_ge(tab_s, 11)
                    with dve.Fori(0, n) as i:
                        step = linker(dve, link2_s, again=True)
                        for u in range(2):
                            xq = x[u][:, 0:2, :]
                            dve.wait_ge(in_x[u], i * 48 + 48)
                            step(nc.vector.tensor_tensor(
                                xc[:].rearrange("p a (h c) -> p a h c", h=H), xq.rearrange("p a (h c) -> p a h c", h=H),
                                cos[u][:].unsqueeze(2).broadcast_to([P, 2, H, HD]), ALU.mult))
                            for a in range(2):
                                v = xq[:, a, :].rearrange("p (h s j f) -> p h s j f", h=H, s=2, j=2)
                                sn = sin[u][:, a, :].rearrange("p (s f) -> p s f", s=2).unsqueeze(1)\
                                    .broadcast_to([P, H, 2, 16])
                                for j, t in ((0, t1), (1, t2)):
                                    step(nc.vector.tensor_tensor(
                                        t[:, a, :].rearrange("p (h s f) -> p h s f", h=H, s=2), v[:, :, :, j, :],
                                        sn, ALU.mult))
                            dve.wait_ge(mm_s[u], i + 1)
                            half = lambda w, j: w[:].rearrange("p a (b j f) -> p (a b) j f", j=2, f=16)[:, :, j, :]
                            full = lambda w: w[:].rearrange("p a (b f) -> p (a b) f", f=16)
                            step(nc.vector.tensor_tensor(half(rot[u], 0), half(xc, 0), full(t2), ALU.subtract))
                            nc.vector.tensor_tensor(half(rot[u], 1), half(xc, 1), full(t1), ALU.add)\
                                .then_inc(rot_s[u], 1)
                            dve.wait_ge(rot_s[u], i + 2)
                            step(nc.vector.tensor_tensor(
                                ks[u][:, 0, :].rearrange("p (h c) -> p h c", h=H),
                                rot[u][:, 1, :].rearrange("p (h c) -> p h c", h=H),
                                sd[:, 0, :].unsqueeze(2).broadcast_to([P, H, HD]), ALU.mult))
                            nc.vector.tensor_tensor(
                                ks[u][:, 1, :].rearrange("p (h c) -> p h c", h=H),
                                rot[u][:, 1, :].rearrange("p (h c) -> p h c", h=H),
                                sd[:, 1, :].unsqueeze(2).broadcast_to([P, H, HD]), ALU.mult).then_inc(ks_s[u], 1)
                            dve.wait_ge(mm_s[u], i + 2)
                            for e in range(2):
                                q = slice(e * HD, (e + 1) * HD)
                                cp = nc.vector.tensor_copy(
                                    kv[q, bass.ds(i * 2 + u, 1), :, :].rearrange("p o a c -> p (o a) c"),
                                    pkv[u][q, :, q])
                            cp.then_inc(kcp_s[u], 1)

        with ExitStack() as ctx:
            sb, pb, sem = opener(nc, ctx)
            qk = [sb(f"ret_qk{u}", [P, 2 * PAIRS, P]) for u in range(2)]
            v = [sb(f"ret_v{u}", [P, 512]) for u in range(2)]
            qs = [sb(f"ret_qs{u}", [P, 2, PAIRS, P]) for u in range(2)]
            rs = [sb(f"ret_rs{u}", [P, 2 * PAIRS, HD]) for u in range(2)]
            pm = [sb(f"ret_pm{u}", [P, H, P]) for u in range(2)]
            fin = sb("ret_fin", [P, 2 * PAIRS, HD])
            dead = sb("ret_dead", [P, 2 * PAIRS, HD])
            psc = [pb(f"ret_psc{u}", [P, H, P]) for u in range(2)]
            po = [pb(f"ret_po{u}", [P, PAIRS, P]) for u in range(2)]
            in_s, rec_s, fin_s, out_s = sem("r2_in"), sem("r2_rec"), sem("r2_fin"), sem("r2_out")
            in_q = [sem(f"r2_in_q{u}") for u in range(2)]
            rs_s = [sem(f"r2_rs{u}") for u in range(2)]
            qs_s = [sem(f"r2_qs{u}") for u in range(2)]
            sc_s = [sem(f"r2_sc{u}") for u in range(2)]
            pm_s = [sem(f"r2_pm{u}") for u in range(2)]
            po_s = [sem(f"r2_po{u}") for u in range(2)]
            oc_s = [sem(f"r2_oc{u}") for u in range(2)]
            FW, BW = slice(0, PAIRS), slice(PAIRS, 2 * PAIRS)
            count_from_one(nc, oc_s, pm_s, po_s)
            with nc.Block() as block:

                @block.sync
                def _(sp):
                    sp.dma_start(rin[:, 2, FW, :], d["ret_state"][:, FW, :]).then_inc(in_s, 16)
                    sp.dma_start(rin[:, NT - 1, BW, :], d["ret_state"][:, BW, :]).then_inc(in_s, 16)
                    with sp.Fori(0, n) as i:
                        for u in range(2):
                            sp.wait_ge(po_s[u], i + 1)
                            t = i * 2 + u
                            sp.dma_start(qk[u][:], qkT_dram[bass.ds(t, 1), :, :, :].rearrange("o p a n -> p (o a) n"))\
                                .then_inc(in_q[u], 16)
                            sp.dma_start(v[u][:], qkv[bass.ds(t, 1), :, 2, :].rearrange("o p n -> p (o n)"))\
                                .then_inc(in_q[u], 16)
                    sp.wait_ge(fin_s, 1)
                    sp.dma_start(state_out, fin[:]).then_inc(out_s, 16)
                    sp.wait_ge(out_s, 16)

                @block.scalar
                def _(act):
                    act.wait_ge(fin_s, 1)
                    with act.Fori(0, n) as i:
                        for u in range(2):
                            act.wait_ge(po_s[u], i + 1)
                            nc.scalar.activation(rs[u][:], rin[:, bass.ds(i * 2 + u, 1), :, :]
                                                 .rearrange("p o a c -> p (o a) c"), ACT.Copy).then_inc(rs_s[u], 1)
                            act.wait_ge(po_s[u], i + 2)
                            nc.scalar.activation(oT[:, :, bass.ds((i * 2 + u) * P, P)], po[u][:], ACT.Copy)\
                                .then_inc(oc_s[u], 1)

                @block.tensor
                def _(pe):
                    with pe.Fori(0, n) as i:
                        for u in range(2):
                            pe.wait_ge(in_q[u], i * 32 + 32)
                            pe.wait_ge(pm_s[u], i + 1)
                            for h in range(H):
                                e, j = h % 2, h // 2
                                q = slice(e * HD, (e + 1) * HD)
                                mm = nc.tensor.matmul(psc[u][:, e * PAIRS + j, :], qk[u][q, PAIRS + j, :], qk[u][q, j, :],
                                                      start=True, stop=True)
                            mm.then_inc(sc_s[u], 1)
                            pe.wait_ge(rs_s[u], i + 1)
                            pe.wait_ge(qs_s[u], i + 1)
                            pe.wait_ge(pm_s[u], i + 2)
                            pe.wait_ge(oc_s[u], i + 1)
                            for h in range(H):
                                e, j = h % 2, h // 2
                                q = slice(e * HD, (e + 1) * HD)
                                nc.tensor.matmul(po[u][q, j, :], v[u][:, h * HD:(h + 1) * HD], pm[u][:, e * PAIRS + j, :],
                                                 start=True, stop=False)
                                for r in range(2):
                                    mm = nc.tensor.matmul(po[u][q, j, :], rs[u][q, r * PAIRS + j, :],
                                                          qs[u][q, r, j, :], start=False, stop=(r == 1))
                            mm.then_inc(po_s[u], 1)

                @block.vector
                def _(dve):
                    link = linker(dve, rec_s)
                    link(nc.vector.memset(rin[:, 0, FW, :], 0.0))
                    link(nc.vector.memset(rin[:, 1, BW, :], 0.0))
                    dve.wait_ge(in_s, 32)
                    for lo, hi in ((0, 1), (2, NT - 1)):
                        for s in range(hi - lo + 1):
                            for r, t, to, part in ((0, lo + s, lo + s + 1, FW), (1, hi - s, hi - s - 1, BW)):
                                if lo <= to <= hi:
                                    dst = rin[:, to, part, :]
                                else:
                                    dst = (fin if hi == 1 else dead)[:, part, :]
                                link(nc.vector.tensor_tensor(dst, rin[:, t, part, :],
                                                             cd[:, r, :].unsqueeze(2).broadcast_to([P, PAIRS, HD]),
                                                             ALU.mult))
                                link(nc.vector.tensor_tensor(dst, dst, kv[:, t, part, :], ALU.add))
                    nc.vector.memset(dead[:, 0, 0:1], 0.0).then_inc(fin_s, 1)
                    with dve.Fori(0, n) as i:
                        for u in range(2):
                            dve.wait_ge(in_q[u], i * 32 + 32)
                            dve.wait_ge(po_s[u], i + 1)
                            for r in range(2):
                                op = nc.vector.tensor_tensor(qs[u][:, r, :, :], qk[u][:, 0:PAIRS, :], qd[:, r, :, :],
                                                             ALU.mult)
                            op.then_inc(qs_s[u], 1)
                            dve.wait_ge(sc_s[u], i + 1)
                            nc.vector.tensor_tensor(pm[u][:], psc[u][:], mask[:], ALU.mult).then_inc(pm_s[u], 1)


CH = 64
NCH = T // CH
GRP = 4
NG = NCH // GRP
GT = GRP * CH
CTX_CH = T_CTX // CH
LEVELS = [1, 2, 4, 8, 16, 32]
QA, QR, QB, QK = range(4)
RW_COLS = 16
COL_W0, COL_A0, COL_KK, COL_KA, COL_RK = 9, 11, 13, 14, 15


def rwkv_operands(nc, d, projT, gs, xs, vs, bonus_v):
    with ExitStack() as ctx:
        sb, pb, sem = opener(nc, ctx)
        raw = sb("rw_raw", [P, 2, T])
        raw_v2 = [sb(f"rw_raw_v{b}", [P, T]) for b in range(2)]
        rkv2 = [sb(f"rw_rkv{b}", [P, 3, T]) for b in range(2)]
        tap = sb("rw_tap", [P, 2, T])
        cols2 = [sb(f"rw_cols{b}", [P, RW_COLS]) for b in range(2)]
        omka = sb("rw_omka", [P, 1])
        wa2 = [sb(f"rw_wa{b}", [P, 2, P]) for b in range(2)]
        lora = sb("rw_lora", [P, T])
        reset = sb("rw_reset", [P, T])
        blk = sb("rw_blk", [P, P])
        eps = sb("rw_eps", [P, 1])
        kk, sq, nrm, rkk, bon = (sb("rw_" + x, [P, T]) for x in ("kk", "sq", "nrm", "rkk", "bon"))
        sw, a, cum, u2, kd = (sb("rw_" + x, [P, T]) for x in ("sw", "a", "cum", "u2", "kd"))
        eR, eA, eN = (sb("rw_" + x, [P, T]) for x in ("eR", "eA", "eN"))
        xo = sb("rw_xo", [P, 4, T])
        psA, psB = pb("rw_psA", [P, 3 * 512]), pb("rw_psB", [P, 3 * 512])
        names = ("in0", "in", "tanh", "kkr", "sqr", "n2", "norm", "rkk", "bonmm", "bonv", "zw", "za", "sw", "a", "u",
                 "e", "xo", "xst", "vst", "link", "init", "tap", "conv", "vc", "began",
                 "passed")
        (in0_s, in_s, tanh_s, kkr_s, sqr_s, n2_s, norm_s, rkk_s, bonmm_s, bonv_s, zw_s, za_s, sw_s, a_s, u_s,
         e_s, xo_s, xst_s, vst_s, link_s, init_s, tap_s, conv_s, vc_s, began_s,
         passed_s) = (sem("e1_" + x) for x in names)
        count_from_one(nc, a_s, sw_s, vst_s, xo_s, xst_s, began_s)
        with nc.Block() as block:

            @block.sync
            def _(sp):
                sp.dma_start(lora[:], projT[DWDA]).then_inc(in0_s, 16)
                sp.dma_start(reset[:], d["c_reset"]).then_inc(in0_s, 16)
                sp.dma_start(blk[:], d["c_blk"]).then_inc(in0_s, 16)
                with sp.Fori(0, PAIRS // 2) as j:
                    for b in range(2):
                        i = 2 * j + b
                        groups = bass.ds(i * NG, NG)
                        sp.wait_ge(vc_s, i + 1)
                        sp.dma_start(vs[groups, :, :].rearrange("g p t -> p g t"),
                                     rkv2[b][:, 2, :].rearrange("p (g t) -> p g t", g=NG)).then_inc(vst_s, 16)
                        sp.wait_ge(bonv_s, i + 1)
                        sp.dma_start(bonus_v[bass.ds(i, 1), :, :].rearrange("o p t -> p (o t)"), bon[:])\
                            .then_inc(vst_s, 16)
                        for r in range(2):
                            sp.wait_ge(xo_s, 2 * i + r + 2)
                            for q in range(4):
                                sp.dma_start(xs[groups, :, r, q, :].rearrange("g p t -> p g t"),
                                             xo[:, q, :].rearrange("p (g t) -> p g t", g=NG)).then_inc(xst_s, 16)
                sp.wait_ge(vst_s, 32 * PAIRS + 1)
                sp.wait_ge(xst_s, 16 * 8 * PAIRS + 1)

            @block.gpsimd
            def _(pool):
                G = nc.gpsimd
                with pool.Fori(0, PAIRS // 2) as j:
                    for b in range(2):
                        i = 2 * j + b
                        cols = cols2[b]
                        hold(pool, passed_s, (began_s, i + 1))
                        link = linker(pool, tap_s, again=True)
                        for q, first in enumerate((WR, WK, WV)):
                            pool.dma_start(raw[:, q, :] if q < 2 else raw_v2[b][:], projT[bass.ds(i + first, 1), :, :]
                                           .rearrange("o p t -> p (o t)")).then_inc(in_s, 16)
                        pool.dma_start(cols[:], d["rw_cols"][bass.ds(i, 1), :, :].rearrange("o p t -> p (o t)"))\
                            .then_inc(in_s, 16)
                        pool.dma_start(wa2[b][:], d["rw_wa"][bass.ds(i, 1), :, :, :].rearrange("o p a t -> p (o a) t"))\
                            .then_inc(in_s, 16)
                        hold(pool, passed_s, (in_s, 80 * i + 80))
                        for q in range(2):
                            w = lambda k: cols[:, 3 * q + k:3 * q + k + 1]
                            x, y = raw[:, q, :], rkv2[b][:, q, :]
                            G.tensor_scalar(tap[:, 0, :], x, w(0), None, ALU.mult)
                            G.tensor_scalar(y, x, w(1), None, ALU.mult)
                            link(G.tensor_scalar(tap[:, 1, :], x, w(2), None, ALU.mult))
                            for _, s, e in SEGS:
                                ins = G.tensor_tensor(y[:, s + 1:e], y[:, s + 1:e], tap[:, 0, s:e - 1], ALU.add)
                            link(ins)
                            for _, s, e in SEGS:
                                ins = G.tensor_tensor(y[:, s:e - 1], y[:, s:e - 1], tap[:, 1, s + 1:e], ALU.add)
                            link(ins)
                        pool.sem_inc(conv_s, 1)

            @block.scalar
            def _(act):
                act.wait_ge(in0_s, 48)
                nc.scalar.activation(lora[0:HD, :], lora[0:HD, :], ACT.Tanh).then_inc(tanh_s, 1)
                act.wait_ge(init_s, 1)
                with act.Fori(0, PAIRS // 2) as j:
                    for b in range(2):
                        i = 2 * j + b
                        cols = cols2[b]
                        act.wait_ge(kkr_s, i + 1)
                        nc.scalar.activation(sq[:], kk[:], ACT.Square).then_inc(sqr_s, 1)
                        act.wait_ge(n2_s, i + 1)
                        nc.scalar.activation(nrm[:], psA[:, 0:T], ACT.Sqrt, bias=eps[:, 0:1]).then_inc(norm_s, 1)
                        for r in range(2):
                            n = 2 * i + r
                            act.wait_ge(zw_s, n + 1)
                            act.wait_ge(xo_s, n + 1)
                            nc.scalar.activation(sw[:], psA[:, 0:T], ACT.Sigmoid, bias=cols[:, COL_W0 + r:COL_W0 + r + 1])\
                                .then_inc(sw_s, 1)
                            act.wait_ge(za_s, n + 1)
                            nc.scalar.activation(a[:], psB[:, 0:T], ACT.Sigmoid, bias=cols[:, COL_A0 + r:COL_A0 + r + 1])\
                                .then_inc(a_s, 1)
                            act.wait_ge(u_s, n + 1)
                            for out, src, sign in (((eR, cum, 1.0), (eA, u2, 1.0), (eN, cum, -1.0)) if r == 0 else
                                                   ((eR, u2, -1.0), (eA, cum, -1.0), (eN, u2, 1.0))):
                                nc.scalar.activation(out[:], src[:], ACT.Exp, scale=sign).then_inc(e_s, 1)
                            nc.scalar.activation(gs[:, bass.ds(i, 1), r, :].rearrange("p o c -> p (o c)"),
                                                 cum[:].rearrange("p (c t) -> p c t", t=CH)[:, :, CH - 1], ACT.Exp)\
                                .then_inc(e_s, 1)

            @block.tensor
            def _(pe):
                pe.wait_ge(in0_s, 48)
                pe.wait_ge(tanh_s, 1)
                with pe.Fori(0, PAIRS // 2) as j:
                    for b in range(2):
                        i = 2 * j + b
                        wa = wa2[b]
                        pe.wait_ge(sqr_s, i + 1)
                        pe.wait_ge(sw_s, 2 * i + 1)
                        for x, y in COLS:
                            mm = nc.tensor.matmul(psA[:, x:y], blk[:], sq[:, x:y], start=True, stop=True)
                        mm.then_inc(n2_s, 1)
                        pe.wait_ge(rkk_s, i + 1)
                        pe.wait_ge(a_s, 2 * i + 1)
                        for x, y in COLS:
                            mm = nc.tensor.matmul(psB[:, x:y], blk[:], rkk[:, x:y], start=True, stop=True)
                        mm.then_inc(bonmm_s, 1)
                        pe.wait_ge(in_s, 80 * i + 80)
                        for r in range(2):
                            if r == 0:
                                pe.wait_ge(norm_s, i + 1)
                            else:
                                pe.wait_ge(sw_s, 2 * i + 2)
                            for x, y in COLS:
                                mm = nc.tensor.matmul(psA[:, x:y], wa[0:HD, r, :], lora[0:HD, x:y], start=True, stop=True)
                            mm.then_inc(zw_s, 1)
                            if r == 0:
                                pe.wait_ge(bonv_s, i + 1)
                            else:
                                pe.wait_ge(a_s, 2 * i + 2)
                            for x, y in COLS:
                                mm = nc.tensor.matmul(psB[:, x:y], wa[HD:P, r, :], lora[HD:P, x:y], start=True, stop=True)
                            mm.then_inc(za_s, 1)

            @block.vector
            def _(dve):
                V = nc.vector
                V.memset(eps[:], 1e-12).then_inc(init_s, 1)
                dve.wait_ge(in0_s, 48)
                with dve.Fori(0, PAIRS // 2) as j:
                    for b in range(2):
                        i = 2 * j + b
                        cols, rkv = cols2[b], rkv2[b]
                        link = linker(dve, link_s, again=True)
                        hold(dve, began_s, (xo_s, 2 * i + 1), (vst_s, 32 * i + 1))
                        dve.wait_ge(conv_s, i + 1)
                        r_, k_, v_ = (rkv[:, q, :] for q in range(3))
                        V.tensor_scalar(kk[:], k_, cols[:, COL_KK:COL_KK + 1], None, ALU.mult).then_inc(kkr_s, 1)
                        V.scalar_tensor_tensor(rkk[:], r_, cols[:, COL_RK:COL_RK + 1], k_, ALU.mult, ALU.mult)\
                            .then_inc(rkk_s, 1)
                        raw_v = raw_v2[b]
                        tap_of = lambda k: cols[:, 6 + k:7 + k]
                        link(V.tensor_scalar(v_, raw_v[:], tap_of(1), None, ALU.mult))
                        for _, s, e in SEGS:
                            ins = V.scalar_tensor_tensor(v_[:, s + 1:e], raw_v[:, s:e - 1], tap_of(0), v_[:, s + 1:e],
                                                         ALU.mult, ALU.add)
                        link(ins)
                        for _, s, e in SEGS:
                            ins = V.scalar_tensor_tensor(v_[:, s:e - 1], raw_v[:, s + 1:e], tap_of(2), v_[:, s:e - 1],
                                                         ALU.mult, ALU.add)
                        ins.then_inc(vc_s, 1)
                        link(V.tensor_scalar(omka[:], cols[:, COL_KA:COL_KA + 1], -1.0, 1.0, ALU.mult, ALU.add))
                        dve.wait_ge(norm_s, i + 1)
                        dve.wait_ge(kkr_s, i + 1)
                        link(V.reciprocal(nrm[:], nrm[:]))
                        link(V.tensor_tensor(kk[:], kk[:], nrm[:], ALU.mult))
                        dve.wait_ge(bonmm_s, i + 1)
                        dve.wait_ge(vc_s, i + 1)
                        V.tensor_tensor(bon[:], psB[:, 0:T], v_, ALU.mult).then_inc(bonv_s, 1)
                        for r in range(2):
                            n = 2 * i + r
                            dve.wait_ge(sw_s, n + 2)
                            link(V.tensor_scalar(sw[:], sw[:], -math.exp(-0.5), None, ALU.mult))
                            link(V.tensor_tensor_scan(cum[:], reset[:], sw[:], 0.0, ALU.mult, ALU.add))
                            c3 = cum[:].rearrange("p (c t) -> p c t", t=CH)
                            link(V.tensor_scalar(kd[:, 0:NCH], c3[:, :, CH - 1], -0.5, None, ALU.mult))
                            link(V.tensor_tensor(c3, c3, kd[:, 0:NCH].unsqueeze(2).broadcast_to([P, NCH, CH]), ALU.add))
                            V.tensor_tensor(u2[:], cum[:], sw[:], ALU.subtract).then_inc(u_s, 1)
                            dve.wait_ge(a_s, n + 2)
                            link(V.tensor_scalar(kd[:], a[:], cols[:, COL_KA:COL_KA + 1], omka[:, 0:1], ALU.mult, ALU.add))
                            link(V.tensor_tensor(kd[:], kd[:], k_, ALU.mult))
                            link(V.tensor_tensor(a[:], a[:], kk[:], ALU.mult))
                            dve.wait_ge(e_s, 4 * n + 4)
                            dve.wait_ge(xst_s, 64 * n + 1)
                            V.tensor_tensor(xo[:, QA, :], kk[:], eA[:], ALU.mult)
                            V.tensor_tensor(xo[:, QR, :], r_, eR[:], ALU.mult)
                            link(V.tensor_tensor(xo[:, QB, :], a[:], eN[:], ALU.mult))
                            V.tensor_tensor(xo[:, QK, :], kd[:], eN[:], ALU.mult).then_inc(xo_s, 1)



def rwkv_chunks(nc, d, xs, vs, ef, mn):
    U = 2 * GRP
    with ExitStack() as ctx:
        sb, pb, sem = opener(nc, ctx)
        x = [sb(f"ch_x{u}", [P, 2, 4, GT]) for u in range(2)]
        vT = [sb(f"ch_vT{u}", [P, GT]) for u in range(2)]
        ident, idb = sb("ch_ident", [P, P]), sb("ch_idb", [P, HD])
        mar = sb("ch_mar", [P, 2, 2 * CH])
        mba = sb("ch_mba", [P, 2, CH])
        lev = sb("ch_lev", [P, len(LEVELS), 2, CH])
        gb = sb("ch_gb", [P, U, 3, CH])
        gk = sb("ch_gk", [P, U, 2, CH])
        lm = sb("ch_lm", [P, U, CH])
        ct = sb("ch_ct", [P, len(LEVELS) + 1, U, CH])
        ay = sb("ch_ay", [P, U, 2, CH])
        kn, vn = sb("ch_kn", [P, U, CH]), sb("ch_vn", [P, GRP, HD])
        tt, uu, yy = sb("ch_tt", [P, U, CH]), sb("ch_uu", [P, U, CH]), sb("ch_yy", [P, U, CH])
        xx, yn = sb("ch_xx", [P, U, CH]), sb("ch_yn", [P, U, CH])
        oe = sb("ch_oe", [P, U + GRP, CH])
        om = sb("ch_om", [P, U, 2, CH])
        b01, b23 = pb("ch_b01", [P, U, 2, CH]), pb("ch_b23", [P, U, 2, CH])
        b4, b5, b6, b7 = (pb(f"ch_b{n}", [P, U, CH]) for n in (4, 5, 6, 7))
        turn = lambda b, k: b[:].rearrange("p (k j) q t -> p k (j q) t", k=2)[:, k]
        nat = [turn(b01, 0), turn(b01, 1), turn(b23, 0)]
        names = ("in0", "gram", "gram_k", "gbm", "gkm", "lm", "nat", "ncp", "vmm", "vcp", "ct", "t0", "y", "ycp", "tm", "um",
                 "tu", "y0", "y0c", "xy", "xyc", "me", "nf", "ec", "mc", "nc", "est", "mst")
        (in0_s, gram_s, gram_k_s, gbm_s, gkm_s, lm_s, nat_s, ncp_s, vmm_s, vcp_s, ct_s, t0_s, y_s, ycp_s, tm_s, um_s,
         tu_s, y0_s, y0c_s, xy_s, xyc_s, me_s, nf_s, ec_s, mc_s, nc_s, est_s, mst_s) = (
            sem("e2_" + n) for n in names)
        in_s = [sem(f"e2_inx{u}") for u in range(2)]
        fc_s = [sem(f"e2_fc{u}") for u in range(2)]
        passed_s = sem("e2_passed")
        NL = len(LEVELS) - 1
        half = [slice(0, HD), slice(HD, P)]
        units = [(e, r, c) for r in range(2) for c in range(GRP) for e in range(2)]
        count_from_one(nc, ct_s, est_s, fc_s, mc_s, mst_s, nc_s, nf_s, tu_s, um_s, xyc_s)
        with nc.Block() as block:

            @block.sync
            def _(sp):
                for t, s in ((ident, "c_ident"), (idb, "c_idb"), (mar, "c_mar"), (mba, "c_mba"), (lev, "c_lev")):
                    sp.dma_start(t[:], d[s]).then_inc(in0_s, 16)
                with sp.Fori(0, PAIRS * NG // 2) as i:
                    for u in range(2):
                        sp.wait_ge(fc_s[u], i + 1)
                        sp.dma_start(x[u][:], xs[bass.ds(2 * i + u, 1), :, :, :, :].rearrange("o p r q t -> p (o r) q t"))\
                            .then_inc(in_s[u], 16)
                        sp.dma_start(vT[u][:], vs[bass.ds(2 * i + u, 1), :, :].rearrange("o p t -> p (o t)"))\
                            .then_inc(in_s[u], 16)

            def parts(u):
                X = lambda e, r, q, c: x[u][half[e], r, q, c * CH:(c + 1) * CH]
                return X

            @block.tensor
            def _(pe):
                MM = nc.tensor.matmul

                def transpose(e, out, x):
                    if e == 0:
                        return nc.tensor.transpose(out, x, ident[half[e], half[e]])
                    return MM(out, x, ident[half[e], half[e]], start=True, stop=True)

                pe.wait_ge(in0_s, 80)
                with pe.Fori(0, PAIRS * NG // 2) as i:
                    for u in range(2):
                        n = 2 * i + u
                        X = parts(u)
                        hold(pe, passed_s, (in_s[u], 32 * i + 32), (xyc_s, 2 * n + 1))
                        for e, r, c in units:
                            MM(b01[half[e], r * GRP + c, :, :], X(e, r, QB, c),
                               x[u][half[e], r, QA:QR + 1, c * CH:(c + 1) * CH], start=True, stop=True)
                        for e, r, c in units:
                            mm = MM(b4[half[e], r * GRP + c, :], X(e, r, QA, c), X(e, r, QB, c), start=True, stop=True)
                        mm.then_inc(gram_s, 1)
                        hold(pe, passed_s, (mc_s, n + 1))
                        for e, r, c in units:
                            mm = MM(b23[half[e], r * GRP + c, :, :], X(e, r, QK, c),
                                    x[u][half[e], r, QA:QR + 1, c * CH:(c + 1) * CH], start=True, stop=True)
                        mm.then_inc(gram_k_s, 1)

                        def turned(q, out):
                            for e, r, c in units:
                                mm = transpose(e, out[half[e], r * GRP + c, :], X(e, r, q, c))
                            mm.then_inc(nat_s, 1)

                        hold(pe, passed_s, (lm_s, n + 1))
                        for c in range(GRP):
                            for e in range(2):
                                mm = transpose(e, b4[half[e], c, :], vT[u][half[e], c * CH:(c + 1) * CH])
                        mm.then_inc(vmm_s, 1)
                        turned(QA, nat[0])

                        def between(l):
                            if l == 0:
                                turned(QB, nat[1])
                            if l == 1:
                                hold(pe, passed_s, (gkm_s, n + 1))
                                turned(QK, nat[2])
                            if l == 2:
                                hold(pe, passed_s, (vcp_s, n + 1))
                                for e, r, c in units:
                                    j = r * GRP + c
                                    mm = MM(b4[half[e], j, :], gk[half[e], j, 0, :], vn[half[e], c, :],
                                            start=True, stop=True)
                                mm.then_inc(y0_s, 1)

                        hold(pe, passed_s, (nc_s, n + 1), (fc_s[1 - u], i + u + 1))
                        for l in range(NL):
                            hold(pe, passed_s, (ct_s, n * (NL + 2) + l + 3 + 1),
                                 (t0_s, 2 * n + 2) if l == 0 else (tu_s, n * (2 * NL - 1) + 2 * l + 1))
                            for e, r, c in units:
                                j = r * GRP + c
                                mm = MM(b5[half[e], j, :], ct[half[e], l + 1, j, :], tt[half[e], j, :],
                                        start=True, stop=True)
                            mm.then_inc(y_s, 1)
                            between(l)
                            hold(pe, passed_s, (ycp_s, n * NL + l + 1))
                            if l < NL - 1:
                                for e, r, c in units:
                                    j = r * GRP + c
                                    mm = MM(b6[half[e], j, :], uu[half[e], j, :], yy[half[e], j, :],
                                            start=True, stop=True)
                                mm.then_inc(tm_s, 1)
                            for e, r, c in units:
                                j = r * GRP + c
                                mm = MM(b7[half[e], j, :], yy[half[e], j, :], uu[half[e], j, :],
                                        start=True, stop=True)
                            mm.then_inc(um_s, 1)
                        hold(pe, passed_s, (y0c_s, n + 1), (ncp_s, 3 * n + 3), (tu_s, (n + 1) * (2 * NL - 1) + 1))
                        for e, r, c in units:
                            j = r * GRP + c
                            mm = MM(b01[half[e], j, :, :], uu[half[e], j, :], ay[half[e], j, :, :],
                                    start=True, stop=True)
                        mm.then_inc(xy_s, 1)
                        hold(pe, passed_s, (xyc_s, 2 * n + 2 + 1))
                        for e, r, c in units:
                            j = r * GRP + c
                            mm = MM(b23[half[e], j, :, :], xx[half[e], j, :], gb[half[e], j, 1:3, :],
                                    start=True, stop=True)
                        mm.then_inc(me_s, 1)
                        for e, r, c in units:
                            j = r * GRP + c
                            MM(b5[half[e], j, :], kn[half[e], j, :], vn[half[e], c, :], start=True, stop=False)
                            MM(b5[half[e], j, :], gb[half[e], j, 2, :], yn[half[e], j, :], start=False, stop=True)
                        for c in range(GRP):
                            for e in range(2):
                                for r in range(2):
                                    j = r * GRP + c
                                    MM(b6[half[e], c, :], vn[half[e], c, :], gk[half[e], j, 1, :],
                                       start=(r == 0), stop=False)
                                    mm = MM(b6[half[e], c, :], yn[half[e], j, :], gb[half[e], j, 1, :],
                                            start=False, stop=(r == 1))
                        mm.then_inc(nf_s, 1)

            @block.scalar
            def _(act):
                A = nc.scalar.activation
                with act.Fori(0, PAIRS * NG // 2) as i:
                    for u in range(2):
                        n = 2 * i + u
                        act.wait_ge(nf_s, n + 1)
                        natural = (ay[:, :, 0, :], gb[:, :, 2, :], kn[:])

                        def copy_turned(k):
                            act.wait_ge(nat_s, 3 * n + k + 1)
                            A(natural[k], nat[k], ACT.Copy).then_inc(ncp_s, 1)

                        act.wait_ge(vmm_s, n + 1)
                        A(vn[:], b4[:, 0:GRP, :], ACT.Copy).then_inc(vcp_s, 1)
                        copy_turned(0)
                        for l in range(NL):
                            act.wait_ge(y_s, n * NL + l + 1)
                            if l:
                                act.wait_ge(um_s, n * NL + l + 1)
                            A(yy[:], b5[:], ACT.Copy).then_inc(ycp_s, 1)
                            if l < 2:
                                copy_turned(l + 1)
                            if l == 2:
                                act.wait_ge(y0_s, n + 1)
                                A(ay[:, :, 1, :], b4[:], ACT.Copy).then_inc(y0c_s, 1)
                        act.wait_ge(xy_s, n + 1)
                        A(xx[:], b01[:, :, 0, :], ACT.Copy).then_inc(xyc_s, 1)
                        A(yn[:], b01[:, :, 1, :], ACT.Copy, scale=-1.0).then_inc(xyc_s, 1)
                        act.wait_ge(nf_s, n + 2)
                        act.wait_ge(mst_s, 32 * n + 1)
                        A(om[:, :, 1, :], b5[:], ACT.Copy).then_inc(nc_s, 1)
                        act.wait_ge(nc_s, n + 2)
                        act.wait_ge(mc_s, n + 2)
                        for r in range(2):
                            act.dma_start(mn[r, bass.ds(n * GRP, GRP), :, :].rearrange("c p k -> p c k"),
                                          om[:, r * GRP:(r + 1) * GRP, :, :].rearrange("p c m k -> p c (m k)"))\
                                .then_inc(mst_s, 16)
                        act.wait_ge(fc_s[u], i + 2)
                        act.dma_start(ef[bass.ds(n, 1), :, :, :].rearrange("o p a t -> p (o a) t"), oe[:])\
                            .then_inc(est_s, 16)
                act.wait_ge(mst_s, 32 * PAIRS * NG + 1)
                act.wait_ge(est_s, 16 * PAIRS * NG + 1)

            @block.gpsimd
            def _(pool):
                with pool.Fori(0, PAIRS * NG // 2) as i:
                    for u in range(2):
                        n = 2 * i + u
                        def bc(k, flip):
                            order = (1, 0) if flip else (0, 1)
                            return [lev[:, k, r, :].unsqueeze(1).broadcast_to([P, GRP, CH]) for r in order]
                        pool.wait_ge(lm_s, n + 1)
                        pool.wait_ge(gbm_s, n + 1)
                        pool.wait_ge(um_s, n * NL + 1)
                        for k, src in [(len(LEVELS), lm)] + [(k, gb) for k in range(len(LEVELS))]:
                            m = bc(0, True) if src is lm else bc(k, False)
                            for r in range(2):
                                j = slice(r * GRP, (r + 1) * GRP)
                                op = nc.gpsimd.tensor_tensor(ct[:, k, j, :], lm[:, j, :] if src is lm else gb[:, j, 0, :],
                                                             m[r], ALU.mult)
                            op.then_inc(ct_s, 1)

            @block.vector
            def _(dve):
                V = nc.vector
                dve.wait_ge(in0_s, 80)
                with dve.Fori(0, PAIRS * NG // 2) as i:
                    for u in range(2):
                        n = 2 * i + u
                        dve.wait_ge(gram_s, n + 1)
                        dve.wait_ge(nf_s, n + 1)
                        dve.wait_ge(ct_s, n * (NL + 2) + 1)
                        for r in range(2):
                            j = slice(r * GRP, (r + 1) * GRP)
                            m = mar[:, r, :].unsqueeze(1).broadcast_to([P, GRP, 2 * CH])
                            op = V.tensor_tensor(gb[:, j, 0:2, :].rearrange("p c q t -> p c (q t)"),
                                                 b01[:, j, :, :].rearrange("p c q t -> p c (q t)"), m, ALU.mult)
                        op.then_inc(gbm_s, 1)
                        for r in range(2):
                            j = slice(r * GRP, (r + 1) * GRP)
                            op = V.tensor_tensor(lm[:, j, :], b4[:, j, :],
                                                 mba[:, r, :].unsqueeze(1).broadcast_to([P, GRP, CH]), ALU.mult)
                        op.then_inc(lm_s, 1)
                        dve.wait_ge(gram_k_s, n + 1)
                        for r in range(2):
                            j = slice(r * GRP, (r + 1) * GRP)
                            m = mar[:, r, :].unsqueeze(1).broadcast_to([P, GRP, 2 * CH])
                            op = V.tensor_tensor(gk[:, j, :, :].rearrange("p c q t -> p c (q t)"),
                                                 b23[:, j, :, :].rearrange("p c q t -> p c (q t)"), m, ALU.mult)
                        op.then_inc(gkm_s, 1)
                        eye = idb[:].unsqueeze(1).broadcast_to([P, U, CH])
                        dve.wait_ge(ct_s, n * (NL + 2) + 2 + 1)
                        V.tensor_tensor(tt[:], eye, ct[:, len(LEVELS), :, :], ALU.subtract).then_inc(t0_s, 1)
                        V.tensor_tensor(uu[:], eye, ct[:, 0, :, :], ALU.subtract).then_inc(t0_s, 1)
                        for l in range(NL):
                            if l == 0:
                                dve.wait_ge(t0_s, 2 * n + 2)
                            if l < NL - 1:
                                dve.wait_ge(tm_s, n * (NL - 1) + l + 1)
                                V.tensor_tensor(tt[:], tt[:], b6[:], ALU.subtract).then_inc(tu_s, 1)
                            dve.wait_ge(um_s, n * NL + l + 2)
                            V.tensor_tensor(uu[:], uu[:], b7[:], ALU.subtract).then_inc(tu_s, 1)
                            dve.wait_ge(tu_s, n * (2 * NL - 1) + min(2 * l + 2, 2 * NL - 1) + 1)
                        dve.wait_ge(me_s, n + 1)
                        dve.wait_ge(est_s, 16 * n + 1)
                        dve.wait_ge(mst_s, 32 * n + 1)
                        V.tensor_tensor(oe[:, 0:U, :].rearrange("p (r c) t -> p r c t", r=2),
                                        x[u][:, :, QR, :].rearrange("p r (c t) -> p r c t", c=GRP),
                                        b23[:, :, 0, :].rearrange("p (r c) t -> p r c t", r=2), ALU.subtract)\
                            .then_inc(ec_s, 1)
                        V.tensor_tensor(om[:, :, 0, :], eye, b23[:, :, 1, :], ALU.subtract).then_inc(mc_s, 1)
                        dve.wait_ge(nf_s, n + 2)
                        V.tensor_copy(oe[:, U:U + GRP, :], b6[:, 0:GRP, :]).then_inc(fc_s[u], 1)


def rwkv_scan(nc, d, mn, gs, qs, state_out):
    U = 2 * PAIRS
    LAT = NCH - CTX_CH
    with ExitStack() as ctx:
        sb, pb, sem = opener(nc, ctx)
        mb = [sb(f"sc_mn{u}", [P, U, 2 * CH]) for u in range(2)]
        q = sb("sc_q", [P, U, HD])
        t = sb("sc_t", [P, U, HD])
        fin = sb("sc_fin", [P, U, HD])
        init = sb("sc_init", [P, U, HD])
        g2 = sb("sc_g2", [P, PAIRS, 2, NCH])
        ps = pb("sc_ps", [P, U, HD])
        init_s, mm_s, q_s, cp_s, t_s, fin_s, out_s, link_s, g_s = (
            sem("e3_" + x) for x in ("init", "mm", "q", "cp", "t", "fin", "out", "link", "g"))
        in_s = [sem(f"e3_in{u}") for u in range(2)]
        half = [slice(0, HD), slice(HD, P)]
        FW, BW = slice(0, PAIRS), slice(PAIRS, U)
        passed_s = sem("e3_passed")
        ctx_steps = [(s, CTX_CH - 1 - s) for s in range(CTX_CH)]
        mnv = [mn[r].rearrange("(j c) p k -> p c j k", c=NCH) for r in range(2)]
        count_from_one(nc, in_s, t_s)
        with nc.Block() as block:

            @block.sync
            def _(sp):
                sp.dma_start(init[:], d["rw_state"]).then_inc(init_s, 16)

                def load(u, chunks, k):
                    sp.wait_ge(t_s, k + 1)
                    for r, c in enumerate(chunks):
                        sp.dma_start(mb[u][:, r * PAIRS:(r + 1) * PAIRS, :],
                                     mnv[r][:, bass.ds(c, 1), :, :].rearrange("p o j k -> p (o j) k"))\
                            .then_inc(in_s[u], 16)

                for k, chunks in enumerate(ctx_steps):
                    if k < 2:
                        for r, c in enumerate(chunks):
                            sp.dma_start(mb[k][:, r * PAIRS:(r + 1) * PAIRS, :], mnv[r][:, c, :, :])\
                                .then_inc(in_s[k], 16)
                    else:
                        load(k % 2, chunks, k - 1)
                with sp.Fori(0, LAT // 2) as i:
                    for u in range(2):
                        s = 2 * i + u
                        load(u, (s + CTX_CH, s * -1 + (NCH - 1)), s + CTX_CH - 1)
                sp.wait_ge(fin_s, 1)
                sp.dma_start(state_out, fin[:]).then_inc(out_s, 16)
                sp.wait_ge(out_s, 16)

            @block.tensor
            def _(pe):
                def step(u, arrivals, k):
                    hold(pe, passed_s, (in_s[u], arrivals + 1), (q_s, k + 1))
                    for j in range(U):
                        for e in range(2):
                            mm = nc.tensor.matmul(ps[half[e], j, :], mb[u][half[e], j, 0:CH], q[half[e], j, :],
                                                  start=True, stop=True)
                    mm.then_inc(mm_s, 1)

                for k in range(CTX_CH):
                    step(k % 2, 32 * (k // 2 + 1), k)
                with pe.Fori(0, LAT // 2) as i:
                    for u in range(2):
                        step(u, 32 * i + 32 * (CTX_CH // 2 + 1), 2 * i + (u + CTX_CH))

            @block.scalar
            def _(act):
                def keep(chunks, k):
                    act.wait_ge(q_s, k + 1)
                    for c, w in zip(chunks, (FW, BW)):
                        nc.scalar.activation(qs[:, bass.ds(c, 1), w, :].rearrange("p o j v -> p (o j) v"),
                                             q[:, w, :], ACT.Copy).then_inc(cp_s, 1)

                for k, chunks in enumerate(ctx_steps):
                    keep(chunks, k)
                with act.Fori(0, LAT) as i:
                    keep((i + CTX_CH, i * -1 + (NCH - 1)), i + CTX_CH)

            @block.vector
            def _(dve):
                V = nc.vector
                link = linker(dve, link_s)
                gv = lambda r, c, a=gs: a[:, :, r, bass.ds(c, 1)].broadcast_to([P, PAIRS, HD])
                V.tensor_tensor(g2[:, :, 0, 0:NCH - 1], gs[:, :, 0, 0:NCH - 1], gs[:, :, 0, 1:NCH], ALU.mult)\
                    .then_inc(g_s, 1)
                V.tensor_tensor(g2[:, :, 1, 1:NCH], gs[:, :, 1, 1:NCH], gs[:, :, 1, 0:NCH - 1], ALU.mult)\
                    .then_inc(g_s, 1)
                V.memset(g2[:, :, 0, NCH - 1:NCH], 0.0).then_inc(g_s, 1)
                V.memset(g2[:, :, 1, 0:1], 0.0).then_inc(g_s, 1)
                V.memset(q[:], 0.0).then_inc(q_s, 1)
                dve.wait_ge(g_s, 4)
                dve.wait_ge(init_s, 16)

                def summed(k, u):
                    dve.wait_ge(mm_s, k + 1)
                    V.tensor_tensor(t[:], ps[:], mb[u][:, :, CH:2 * CH], ALU.add).then_inc(t_s, 1)
                    dve.wait_ge(t_s, k + 2)
                    dve.wait_ge(cp_s, 2 * k + 2)

                def hand_over(chunks):
                    V.tensor_tensor(q[:, FW, :], t[:, FW, :], gv(0, chunks[0], g2), ALU.mult)
                    V.tensor_tensor(q[:, BW, :], t[:, BW, :], gv(1, chunks[1], g2), ALU.mult).then_inc(q_s, 1)

                for k, chunks in enumerate(ctx_steps):
                    summed(k, k % 2)
                    if k < CTX_CH - 1:
                        hand_over(chunks)
                link(V.tensor_tensor(fin[:, FW, :], t[:, FW, :], gv(0, CTX_CH - 1), ALU.mult))
                V.tensor_tensor(fin[:, BW, :], t[:, BW, :], gv(1, 0), ALU.mult).then_inc(fin_s, 1)
                V.tensor_tensor(q[:, FW, :], init[:, FW, :], gv(0, CTX_CH), ALU.mult)
                V.tensor_tensor(q[:, BW, :], init[:, BW, :], gv(1, NCH - 1), ALU.mult).then_inc(q_s, 1)
                with dve.Fori(0, LAT // 2) as i:
                    for u in range(2):
                        s = 2 * i + u
                        summed(s + CTX_CH, u)
                        hand_over((s + CTX_CH, s * -1 + (NCH - 1)))


def rwkv_outputs(nc, ef, qs, yT):
    U = 2 * GRP
    with ExitStack() as ctx:
        sb, pb, sem = opener(nc, ctx)
        e_ = [sb(f"y_ef{u}", [P, U + GRP, CH]) for u in range(2)]
        qv = [sb(f"y_q{u}", [P, 2, GRP, HD]) for u in range(2)]
        ps = [pb(f"y_ps{u}", [P, GRP, CH]) for u in range(2)]
        in_s, qc_s, mm_s, y_s = ([sem(f"e4_{x}{u}") for u in range(2)] for x in ("in", "qc", "mm", "y"))
        half = [slice(0, HD), slice(HD, P)]
        passed_s = sem("e4_passed")
        count_from_one(nc, mm_s, y_s)
        with nc.Block() as block:

            @block.sync
            def _(sp):
                with sp.Fori(0, PAIRS * NG // 2) as i:
                    for u in range(2):
                        sp.wait_ge(y_s[u], i + 1)
                        sp.dma_start(e_[u][:], ef[bass.ds(2 * i + u, 1), :, :, :].rearrange("o p a t -> p (o a) t"))\
                            .then_inc(in_s[u], 16)

            @block.scalar
            def _(act):
                for j in range(PAIRS):
                    for q in range(NG):
                        n = j * NG + q
                        u = n % 2
                        if n >= 2:
                            act.wait_ge(mm_s[u], n // 2 + 1)
                        for r in range(2):
                            op = nc.scalar.activation(qv[u][:, r, :, :], qs[:, q * GRP:(q + 1) * GRP, r * PAIRS + j, :],
                                                      ACT.Copy)
                        op.then_inc(qc_s[u], 1)

            @block.tensor
            def _(pe):
                with pe.Fori(0, PAIRS * NG // 2) as i:
                    for u in range(2):
                        hold(pe, passed_s, (in_s[u], 16 * i + 16), (qc_s[u], i + 1), (y_s[u], i + 1))
                        for c in range(GRP):
                            for e in range(2):
                                for r in range(2):
                                    mm = nc.tensor.matmul(ps[u][half[e], c, :], qv[u][half[e], r, c, :],
                                                          e_[u][half[e], r * GRP + c, :], start=(r == 0), stop=(r == 1))
                        mm.then_inc(mm_s[u], 1)

            @block.vector
            def _(dve):
                yv = yT[:].rearrange("p j (g t) -> p (j g) t", g=NG)
                with dve.Fori(0, PAIRS * NG // 2) as i:
                    for u in range(2):
                        dve.wait_ge(mm_s[u], i + 2)
                        nc.vector.tensor_tensor(yv[:, bass.ds(2 * i + u, 1), :].rearrange("p o t -> p (o t)"),
                                                ps[u][:].rearrange("p c t -> p (c t)"),
                                                e_[u][:, U:U + GRP, :].rearrange("p c t -> p (c t)"), ALU.add)\
                            .then_inc(y_s[u], 1)


def group_norms(nc, d, projT, bonus_v, oT, yT):
    with ExitStack() as ctx:
        sb, pb, sem = opener(nc, ctx)
        blk = sb("gn_blk", [P, P])
        eps = sb("gn_eps", [P, 1])
        wb = sb("gn_wb", [P, 2, 2, PAIRS])
        g2 = [sb(f"gn_g2{u}", [P, P]) for u in range(2)]
        dg = sb("gn_dg", [P, T])
        dev = [sb(f"gn_dev{u}", [P, T]) for u in range(2)]
        sq = [sb(f"gn_sq{u}", [P, T]) for u in range(2)]
        gate, sg, bv = sb("gn_gate", [P, T]), sb("gn_sg", [P, T]), sb("gn_bv", [P, T])
        psA, psB = pb("gn_psA", [P, 3 * 512]), pb("gn_psB", [P, 3 * 512])
        names = ("in0", "eps", "dg", "sum", "dev", "sq", "var", "root", "gmm", "sg", "out", "link")
        (in0_s, eps_s, dg_s, sum_s, dev_s, sq_s, var_s, root_s, gmm_s, sg_s, out_s, link_s) = (
            sem("f1_" + x) for x in names)
        in_s = sem("f1_in")
        z = [oT, yT]
        flat = lambda a: a.rearrange("p o t -> p (o t)")
        count_from_one(nc, out_s, root_s)
        with nc.Block() as block:

            @block.sync
            def _(sp):
                sp.dma_start(blk[:], d["c_blk"]).then_inc(in0_s, 16)
                sp.dma_start(wb[:], d["gn_wb"]).then_inc(in0_s, 16)
                sp.dma_start(dg[:], projT[DG]).then_inc(in0_s, 16)
                with sp.Fori(0, PAIRS) as i:
                    sp.wait_ge(out_s, 2 * i + 1)
                    for dst, src, first in ((gate, projT, RG), (bv, bonus_v, 0)):
                        sp.dma_start(dst[:], src[bass.ds(i + first, 1), :, :].rearrange("o p t -> p (o t)"))\
                            .then_inc(in_s, 16)
                    sp.dma_start(g2[0][:], d["rw_g2"][bass.ds(i, 1), :, :].rearrange("o p t -> p (o t)"))\
                        .then_inc(in_s, 16)

            @block.scalar
            def _(act):
                act.wait_ge(in0_s, 48)
                act.wait_ge(eps_s, 1)
                nc.scalar.activation(dg[:], dg[:], ACT.Sigmoid).then_inc(dg_s, 1)
                with act.Fori(0, PAIRS) as i:
                    for u in range(2):
                        act.wait_ge(dev_s, 2 * i + u + 1)
                        nc.scalar.activation(sq[u][:], dev[u][:], ACT.Square).then_inc(sq_s, 1)
                        act.wait_ge(var_s, 2 * i + u + 1)
                        nc.scalar.activation(sq[u][:], psA[:, 0:T], ACT.Sqrt, bias=eps[:, 0:1], scale=1.0 / HD)\
                            .then_inc(root_s, 1)
                        if u == 0:
                            act.wait_ge(in_s, 48 * i + 48)
                            act.wait_ge(out_s, 2 * i + 1)
                            nc.scalar.activation(sg[:], gate[:], ACT.Sigmoid).then_inc(sg_s, 1)

            @block.tensor
            def _(pe):
                pe.wait_ge(in0_s, 48)
                pe.wait_ge(dg_s, 1)
                with pe.Fori(0, PAIRS) as i:
                    for u in range(2):
                        zf = flat(z[u][:, bass.ds(i, 1), :])
                        pe.wait_ge(root_s, 2 * i + u + 1)
                        for x, y in COLS:
                            mm = nc.tensor.matmul(psA[:, x:y], blk[:], z[u][:, bass.ds(i, 1), x:y]
                                                  .rearrange("p o t -> p (o t)"), start=True, stop=True)
                        mm.then_inc(sum_s, 1)
                        pe.wait_ge(sq_s, 2 * i + u + 1)
                        for x, y in COLS:
                            mm = nc.tensor.matmul(psA[:, x:y], blk[:], sq[u][:, x:y], start=True, stop=True)
                        mm.then_inc(var_s, 1)
                    pe.wait_ge(in_s, 48 * i + 48)
                    pe.wait_ge(out_s, 2 * i + 1)
                    for x, y in COLS:
                        mm = nc.tensor.matmul(psB[:, x:y], g2[0][:], dg[:, x:y], start=True, stop=True)
                    mm.then_inc(gmm_s, 1)

            @block.vector
            def _(dve):
                V = nc.vector
                V.memset(eps[:], GN_EPS).then_inc(eps_s, 1)
                dve.wait_ge(in0_s, 48)

                def centre(i, u):
                    dve.wait_ge(sum_s, 2 * i + u + 1)
                    V.scalar_tensor_tensor(dev[u][:], psA[:, 0:T], -1.0 / HD, flat(z[u][:, bass.ds(i, 1), :]),
                                           ALU.mult, ALU.add).then_inc(dev_s, 1)

                def finish(i, u, last=False):
                    zf = flat(z[u][:, bass.ds(i, 1), :])
                    w, b = (wb[:, q, u, bass.ds(i, 1)] for q in range(2))
                    link = linker(dve, link_s, again=True)
                    dve.wait_ge(root_s, 2 * i + u + 2)
                    link(V.reciprocal(sq[u][:], sq[u][:]))
                    dve.wait_ge(out_s, 2 * i + u + 1)
                    if not (last and u == 1):
                        centre(i + u, 1 - u)
                    link(V.tensor_tensor(dev[u][:], dev[u][:], sq[u][:], ALU.mult))
                    link(V.tensor_scalar(dev[u][:], dev[u][:], w, b, ALU.mult, ALU.add))
                    if u == 0:
                        dve.wait_ge(sg_s, i + 1)
                        link(V.tensor_tensor(gate[:], gate[:], sg[:], ALU.mult))
                        V.tensor_tensor(zf, dev[u][:], gate[:], ALU.mult).then_inc(out_s, 1)
                    else:
                        dve.wait_ge(in_s, 48 * i + 48)
                        link(V.tensor_tensor(dev[u][:], dev[u][:], bv[:], ALU.add))
                        dve.wait_ge(gmm_s, i + 1)
                        V.tensor_tensor(zf, psB[:, 0:T], dev[u][:], ALU.mult).then_inc(out_s, 1)

                centre(0, 0)
                with dve.Fori(0, PAIRS - 1) as i:
                    for u in range(2):
                        finish(i, u)
                for u in range(2):
                    finish(PAIRS - 1, u, True)


def branches(nc, d, projT, oT, yT, hh, hl):
    with ExitStack() as ctx:
        sb, pb, sem = opener(nc, ctx)
        w = [sb(f"br_w{u}", [P, 2, PAIRS, P]) for u in range(2)]
        ga = [sb(f"br_ga{u}", [P, 2, T]) for u in range(2)]
        t1 = sb("br_t1", [P, T])
        t2 = sb("br_t2", [P, T])
        merged = [sb(f"br_m{u}", [P, T]) for u in range(2)]
        ps = [pb(f"br_ps{q}", [P, 3 * 512]) for q in range(2)]
        in_s = [sem(f"f2_in{u}") for u in range(2)]
        ing_s = [sem(f"f2_ing{u}") for u in range(2)]
        mm_s = [sem(f"f2_mm{q}") for q in range(2)]
        cp_s = [sem(f"f2_cp{q}") for q in range(2)]
        out_s = [sem(f"f2_out{u}") for u in range(2)]
        sg_s, merged_s, hi_s = sem("f2_sg"), sem("f2_merged"), sem("f2_hi")
        of = lambda t, m: t[:, bass.ds(m, 1), :].rearrange("p o t -> p (o t)")
        z = [oT, yT]
        count_from_one(nc, cp_s, out_s)
        with nc.Block() as block:

            @block.sync
            def _(sp):
                with sp.Fori(0, KD // 2) as i:
                    for u in range(2):
                        m = 2 * i + u
                        sp.wait_ge(out_s[u], i + 1)
                        sp.dma_start(w[u][:], d["w_br"][bass.ds(m, 1), :, :, :, :].rearrange("o p q k n -> p (o q) k n"))\
                            .then_inc(in_s[u], 16)
                        for q, first in enumerate((GA, GB)):
                            sp.dma_start(ga[u][:, q, :], projT[bass.ds(m + first, 1), :, :]
                                         .rearrange("o p t -> p (o t)")).then_inc(ing_s[u], 16)

            @block.scalar
            def _(act):
                with act.Fori(0, KD // 2) as i:
                    for u in range(2):
                        act.wait_ge(ing_s[u], 32 * i + 32)
                        nc.scalar.activation(ga[u][:], ga[u][:], ACT.Sigmoid).then_inc(sg_s, 1)
                        act.wait_ge(merged_s, 2 * i + u + 1)
                        nc.scalar.activation(of(hh, 2 * i + u), merged[u][:], ACT.Copy).then_inc(hi_s, 1)

            @block.tensor
            def _(pe):
                with pe.Fori(0, KD // 2) as i:
                    for u in range(2):
                        m = 2 * i + u
                        pe.wait_ge(in_s[u], 16 * i + 16)
                        for q in range(2):
                            pe.wait_ge(cp_s[q], m + 1)
                            for x, y in COLS:
                                for k in range(PAIRS):
                                    mm = nc.tensor.matmul(ps[q][:, x:y], w[u][:, q, k, :], z[q][:, k, x:y],
                                                          start=(k == 0), stop=(k == PAIRS - 1))
                            mm.then_inc(mm_s[q], 1)

            @block.vector
            def _(dve):
                V = nc.vector
                with dve.Fori(0, KD // 2) as i:
                    for u in range(2):
                        m = 2 * i + u
                        dve.wait_ge(sg_s, m + 1)
                        for q, t in enumerate((t1, t2)):
                            dve.wait_ge(mm_s[q], m + 1)
                            if q == 0:
                                dve.wait_ge(out_s[1 - u], i + u + 1)
                            V.tensor_tensor(t[:], ps[q][:, 0:T], ga[u][:, q, :], ALU.mult).then_inc(cp_s[q], 1)
                        for q in range(2):
                            dve.wait_ge(cp_s[q], m + 2)
                        V.tensor_tensor(merged[u][:], t1[:], t2[:], ALU.add).then_inc(merged_s, 1)
                        dve.wait_ge(hi_s, m + 1)
                        V.tensor_tensor(of(hl, m), merged[u][:], of(hh, m), ALU.subtract).then_inc(out_s[u], 1)


def out_projection(nc, d, g, hh, hl, x1):
    with ExitStack() as ctx:
        sb, pb, sem = opener(nc, ctx)
        w = [sb(f"op_w{u}", [P, KD, P]) for u in range(2)]
        wh, wl = ([sb(f"op_w{y}{u}", [P, KD, P], F32R) for u in range(2)] for y in "hl")
        x = [sb(f"op_x{u}", [P, T]) for u in range(2)]
        ps = [pb(f"op_ps{u}", [P, 3 * 512]) for u in range(2)]
        in_w, in_x, w_hi, w_lo, mm_s, out_s, st_s = (
            [sem(f"f3_{n}{u}") for u in range(2)] for n in ("in_w", "in_x", "whi", "wlo", "mm", "out", "st"))
        ROUNDS = KD // 2
        count_from_one(nc, w_lo, out_s, st_s)
        with nc.Block() as block:

            @block.sync
            def _(sp):
                with sp.Fori(0, ROUNDS) as i:
                    for u in range(2):
                        sp.wait_ge(w_lo[u], i + 1)
                        sp.dma_start(w[u][:], d["w_out"][bass.ds(2 * i + u, 1), :, :, :].rearrange("o p k n -> p (o k) n"))\
                            .then_inc(in_w[u], 16)

            @block.gpsimd
            def _(pool):
                with pool.Fori(0, ROUNDS) as i:
                    for u in range(2):
                        pool.wait_ge(st_s[u], 16 * i + 1)
                        pool.dma_start(x[u][:], d["xT"][bass.ds(2 * i + u, 1), :, :].rearrange("o p t -> p (o t)"))\
                            .then_inc(in_x[u], 16)

            @block.tensor
            def _(pe):
                with pe.Fori(0, ROUNDS) as i:
                    for u in range(2):
                        pe.wait_ge(w_lo[u], i + 2)
                        pe.wait_ge(out_s[u], i + 1)
                        for a, b in COLS:
                            for k in range(KD):
                                mm = split_matmul(nc, ps[u][:, a:b], (wh[u][:, k, :], wl[u][:, k, :]),
                                                  (hh[:, k, a:b], hl[:, k, a:b]), k == 0, k == KD - 1)
                        mm.then_inc(mm_s[u], 1)

            @block.vector
            def _(dve):
                g1 = g["mod"][:, 2 * KD:3 * KD, :]

                def split(i, u):
                    dve.wait_ge(w_hi[u], i + 1)
                    nc.vector.tensor_tensor(wl[u][:], w[u][:], wh[u][:], ALU.subtract).then_inc(w_lo[u], 1)

                def residual(i, u):
                    dve.wait_ge(mm_s[u], i + 1)
                    dve.wait_ge(in_x[u], 16 * i + 16)
                    for s, a, b in SEGS:
                        op = nc.vector.scalar_tensor_tensor(
                            x[u][:, a:b], ps[u][:, a:b], g1[:, bass.ds(2 * i + u, 1), s:s + 1]
                            .rearrange("p o s -> p (o s)"), x[u][:, a:b], ALU.mult, ALU.add)
                    op.then_inc(out_s[u], 1)

                for u in range(2):
                    split(0, u)
                with dve.Fori(0, ROUNDS - 1) as i:
                    for u in range(2):
                        residual(i, u)
                        split(i + 1, u)
                for u in range(2):
                    residual(ROUNDS - 1, u)

            @block.scalar
            def _(act):
                def split(i, u):
                    act.wait_ge(in_w[u], 16 * i + 16)
                    nc.scalar.activation(wh[u][:], w[u][:], ACT.Copy).then_inc(w_hi[u], 1)

                def store(i, u):
                    act.wait_ge(out_s[u], i + 2)
                    act.dma_start(x1[bass.ds(2 * i + u, 1), :, :].rearrange("o p t -> p (o t)"), x[u][:])\
                        .then_inc(st_s[u], 16)

                for u in range(2):
                    split(0, u)
                with act.Fori(0, ROUNDS - 1) as i:
                    for u in range(2):
                        act.wait_ge(mm_s[u], i + 1)
                        split(i + 1, u)
                        store(i, u)
                for u in range(2):
                    store(ROUNDS - 1, u)
                for u in range(2):
                    act.wait_ge(st_s[u], 16 * ROUNDS + 1)


N_KEYS = 128
TOPK = 16
SLOTS = H * TOPK
TG = 256
GROUPS = T // TG
TW = 64
TR8 = 8


def peer_select(nc, d, hh, hl, slots):
    NTC = 2 * NT
    ROWS = 5
    with ExitStack() as ctx:
        sb, pb, sem = opener(nc, ctx)
        w = [sb(f"ps_w{c}", [P, KD, P]) for c in range(2)]
        wh, wl = ([sb(f"ps_w{x}{c}", [P, KD, P], F32R) for c in range(2)] for x in "hl")
        keys = sb("ps_keys", [P, 2, N_KEYS])
        qT = [sb(f"ps_qT{c}", [P, T]) for c in range(2)]
        sc = sb("ps_sc", [P, NTC, N_KEYS])
        sc2 = sb("ps_sc2", [P, ROWS, N_KEYS])
        v = sb("ps_v", [P, NTC, TOPK])
        ix = sb("ps_ix", [P, NTC, TOPK], U32)
        ixf = [sb(f"ps_ixf{b}", [P, NTC, TOPK]) for b in range(2)]
        cand, cand2 = sb("ps_cand", [P, NT, TOPK, TOPK]), sb("ps_cand2", [P, ROWS, TOPK, TOPK])
        top = sb("ps_top", [P, NT, TOPK])
        pos, pa = sb("ps_pos", [P, NT, TOPK], U32), sb("ps_pa", [P, 2, NT, TOPK], U32)
        paf = [sb(f"ps_paf{c}", [P, NT, TOPK]) for c in range(2)]
        pick = [sb(f"ps_pick{c}", [P, NT, TOPK, TOPK]) for c in range(2)]
        ex, sm = [sb(f"ps_ex{b}", [P, NT, TOPK]) for b in range(2)], sb("ps_sm", [P, NT])
        iota = sb("ps_iota", [P, TOPK])
        ident = sb("ps_ident", [P, P])
        res = sb("ps_res", [P, 3, NT, SLOTS])
        psq = pb("ps_psq", [P, 3 * 512])
        pss = pb("ps_pss", [P, NTC, N_KEYS])
        names = ("in0", "ink", "qmm", "qcp", "smm", "scp", "used", "sub", "ex", "head", "tr", "tcp", "link", "passed",
                 "ranked", "picked")
        (in0_s, ink_s, qmm_s, qcp_s, smm_s, scp_s, used_s, sub_s, ex_s, head_s, tr_s, tcp_s, link_s, passed_s,
         ranked_s, picked_s) = (
            sem("g1_" + x) for x in names)
        inw_s, w_hi, w_lo = ([sem(f"g1_{x}{c}") for c in range(2)] for x in ("inw", "whi", "wlo"))
        TR = 5
        count_from_one(nc, qcp_s, scp_s, smm_s, used_s, w_lo)
        with nc.Block() as block:

            @block.sync
            def _(sp):
                sp.dma_start(iota[:], d["c_iota"][:, 0:TOPK]).then_inc(in0_s, 16)
                sp.dma_start(ident[:], d["c_ident"]).then_inc(in0_s, 16)
                with sp.Fori(0, H) as i:
                    for c in range(2):
                        sp.wait_ge(w_lo[c], i + 1)
                        sp.dma_start(w[c][:], d["peer_wq"][bass.ds(2 * i + c, 1), :, :, :]
                                     .rearrange("o p k n -> p (o k) n")).then_inc(inw_s[c], 16)
                    sp.wait_ge(smm_s, i + 1)
                    sp.dma_start(keys[:], d["peer_keys"][bass.ds(i, 1), :, :, :].rearrange("o p c n -> p (o c) n"))\
                        .then_inc(ink_s, 16)

            @block.gpsimd
            def _(gp):
                G = nc.gpsimd

                def split(i):
                    for c in range(2):
                        gp.wait_ge(w_hi[c], i + 1)
                        G.tensor_tensor(wl[c][:], w[c][:], wh[c][:], ALU.subtract).then_inc(w_lo[c], 1)

                def picks(i, b, last=False):
                    h = 2 * i + b
                    if not (last and b == 1):
                        split(h + 1)
                    gp.wait_ge(ranked_s, h + 1)
                    for c in range(2):
                        G.tensor_tensor(pick[c][:], pick[c][:], ixf[b][:].rearrange("p (t c) k -> p t c k", c=2)
                                        [:, :, c, :].unsqueeze(2).broadcast_to([P, NT, TOPK, TOPK]), ALU.mult)\
                            .then_inc(picked_s, 1)

                split(0)
                with gp.Fori(0, H // 2 - 1) as i:
                    for b in range(2):
                        picks(i, b)
                for b in range(2):
                    picks(H // 2 - 1, b, True)

            @block.tensor
            def _(pe):
                with pe.Fori(0, H) as i:
                    for c in range(2):
                        pe.wait_ge(w_lo[c], i + 2)
                        pe.wait_ge(qcp_s, 2 * i + c + 1)
                        for a, b in COLS:
                            for k in range(KD):
                                mm = split_matmul(nc, psq[:, a:b], (wh[c][:, k, :], wl[c][:, k, :]),
                                                  (hh[:, k, a:b], hl[:, k, a:b]), k == 0, k == KD - 1)
                        mm.then_inc(qmm_s, 1)
                    pe.wait_ge(qcp_s, 2 * i + 2 + 1)
                    pe.wait_ge(ink_s, 16 * i + 16)
                    pe.wait_ge(scp_s, i + 1)
                    for t in range(NT):
                        for c in range(2):
                            mm = nc.tensor.matmul(pss[:, 2 * t + c, :], qT[c][:, t * P:(t + 1) * P], keys[:, c, :],
                                                  start=True, stop=True)
                    mm.then_inc(smm_s, 1)
                pe.wait_ge(head_s, H)
                pe.wait_ge(scp_s, H + 1)
                pe.wait_ge(in0_s, 32)
                for n in range(3 * NT // TR):
                    if n >= 2:
                        pe.wait_ge(tcp_s, n - 1)
                    for y in range(TR):
                        q, t = divmod(n * TR + y, NT)
                        mm = nc.tensor.transpose(pss[:, 8 * (n % 2) + y, :], res[:, q, t, :], ident[:])
                    mm.then_inc(tr_s, 1)

            @block.scalar
            def _(act):
                Copy = lambda out, x: nc.scalar.activation(out, x, ACT.Copy)

                def split(i, c):
                    act.wait_ge(inw_s[c], 16 * i + 16)
                    Copy(wh[c][:], w[c][:]).then_inc(w_hi[c], 1)

                def scores(i, b, last):
                    h = 2 * i + b
                    for c in range(2):
                        act.wait_ge(qmm_s, 2 * h + c + 1)
                        act.wait_ge(smm_s, h + 1)
                        Copy(qT[c][:], psq[:, 0:T]).then_inc(qcp_s, 1)
                        if not last:
                            split(h + 1, c)
                    act.wait_ge(smm_s, h + 2)
                    act.wait_ge(used_s, h + 1)
                    Copy(sc[:], pss[:]).then_inc(scp_s, 1)

                def step(i, b, last=False):
                    if not (last and b == 1):
                        scores(i, b + 1, last)
                    act.wait_ge(sub_s, 2 * i + b + 1)
                    nc.scalar.activation(ex[b][:], ex[b][:], ACT.Exp).then_inc(ex_s, 1)

                for c in range(2):
                    split(0, c)
                scores(0, 0, False)
                with act.Fori(0, H // 2 - 1) as i:
                    for b in range(2):
                        step(i, b)
                for b in range(2):
                    step(H // 2 - 1, b, True)
                for n in range(3 * NT // TR):
                    act.wait_ge(tr_s, n + 1)
                    q, t = divmod(n * TR, NT)
                    nc.scalar.activation(slots[:, q, t * P:(t + TR) * P],
                                         pss[:, 8 * (n % 2):8 * (n % 2) + TR, :].rearrange("p a t -> p (a t)"),
                                         ACT.Copy).then_inc(tcp_s, 1)

            @block.vector
            def _(dve):
                V = nc.vector
                LOW = -3.0e38

                def top16(link, rows, done=None):
                    ops = (lambda x, s, t, at: V.max(t[:, 0:8], x),
                           lambda x, s, t, at: V.max_index(at[:, 0:8], t[:, 0:8], x),
                           lambda x, s, t, at: V.match_replace(s, t[:, 0:8], x, LOW),
                           lambda x, s, t, at: V.max(t[:, 8:16], s),
                           lambda x, s, t, at: V.max_index(at[:, 8:16], t[:, 8:16], s))
                    for op in ops:
                        for r in rows[:-1]:
                            op(*r)
                        ins = op(*rows[-1])
                        if op is ops[-1] and done is not None:
                            ins.then_inc(done, 1)
                        else:
                            link(ins)

                def rank(i, b):
                    h = 2 * i + b
                    link = linker(dve, link_s, again=True)
                    hold(dve, passed_s, (scp_s, h + 2))
                    for n in range(0, NTC, ROWS):
                        top16(link, [(sc[:, n + y, :], sc2[:, y, :], v[:, n + y, :], ix[:, n + y, :])
                                     for y in range(ROWS)], used_s if n == NTC - ROWS else None)
                    dve.wait_ge(used_s, h + 2)
                    V.tensor_copy(ixf[b][:], ix[:])
                    vv = v[:].rearrange("p (t c) k -> p t c k", c=2)
                    link(V.tensor_tensor(cand[:], vv[:, :, 0, :].unsqueeze(3).broadcast_to([P, NT, TOPK, TOPK]),
                                         vv[:, :, 1, :].unsqueeze(2).broadcast_to([P, NT, TOPK, TOPK]), ALU.add))
                    for t in range(0, NT, ROWS):
                        top16(link, [(cand[:, t + y, :, :].rearrange("p a b -> p (a b)"),
                                      cand2[:, y, :, :].rearrange("p a b -> p (a b)"), top[:, t + y, :],
                                      pos[:, t + y, :]) for y in range(ROWS)])
                    V.tensor_tensor(ex[b][:], top[:], top[:, :, 0:1].broadcast_to([P, NT, TOPK]), ALU.subtract)\
                        .then_inc(sub_s, 1)

                def mark(i, b):
                    link = linker(dve, link_s, again=True)
                    for c, (op, n) in enumerate(((ALU.logical_shift_right, 4), (ALU.bitwise_and, 15))):
                        ins = V.tensor_scalar(pa[:, c], pos[:], n, None, op)
                    link(ins)
                    for c in range(2):
                        ins = V.tensor_copy(paf[c][:], pa[:, c])
                    link(ins)
                    for c in range(2):
                        ins = V.tensor_tensor(pick[c][:].rearrange("p t a b -> p (t a) b"),
                                              paf[c][:].rearrange("p t k -> p (t k)").unsqueeze(2)
                                              .broadcast_to([P, NT * TOPK, TOPK]),
                                              iota[:].unsqueeze(1).broadcast_to([P, NT * TOPK, TOPK]), ALU.is_equal)
                    ins.then_inc(ranked_s, 1)

                def finish(i, b):
                    h = 2 * i + b
                    link = linker(dve, link_s, again=True)
                    dve.wait_ge(ex_s, h + 1)
                    link(V.tensor_reduce(sm[:], ex[b][:], AX.X, ALU.add))
                    link(V.reciprocal(sm[:], sm[:]))
                    V.tensor_tensor(res[:, 2, :, bass.ds(h * TOPK, TOPK)], ex[b][:],
                                    sm[:].unsqueeze(2).broadcast_to([P, NT, TOPK]), ALU.mult)
                    dve.wait_ge(picked_s, 2 * h + 2)
                    for c in range(2):
                        ins = V.tensor_reduce(res[:, c, :, bass.ds(h * TOPK, TOPK)], pick[c][:], AX.X, ALU.add)
                    ins.then_inc(head_s, 1)

                def step(i, b, last=False):
                    if not (last and b == 1):
                        rank(i + (b + 1) // 2, (b + 1) % 2)
                    finish(i, b)
                    if not (last and b == 1):
                        mark(i + (b + 1) // 2, (b + 1) % 2)

                dve.wait_ge(in0_s, 32)
                rank(0, 0)
                mark(0, 0)
                with dve.Fori(0, H // 2 - 1) as i:
                    for b in range(2):
                        step(i, b)
                for b in range(2):
                    step(H // 2 - 1, b, True)


def peer_gates(nc, d, slots, gates):
    with ExitStack() as ctx:
        sb, pb, sem = opener(nc, ctx)
        slab = [sb(f"pg_slab{p}", [P, N_KEYS, TW]) for p in range(2)]
        row = sb("pg_row", [P, P])
        iota = sb("pg_iota", [P, P, TR8], BF16)
        part = sb("pg_part", [P, 5, T], BF16)
        rest = sb("pg_rest", [P, T])
        o1 = [sb(f"pg_o1{b}", [P, P, TR8], BF16) for b in range(2)]
        hot = [sb(f"pg_hot{b}", [P, P, TR8], BF16) for b in range(2)]
        o2 = [sb(f"pg_o2{b}", [P, 3, P, TR8], BF16) for b in range(2)]
        ps = [pb(f"pg_ps{b}", [P, TR8, P]) for b in range(2)]
        in_s, link_s = sem("gg_in"), sem("gg_link")
        hot_s, mm_s, copied_s = ([sem(f"gg_{x}{b}") for b in range(2)] for x in ("hot", "mm", "copied"))
        st_s = [sem(f"gg_st{p}") for p in range(2)]
        ROUNDS = TW // TR8
        count_from_one(nc, mm_s, copied_s, st_s)
        with nc.Block() as block:

            @block.sync
            def _(sp):
                sp.dma_start(row[:], d["c_iota"]).then_inc(in_s, 16)
                with sp.Fori(0, T // TW // 2) as s:
                    for p in range(2):
                        for b in range(2):
                            sp.wait_ge(copied_s[b], (2 * s + (p + 1)) * (ROUNDS // 2) + 1)
                        sp.dma_start(gates[:, :, bass.ds(2 * s + p, 1), :, :].rearrange("n p o b t -> p n (o b t)"),
                                     slab[p][:].rearrange("p (n b) t -> p n (b t)", b=2)).then_inc(st_s[p], 16)
                for p in range(2):
                    sp.wait_ge(st_s[p], 16 * (T // TW // 2) + 1)

            @block.vector
            def _(dve):
                V = nc.vector
                link = linker(dve, link_s)
                dve.wait_ge(in_s, 16)
                link(V.tensor_copy(iota[:], row[:].unsqueeze(2).broadcast_to([P, P, TR8])))
                link(V.tensor_copy(part[:, 0:3, :], slots[:]))
                link(V.tensor_tensor(rest[:], slots[:, 2, :], part[:, 2, :], ALU.subtract))
                link(V.tensor_copy(part[:, 3, :], rest[:]))
                link(V.tensor_tensor(rest[:], rest[:], part[:, 3, :], ALU.subtract))
                link(V.tensor_copy(part[:, 4, :], rest[:]))
                with dve.Fori(0, T // TR8 // 2) as i:
                    again = linker(dve, link_s, again=True)
                    for b in range(2):
                        at = lambda a: part[:, a, bass.ds(i * (2 * TR8) + b * TR8, TR8)].unsqueeze(1)\
                            .broadcast_to([P, P, TR8])
                        dve.wait_ge(mm_s[b], i + 1)
                        again(V.tensor_tensor(hot[b][:], iota[:], at(1), ALU.is_equal))
                        V.tensor_tensor(o1[b][:], iota[:], at(0), ALU.is_equal)
                        for a in range(3):
                            op = V.tensor_tensor(o2[b][:, a], hot[b][:], at(2 + a), ALU.mult)
                        op.then_inc(hot_s[b], 1)

            @block.tensor
            def _(pe):
                with pe.Fori(0, T // TR8 // 2) as i:
                    for b in range(2):
                        pe.wait_ge(hot_s[b], i + 1)
                        pe.wait_ge(copied_s[b], i + 1)
                        for t in range(TR8):
                            for a in range(3):
                                mm = nc.tensor.matmul(ps[b][:, t, :], o1[b][:, :, t], o2[b][:, a, :, t],
                                                      start=(a == 0), stop=(a == 2))
                        mm.then_inc(mm_s[b], 1)

            @block.scalar
            def _(act):
                with act.Fori(0, T // TW // 2) as s:
                    for p in range(2):
                        act.wait_ge(st_s[p], 16 * s + 1)
                        with act.Fori(0, ROUNDS // 2) as i:
                            for b in range(2):
                                act.wait_ge(mm_s[b], (2 * s + p) * (ROUNDS // 2) + i + 2)
                                nc.scalar.activation(slab[p][:, :, bass.ds(i * (2 * TR8) + b * TR8, TR8)]
                                                     .rearrange("p k t -> p t k"),
                                                     ps[b][:], ACT.Copy).then_inc(copied_s[b], 1)


def peer_experts(nc, d, hh, hl, gates, acc):
    with ExitStack() as ctx:
        sb, pb, sem = opener(nc, ctx)
        ur, vr = sb("pe_ur", [P, KD, P]), sb("pe_vr", [P, D])
        uh, ul = ([[sb(f"pe_u{x}{b}{y}", [P, KD, P], F32R) for y in range(2)] for b in range(2)] for x in "hl")
        vh, vl = ([[sb(f"pe_v{x}{b}{y}", [P, D], F32R) for y in range(2)] for b in range(2)] for x in "hl")
        gt = [sb(f"pe_gt{b}", [P, TG // TW, 2, TW]) for b in range(2)]
        w = sb("pe_w", [P, 2, TG])
        wh, wl = ([sb(f"pe_w{x}{b}", [P, 2, TG], F32R) for b in range(2)] for x in "hl")
        sums = pb("pe_sums", [P, KD, TG])
        scores = [pb(f"pe_s{b}", [P, 2, TG]) for b in range(2)]
        names = ("u_in", "v_in", "u_hi", "u_lo", "v_hi", "v_lo", "scored", "gelu", "w_hi", "w_lo", "zeroed")
        (u_in, v_in, u_hi, u_lo, v_hi, v_lo, scored, gelu, w_hi, w_lo, zeroed) = (
            sem("g2_" + x) for x in names)
        g_in, gated, summed, added = (
            [sem(f"g2_{x}{b}") for b in range(2)] for x in ("g_in", "gated", "summed", "added"))
        PAIRED = N_KEYS // 2
        U = 2 * GROUPS
        ROUNDS = PAIRED // 2
        HALF = KD // 2
        count_from_one(nc, u_lo, v_lo, gelu, gated, w_lo, added)

        def split_of(x):
            b, q = divmod(x, GROUPS)
            return None if q == GROUPS - 1 else (q % 2, b + 1, q // 2)

        with nc.Block() as block:

            @block.sync
            def _(sp):
                def weights(i, which, pair, y):
                    m = 4 * i + 2 * pair + y
                    if which == 0:
                        sp.wait_ge(u_lo, m + 1)
                        sp.dma_start(ur[:], d["peer_u"][bass.ds(m, 1), :, :, :].rearrange("o p k n -> p (o k) n"))\
                            .then_inc(u_in, 16)
                    else:
                        sp.wait_ge(v_lo, m + 1)
                        sp.dma_start(vr[:], d["peer_v"][:, bass.ds(m, 1), :].rearrange("p o n -> p (o n)"))\
                            .then_inc(v_in, 16)

                def unit(i, x, last):
                    b, q = divmod(x, GROUPS)
                    sp.wait_ge(gated[x % 2], i * GROUPS + x // 2 + 1)
                    sp.dma_start(gt[x % 2][:], gates[bass.ds(2 * i + b, 1), :, 4 * q:4 * q + 4, :, :]
                                 .rearrange("o p x b t -> p (o x) b t")).then_inc(g_in[x % 2], 16)
                    if split_of(x) and not (last and b == 1):
                        weights(i, *split_of(x))

                for y in range(2):
                    for which in range(2):
                        weights(0, which, 0, y)
                with sp.Fori(0, ROUNDS - 1) as i:
                    for x in range(U):
                        unit(i, x, False)
                for x in range(U):
                    unit(ROUNDS - 1, x, True)

            @block.scalar
            def _(act):
                def split(m, which, pair, y):
                    raw, hi, came, done = ((ur, uh, u_in, u_hi), (vr, vh, v_in, v_hi))[which]
                    act.wait_ge(came, 16 * m + 16)
                    nc.scalar.activation(hi[pair % 2][y][:], raw[:], ACT.Copy).then_inc(done, 1)

                def unit(i, x, last):
                    u = i * U + x
                    act.wait_ge(scored, u + 1)
                    act.wait_ge(w_lo, u + 1)
                    nc.scalar.activation(w[:], scores[x % 2][:], ACT.Gelu_apprx_tanh).then_inc(gelu, 1)
                    act.wait_ge(gated[x % 2], i * GROUPS + x // 2 + 2)
                    nc.scalar.activation(wh[x % 2][:], w[:], ACT.Copy).then_inc(w_hi, 1)
                    if split_of(x) and not (last and x >= GROUPS):
                        which, pair, y = split_of(x)
                        split(4 * i + 2 * pair + y, which, pair, y)

                for y in range(2):
                    for which in range(2):
                        split(y, which, 0, y)
                with act.Fori(0, ROUNDS - 1) as i:
                    for x in range(U):
                        unit(i, x, False)
                for x in range(U):
                    unit(ROUNDS - 1, x, True)

            @block.vector
            def _(dve):
                V = nc.vector

                def split(m, which, pair, y):
                    raw, hi, lo, had, done = ((ur, uh, ul, u_hi, u_lo), (vr, vh, vl, v_hi, v_lo))[which]
                    dve.wait_ge(had, m + 1)
                    V.tensor_tensor(lo[pair % 2][y][:], raw[:], hi[pair % 2][y][:], ALU.subtract).then_inc(done, 1)

                def weigh(i, x):
                    u, b = i * U + x, x % 2
                    dve.wait_ge(gelu, u + 2)
                    dve.wait_ge(g_in[b], (i * GROUPS + x // 2) * 16 + 16)
                    V.tensor_tensor(w[:].rearrange("p b (x t) -> p x b t", t=TW),
                                    w[:].rearrange("p b (x t) -> p x b t", t=TW), gt[b][:], ALU.mult)\
                        .then_inc(gated[b], 1)
                    dve.wait_ge(w_hi, u + 1)
                    V.tensor_tensor(wl[b][:], w[:], wh[b][:], ALU.subtract).then_inc(w_lo, 1)

                def unit(i, x, last):
                    if not (last and x == U - 1):
                        weigh(i, x + 1)
                    if split_of(x) and not (last and x >= GROUPS):
                        which, pair, y = split_of(x)
                        split(4 * i + 2 * pair + y, which, pair, y)
                    q = x % GROUPS
                    for a in range(2):
                        dve.wait_ge(summed[a], i * U + x + 1)
                        part = acc[:, a * HALF:(a + 1) * HALF, q * TG:(q + 1) * TG]
                        V.tensor_tensor(part, part, sums[:, a * HALF:(a + 1) * HALF, :], ALU.add).then_inc(added[a], 1)

                V.memset(acc[:], 0.0).then_inc(zeroed, 1)
                for y in range(2):
                    for which in range(2):
                        split(y, which, 0, y)
                weigh(0, 0)
                dve.wait_ge(zeroed, 1)
                with dve.Fori(0, ROUNDS - 1) as i:
                    for x in range(U):
                        unit(i, x, False)
                for x in range(U):
                    unit(ROUNDS - 1, x, True)

            @block.tensor
            def _(pe):
                def score(i, x):
                    u, (b, q) = i * U + x, divmod(x, GROUPS)
                    if q == 0:
                        pe.wait_ge(u_lo, 4 * i + 2 * b + 3)
                    if x > 0:
                        pe.wait_ge(gelu, u)
                    at = slice(q * TG, (q + 1) * TG)
                    for y in range(2):
                        for k in range(KD):
                            u_parts = uh[b % 2][y][:, k, :], ul[b % 2][y][:, k, :]
                            mm = split_matmul(nc, scores[x % 2][:, y, :], u_parts, (hh[:, k, at], hl[:, k, at]),
                                              k == 0, k == KD - 1)
                    mm.then_inc(scored, 1)

                def unit(i, x, last):
                    u, (b, q) = i * U + x, divmod(x, GROUPS)
                    if not (last and x == U - 1):
                        score(i, x + 1)
                    if q == 0:
                        pe.wait_ge(v_lo, 4 * i + 2 * b + 3)
                    pe.wait_ge(w_lo, u + 2)
                    for a in range(2):
                        pe.wait_ge(added[a], u + 1)
                        for k in range(a * HALF, (a + 1) * HALF):
                            for y in range(2):
                                rows = slice(k * P, (k + 1) * P)
                                mm = split_matmul(nc, sums[:, k, :], (vh[b][y][:, rows], vl[b][y][:, rows]),
                                                  (wh[x % 2][:, y, :], wl[x % 2][:, y, :]), y == 0, y == 1)
                        mm.then_inc(summed[a], 1)

                score(0, 0)
                with pe.Fori(0, ROUNDS - 1) as i:
                    for x in range(U):
                        unit(i, x, False)
                for x in range(U):
                    unit(ROUNDS - 1, x, True)


def constants():
    f = np.float32
    i = np.arange(P)
    row, c = np.meshgrid(np.arange(T_LAT // 64), np.arange(64), indexing="ij")
    quarter = HD // 4
    inv = (f(10000.0) ** (-np.arange(quarter, dtype=f) / f(quarter))).astype(f)
    ang = np.stack([row.reshape(-1), c.reshape(-1)], 1).astype(f)[:, :, None] * inv
    ang = np.concatenate([np.zeros((T_CTX, 2, quarter), f), ang])
    scale = np.array([1.0, HD ** -0.5], f)[None, :, None]
    cos = np.repeat(np.cos(ang)[:, :, None, :], 2, axis=2).reshape(T, 1, HD) * scale
    sin = np.sin(ang).reshape(T, 1, HD // 2) * scale
    one = np.ones((P, 1))
    diff = i[None, :] - i[:, None]
    return {
        "c_cos": cos.reshape(NT, P, 2, HD).astype(f), "c_sin": sin.reshape(NT, P, 2, HD // 2).astype(f),
        "c_ret": np.stack([one * (i + 1), one * (P - i), np.maximum(diff, 0), np.maximum(-diff, 0),
                           diff >= 0, diff <= 0], axis=1).astype(f),
        "c_col": np.stack([P - 1 - i, i], axis=1).astype(f),
        "c_iota": np.repeat(np.arange(P, dtype=f)[None], P, axis=0),
        "c_ident": np.eye(P, dtype=f),
        "c_reset": np.repeat((np.arange(T) % CH != 0)[None], P, axis=0).astype(f),
        "c_blk": np.kron(np.eye(2), np.ones((HD, HD))).astype(f),
        "c_idb": np.tile(np.eye(CH), (2, 1)).astype(f),
        **chunk_masks(),
    }


def chunk_masks():
    s, t = np.arange(CH)[:, None], np.arange(CH)[None, :]
    before = [s < t, s > t]
    mar = np.stack([np.concatenate([b, b | (s == t)], axis=1) for b in before], axis=1)
    mba = np.stack([b.T for b in before], axis=1)
    lev = np.stack([np.stack([b & (s // (2 * n) == t // (2 * n)) & (s // n != t // n) for b in before], axis=1)
                    for n in LEVELS], axis=1)
    both = lambda m: np.ascontiguousarray(np.tile(m, (2,) + (1,) * (m.ndim - 1)).astype(np.float32))
    return {"c_mar": both(mar), "c_mba": both(mba), "c_lev": both(lev)}


def pair_rows(s):
    return s.reshape(2, PAIRS, 2, HD, HD).transpose(2, 3, 0, 1, 4).reshape(P, 2 * PAIRS, HD)


def layouts(i):
    a = {k: np.ascontiguousarray(v) for k, v in i.items()}
    rows = lambda w, n: w.reshape(KD, P, n, -1).transpose(2, 1, 0, 3)
    col = lambda v, n: v.reshape(n, P).T
    x = np.concatenate([a["x_prompt"][0], a["x_sample"][0]])
    out = {
        "xT": x.T.reshape(KD, P, T),
        "cT": np.stack([a["c_ctx"], a["c"][0]]).reshape(2, KD, P).transpose(2, 1, 0),
        "ada_w": rows(a["ada_w"][0], MODS * D // 512),
        "ada_b": col(a["ada_b"][0], MODS * KD),
        "norm1_g": col(a["norm1_g"][0], KD), "norm2_g": col(a["norm2_g"][0], KD),
        "final_g": np.repeat(col(a["final_norm_g"], KD)[:, :, None], 2, axis=2),
        "w_br": np.stack([a[n][0].reshape(PAIRS, P, KD, P) for n in ("w_br_a", "w_br_b")]).transpose(3, 2, 0, 1, 4),
        "w_out": rows(a["w_out"][0], KD),
        "rw_g2": a["rwkv_g2"][0].reshape(P, PAIRS, P).transpose(1, 0, 2),
        "gn_wb": np.stack([a[n][0].reshape(PAIRS, P) for n in ("ret_gn_w", "rwkv_gn_w", "ret_gn_b", "rwkv_gn_b")])
                   .reshape(2, 2, PAIRS, P).transpose(3, 0, 1, 2),
        "peer_wq": rows(a["peer_wq"][0], 2 * H),
        "peer_keys": a["peer_keys"][0].transpose(0, 3, 1, 2),
        "peer_u": a["peer_u"][0].reshape(N_KEYS, N_KEYS, KD, P).transpose(1, 3, 2, 0),
        "peer_v": a["peer_v"][0].reshape(N_KEYS, N_KEYS, D),
        "w_qkv": rows(a["w_in"][0][:, :A_BLOCKS * 512], A_BLOCKS),
        "w_rest": rows(a["w_in"][0][:, A_BLOCKS * 512:], B_BLOCKS),
        "ret_state": pair_rows(a["state_ret"][0, 0]),
        "decay_part": np.repeat(a["ret_decay"][0].reshape(2, PAIRS, 2).transpose(2, 0, 1), HD, axis=0),
        "decay_row": np.repeat(a["ret_decay"][0][None], P, axis=0),
    }
    taps = a["rwkv_conv"][0].reshape(3, 3, PAIRS, P).transpose(2, 3, 1, 0).reshape(PAIRS, P, 9)
    ch = lambda v: v.reshape(-1, PAIRS, P).transpose(1, 2, 0)
    out["rw_cols"] = np.concatenate([taps, ch(a["rwkv_w0"][0]), ch(a["rwkv_a0"][0]), ch(a["rwkv_k_k"][0]),
                                     ch(a["rwkv_k_a"][0]), ch(a["rwkv_r_k"][0].reshape(-1))], axis=2)
    out["rw_wa"] = np.concatenate([a["rwkv_w2"][0], a["rwkv_a2"][0]], axis=1).reshape(2, P, PAIRS, P)\
        .transpose(2, 1, 0, 3)
    out["rw_state"] = pair_rows(a["state_rwkv"][0, 0].transpose(0, 1, 3, 2))
    out.update(constants())
    return {k: np.ascontiguousarray(v) for k, v in out.items()}


def rwkv(nc, d, projT, bonus_v, yT, state_out):
    n = PAIRS * NG
    xs = nc.dram_tensor("rw_xs", [n, P, 2, 4, GT], F32).ap()
    vs = nc.dram_tensor("rw_vs", [n, P, GT], F32).ap()
    ef = nc.dram_tensor("rw_ef", [n, P, 3 * GRP, CH], F32).ap()
    mn = nc.dram_tensor("rw_mn", [2, PAIRS * NCH, P, 2 * CH], F32).ap()
    with ExitStack() as ctx:
        gs = ctx.enter_context(nc.sbuf_tensor("rw_gs", [P, PAIRS, 2, NCH], F32))
        rwkv_operands(nc, d, projT, gs, xs, vs, bonus_v)
        rwkv_chunks(nc, d, xs, vs, ef, mn)
        qs = ctx.enter_context(nc.sbuf_tensor("rw_qs", [P, NCH, 2 * PAIRS, HD], F32))
        rwkv_scan(nc, d, mn, gs, qs, state_out)
        rwkv_outputs(nc, ef, qs, yT)


def feed_forward(nc, d, g, x1, y):
    gates = nc.dram_tensor("gates", [N_KEYS // 2, P, T // TW, 2, TW], F32).ap()
    with ExitStack() as ctx:
        rows = lambda c, name, dt=F32: c.enter_context(nc.sbuf_tensor(name, [P, KD, T], dt))
        hh, hl = rows(ctx, "h2_hi", F32R), rows(ctx, "h2_lo", F32R)
        with ExitStack() as c2:
            rms_norm(nc, "n2", rows(c2, "n2_x"), x1, g["gain2"], g["mod"][:, 3 * KD:4 * KD, :], split=(hh, hl))
        with ExitStack() as c2:
            slots = c2.enter_context(nc.sbuf_tensor("slots", [P, 3, T], F32))
            peer_select(nc, d, hh, hl, slots)
            peer_gates(nc, d, slots, gates)
        acc = rows(ctx, "expert_sums")
        peer_experts(nc, d, hh, hl, gates, acc)
        rms_norm(nc, "n3", rows(ctx, "n3_x"), x1, g["nfg"], None, store=y,
                 residual=(acc, g["mod"][:, 5 * KD:6 * KD, :]))


def program(nc, d, out):
    with ExitStack() as ctx:
        sb, pb, sem = opener(nc, ctx)
        g = {
            "mod": sb("mod", [P, MODS * KD, 2]), "gain1": sb("gain1", [P, KD, 2]), "gain2": sb("gain2", [P, KD, 2]),
            "n1g": sb("n1g", [P, KD]), "n2g": sb("n2g", [P, KD]), "nfg": sb("nfg", [P, KD, 2]),
        }
        projT = nc.dram_tensor("projT", [B_BLOCKS, P, T], F32).ap()
        qkv = nc.dram_tensor("qkv", [NT, P, A_BLOCKS, 512], F32).ap()
        modulation(nc, g, d)
        rows = lambda c, name, dt=F32: c.enter_context(nc.sbuf_tensor(name, [P, KD, T], dt))
        with ExitStack() as c2:
            hh, hl = rows(c2, "h_hi", F32R), rows(c2, "h_lo", F32R)
            with ExitStack() as c3:
                rms_norm(nc, "n1", rows(c3, "n1_x"), d["xT"], g["gain1"], g["mod"][:, 0:KD, :], split=(hh, hl))
            projection(nc, "proj", hh, hl, d["w_rest"], B_BLOCKS, projT)
            qkv_projection(nc, hh, hl, d["w_qkv"], qkv)
        mixers = ExitStack()
        oT = mixers.enter_context(nc.sbuf_tensor("oT", [P, PAIRS, T], F32))
        retention(nc, d, qkv, oT, out["ret"])
        bonus_v = nc.dram_tensor("bonus_v", [PAIRS, P, T], F32).ap()
        yT = mixers.enter_context(nc.sbuf_tensor("yT", [P, PAIRS, T], F32))
        rwkv(nc, d, projT, bonus_v, yT, out["rwkv"])
        x1 = nc.dram_tensor("x1", [KD, P, T], F32).ap()
        group_norms(nc, d, projT, bonus_v, oT, yT)
        with ExitStack() as c2:
            hh, hl = rows(c2, "merged_hi", F32R), rows(c2, "merged_lo", F32R)
            branches(nc, d, projT, oT, yT, hh, hl)
            out_projection(nc, d, g, hh, hl, x1)
        mixers.close()
        feed_forward(nc, d, g, x1, out["y"])


def kernel(**inputs):
    import concourse.bacc as bacc
    from concourse.bass_utils import run_bass_kernel_spmd

    laid = layouts({k: np.asarray(v) for k, v in inputs.items()})
    nc = bacc.Bacc("TRN2", target_bir_lowering=False, num_devices=1)
    d = {k: nc.dram_tensor("in_" + k, v.shape, mybir.dt.from_np(v.dtype), kind="ExternalInput").ap()
         for k, v in laid.items()}
    shapes = {"y": [KD, P, T], "ret": [P, 2 * PAIRS, HD], "rwkv": [P, 2 * PAIRS, HD]}
    out = {k: nc.dram_tensor("out_" + k, s, F32, kind="ExternalOutput").ap() for k, s in shapes.items()}
    program(nc, d, out)
    r = run_bass_kernel_spmd(nc, [{"in_" + k: v for k, v in laid.items()}], core_ids=[0]).results[0]
    y = r["out_y"].reshape(D, T).T
    heads = lambda s: s.reshape(2, HD, 2, PAIRS, HD).transpose(2, 3, 0, 1, 4).reshape(2, H, HD, HD)
    ret, rwkv_ = heads(r["out_ret"]), heads(r["out_rwkv"]).transpose(0, 1, 3, 2)
    full = lambda s: np.ascontiguousarray(s)[None, None]
    return (np.ascontiguousarray(y[:T_CTX])[None], np.ascontiguousarray(y[T_CTX:])[None], full(ret), full(rwkv_))
```
